# Optimizing a Trainium2 kernel written in Bass

```python
import jax, jax.numpy as jnp
from jax import lax
import numpy as np
import math

D_MODEL = 1024
BATCH = 1
SEQ = 256
DEPTH = 1

MLA_HEADS = 8
MLA_NOPE = 64
MLA_ROPE = 32
MLA_QK = MLA_NOPE + MLA_ROPE
MLA_V = 64
MLA_W = MLA_HEADS * MLA_V
MLA_Q_RANK = 256
MLA_KV_RANK = 128
ROPE_THETA = 10000.0
Q_BLOCK = 128

RWKV_HEADS = 8
RWKV_N = 64
RWKV_W = RWKV_HEADS * RWKV_N
DECAY_LORA = 64
AAA_LORA = 64
GATE_LORA = 128

MIX_W = MLA_W + RWKV_W
MLA_IN = MLA_Q_RANK + MLA_KV_RANK + MLA_ROPE
RWKV_IN = 3 * RWKV_W + DECAY_LORA + AAA_LORA + GATE_LORA
IN_W = MLA_IN + RWKV_IN

N_GROUPS = 4
EXPERTS_PER_GROUP = 8
N_EXPERTS = N_GROUPS * EXPERTS_PER_GROUP
TOP_K = 2
D_EXPERT = 256

NORM_EPS = 1e-6
LNX_EPS = 64e-5


def rms_norm(x, g, eps=NORM_EPS):
    xf = x.astype(jnp.float32)
    y = xf * lax.rsqrt(jnp.mean(xf * xf, axis=-1, keepdims=True) + eps)
    return (y * g.astype(jnp.float32)).astype(x.dtype)

def rope_tables(positions):
    half = MLA_ROPE // 2
    inv_freq = 1.0 / (ROPE_THETA ** (jnp.arange(half, dtype=jnp.float32) / half))
    ang = positions.astype(jnp.float32)[..., None] * inv_freq
    return jnp.cos(ang)[:, :, None, :], jnp.sin(ang)[:, :, None, :]

def apply_rope(x, cos, sin):
    half = MLA_ROPE // 2
    xf = x.astype(jnp.float32)
    x1, x2 = xf[..., :half], xf[..., half:]
    return jnp.concatenate([x1 * cos - x2 * sin, x2 * cos + x1 * sin], axis=-1).astype(x.dtype)

def mla_group(c_q, c_kv, k_rope, positions, g_cq, w_uq, g_ckv, w_uk, w_uv, g_qn, g_kn):
    bsz, s, _ = c_q.shape
    q = jnp.einsum('bsr,rhd->bshd', rms_norm(c_q, g_cq), w_uq)
    ckv = rms_norm(c_kv, g_ckv)
    k_nope = jnp.einsum('bsr,rhd->bshd', ckv, w_uk)
    v = jnp.einsum('bsr,rhd->bshd', ckv, w_uv)
    k_rope_h = jnp.broadcast_to(k_rope[:, :, None, :], (bsz, s, MLA_HEADS, MLA_ROPE))
    k = jnp.concatenate([k_nope, k_rope_h], axis=-1)
    q = rms_norm(q, g_qn)
    k = rms_norm(k, g_kn)
    cos, sin = rope_tables(positions)
    q = jnp.concatenate([q[..., :MLA_NOPE], apply_rope(q[..., MLA_NOPE:], cos, sin)], axis=-1)
    k = jnp.concatenate([k[..., :MLA_NOPE], apply_rope(k[..., MLA_NOPE:], cos, sin)], axis=-1)
    scale = MLA_QK ** -0.5
    outs = []
    for blk in range(s // Q_BLOCK):
        q0 = blk * Q_BLOCK
        kend = q0 + Q_BLOCK
        scores = jnp.einsum('bqhd,bkhd->bhqk', q[:, q0:kend], k[:, :kend]).astype(jnp.float32) * scale
        causal = (q0 + jnp.arange(Q_BLOCK))[:, None] >= jnp.arange(kend)[None, :]
        scores = jnp.where(causal, scores, -jnp.inf)
        probs = jax.nn.softmax(scores, axis=-1).astype(v.dtype)
        outs.append(jnp.einsum('bhqk,bkhd->bqhd', probs, v[:, :kend]))
    return jnp.concatenate(outs, axis=1).reshape(bsz, s, MLA_W)

def rwkv7_group(feat, mu, w0, w2, a0, a2, g2, k_k, k_a, r_k, lnx_g, lnx_b):
    bsz, s, _ = feat.shape
    prev = jnp.pad(feat, ((0, 0), (1, 0), (0, 0)))[:, :-1]
    feat = feat + (prev - feat) * mu
    splits = np.cumsum([RWKV_W, RWKV_W, RWKV_W, DECAY_LORA, AAA_LORA]).tolist()
    r, k, v, wl, al, gl = jnp.split(feat, splits, axis=-1)
    w = -jax.nn.softplus(-(w0 + jnp.tanh(wl) @ w2)) - 0.5
    a = jax.nn.sigmoid(a0 + al @ a2)
    g = jax.nn.sigmoid(gl) @ g2
    heads = lambda t: t.reshape(bsz, s, RWKV_HEADS, RWKV_N).astype(jnp.float32)
    kk = heads(k * k_k)
    kk = kk * lax.rsqrt(jnp.sum(kk * kk, axis=-1, keepdims=True) + 1e-12)
    k = k * (1.0 + (a - 1.0) * k_a)
    rh, kh, vh, ah = heads(r), heads(k), heads(v), heads(a)
    decay = jnp.exp(-jnp.exp(heads(w)))

    def step(state, inp):
        r_t, k_t, v_t, kk_t, b_t, d_t = inp
        sa = jnp.einsum('bhvk,bhk->bhv', state, -kk_t)
        state = (state * d_t[:, :, None, :] + sa[..., None] * b_t[:, :, None, :]
                 + v_t[..., None] * k_t[:, :, None, :])
        return state, jnp.einsum('bhvk,bhk->bhv', state, r_t)

    tm = lambda t: jnp.swapaxes(t, 0, 1)
    state0 = jnp.zeros((bsz, RWKV_HEADS, RWKV_N, RWKV_N), jnp.float32)
    _, y = lax.scan(step, state0, (tm(rh), tm(kh), tm(vh), tm(kk), tm(kk * ah), tm(decay)))
    y = tm(y)
    mean = jnp.mean(y, axis=-1, keepdims=True)
    var = jnp.mean(jnp.square(y - mean), axis=-1, keepdims=True)
    y = ((y - mean) * lax.rsqrt(var + LNX_EPS)).reshape(bsz, s, RWKV_W)
    y = y * lnx_g.astype(jnp.float32) + lnx_b.astype(jnp.float32)
    bonus = jnp.sum(rh * kh * r_k.astype(jnp.float32), axis=-1, keepdims=True) * vh
    y = y + bonus.reshape(bsz, s, RWKV_W)
    return (y * g.astype(jnp.float32)).astype(feat.dtype)

def hier_moe(h, w_group, b_group, w_expert, b_expert, w_gate, w_up, w_down):
    bsz, s, d = h.shape
    t = h.reshape(bsz * s, d)
    n = t.shape[0]
    rows = jnp.arange(n)
    group_logits = (t @ w_group).astype(jnp.float32) + b_group.astype(jnp.float32)
    group_probs = jax.nn.softmax(group_logits, axis=-1)
    _, gsel = lax.top_k(group_logits, 1)
    gsel = gsel[:, 0]
    expert_logits = ((t @ w_expert).astype(jnp.float32) + b_expert.astype(jnp.float32)).reshape(
        n, N_GROUPS, EXPERTS_PER_GROUP)
    in_group = expert_logits[rows, gsel]
    top_vals, top_idx = lax.top_k(in_group, TOP_K)
    weights = jax.nn.softmax(top_vals, axis=-1) * group_probs[rows, gsel][:, None]
    expert_ids = gsel[:, None] * EXPERTS_PER_GROUP + top_idx
    combine = jnp.sum(jax.nn.one_hot(expert_ids, N_EXPERTS, dtype=jnp.float32) * weights[..., None],
                      axis=1).astype(t.dtype)
    y = jnp.zeros_like(t)
    for e in range(N_EXPERTS):
        hidden = jax.nn.silu(t @ w_gate[e]) * (t @ w_up[e])
        y = y + combine[:, e:e + 1] * (hidden @ w_down[e])
    return y.reshape(bsz, s, d)

def hybrid_layer(x, positions, g_mix, w_in, g_cq, w_uq, g_ckv, w_uk, w_uv, g_qn, g_kn, g_mla_out,
                 rw_mu, rw_w0, rw_w2, rw_a0, rw_a2, rw_g2, rw_k_k, rw_k_a, rw_r_k, rw_lnx_g, rw_lnx_b,
                 w_o, g_ffn, w_group, b_group, w_expert, b_expert, w_gate, w_up, w_down):
    h = rms_norm(x, g_mix)
    proj = h @ w_in
    c_q = proj[..., :MLA_Q_RANK]
    c_kv = proj[..., MLA_Q_RANK:MLA_Q_RANK + MLA_KV_RANK]
    k_rope = proj[..., MLA_Q_RANK + MLA_KV_RANK:MLA_IN]
    feat = proj[..., MLA_IN:]
    mla_out = rms_norm(mla_group(c_q, c_kv, k_rope, positions, g_cq, w_uq, g_ckv, w_uk, w_uv, g_qn, g_kn),
                       g_mla_out)
    rw_out = rwkv7_group(feat, rw_mu, rw_w0, rw_w2, rw_a0, rw_a2, rw_g2, rw_k_k, rw_k_a, rw_r_k,
                         rw_lnx_g, rw_lnx_b)
    x = x + jnp.concatenate([mla_out, rw_out], axis=-1) @ w_o
    x = x + hier_moe(rms_norm(x, g_ffn), w_group, b_group, w_expert, b_expert, w_gate, w_up, w_down)
    return x

def first_inputs(seed: int = 0) -> dict:
    key = jax.random.key(seed)
    ks = iter(jax.random.split(key, 40))
    L = DEPTH

    def nrm(shape, scale):
        return jax.random.normal(next(ks), shape, jnp.float32) * scale

    def gain(shape):
        return 1.0 + nrm(shape, 0.02)

    x = nrm((BATCH, SEQ, D_MODEL), 1.0)
    positions = (jnp.arange(SEQ, dtype=jnp.int32)[None, :]
                 + jax.random.randint(next(ks), (BATCH, 1), 0, 1024, jnp.int32))
    return {
        'x': x,
        'positions': positions,
        'g_mix': gain((L, D_MODEL)),
        'w_in': nrm((L, D_MODEL, IN_W), D_MODEL ** -0.5),
        'g_cq': gain((L, MLA_Q_RANK)),
        'w_uq': nrm((L, MLA_Q_RANK, MLA_HEADS, MLA_QK), MLA_Q_RANK ** -0.5),
        'g_ckv': gain((L, MLA_KV_RANK)),
        'w_uk': nrm((L, MLA_KV_RANK, MLA_HEADS, MLA_NOPE), MLA_KV_RANK ** -0.5),
        'w_uv': nrm((L, MLA_KV_RANK, MLA_HEADS, MLA_V), MLA_KV_RANK ** -0.5),
        'g_qn': gain((L, MLA_QK)),
        'g_kn': gain((L, MLA_QK)),
        'g_mla_out': gain((L, MLA_W)),
        'rw_mu': jax.random.uniform(next(ks), (L, RWKV_IN), jnp.float32, 0.0, 1.0),
        'rw_w0': jax.random.uniform(next(ks), (L, RWKV_W), jnp.float32, -4.0, 2.0),
        'rw_w2': nrm((L, DECAY_LORA, RWKV_W), 0.5 * DECAY_LORA ** -0.5),
        'rw_a0': nrm((L, RWKV_W), 0.1),
        'rw_a2': nrm((L, AAA_LORA, RWKV_W), 0.5 * AAA_LORA ** -0.5),
        'rw_g2': nrm((L, GATE_LORA, RWKV_W), GATE_LORA ** -0.5),
        'rw_k_k': 0.85 + nrm((L, RWKV_W), 0.02),
        'rw_k_a': 1.0 + nrm((L, RWKV_W), 0.02),
        'rw_r_k': nrm((L, RWKV_HEADS, RWKV_N), 0.1),
        'rw_lnx_g': gain((L, RWKV_W)),
        'rw_lnx_b': nrm((L, RWKV_W), 0.01),
        'w_o': nrm((L, MIX_W, D_MODEL), MIX_W ** -0.5),
        'g_ffn': gain((L, D_MODEL)),
        'w_group': nrm((L, D_MODEL, N_GROUPS), D_MODEL ** -0.5),
        'b_group': nrm((L, N_GROUPS), 0.01),
        'w_expert': nrm((L, D_MODEL, N_EXPERTS), D_MODEL ** -0.5),
        'b_expert': nrm((L, N_EXPERTS), 0.01),
        'w_gate': nrm((L, N_EXPERTS, D_MODEL, D_EXPERT), D_MODEL ** -0.5),
        'w_up': nrm((L, N_EXPERTS, D_MODEL, D_EXPERT), D_MODEL ** -0.5),
        'w_down': nrm((L, N_EXPERTS, D_EXPERT, D_MODEL), D_EXPERT ** -0.5),
    }

def first_block(x, positions, g_mix, w_in, g_cq, w_uq, g_ckv, w_uk, w_uv, g_qn, g_kn, g_mla_out,
              rw_mu, rw_w0, rw_w2, rw_a0, rw_a2, rw_g2, rw_k_k, rw_k_a, rw_r_k, rw_lnx_g, rw_lnx_b,
              w_o, g_ffn, w_group, b_group, w_expert, b_expert, w_gate, w_up, w_down):
    for l in range(DEPTH):
        x = hybrid_layer(x, positions, g_mix[l], w_in[l], g_cq[l], w_uq[l], g_ckv[l], w_uk[l], w_uv[l],
                         g_qn[l], g_kn[l], g_mla_out[l], rw_mu[l], rw_w0[l], rw_w2[l], rw_a0[l],
                         rw_a2[l], rw_g2[l], rw_k_k[l], rw_k_a[l], rw_r_k[l], rw_lnx_g[l], rw_lnx_b[l],
                         w_o[l], g_ffn[l], w_group[l], b_group[l], w_expert[l], b_expert[l],
                         w_gate[l], w_up[l], w_down[l])
    return x


DEPTH_2 = 2


A_HEADS = 8
A_NOPE = 64
A_ROPE = 32
A_KV_RANK = 128
A_V_DIM = 64
A_SCALE = (A_NOPE + A_ROPE) ** -0.5
IDX_HEADS = 8
IDX_DIM = 64
TOPK_MAX = 256

B_HEADS = 4
B_QK_DIM = 64
B_V_DIM = 2 * B_QK_DIM

C_HEADS = 16
C_GROUPS = 4
C_HPG = C_HEADS // C_GROUPS
C_DIM = 64
CMP_LEN = 32
CMP_STRIDE = 16
CMP_HIDDEN = 128
SEL_BLOCK = 64
SEL_TOPN = 16
WINDOW = 512
C_Q_BLOCK = 16

D_FF = -(-8 * D_MODEL // (3 * 256)) * 256

EVEN_SPLITS = [A_HEADS * A_NOPE, A_HEADS * A_ROPE, A_KV_RANK, A_ROPE, IDX_HEADS * IDX_DIM, IDX_DIM, IDX_HEADS,
               B_HEADS * 2 * B_QK_DIM, B_HEADS * 2 * B_QK_DIM, B_HEADS * B_V_DIM]
EVEN_IN = sum(EVEN_SPLITS)
ODD_SPLITS = [C_HEADS * C_DIM] + [C_GROUPS * C_DIM] * 6 + [C_HEADS * 3]
ODD_IN = sum(ODD_SPLITS)


def rmsnorm(x, g):
    xf = x.astype(jnp.float32)
    y = xf * lax.rsqrt(jnp.mean(xf * xf, axis=-1, keepdims=True) + NORM_EPS)
    return (y * g.astype(jnp.float32)).astype(x.dtype)

def rope(x, pos):
    d = x.shape[-1]
    inv = ROPE_THETA ** (-jnp.arange(0, d, 2, dtype=jnp.float32) / d)
    ang = pos.astype(jnp.float32)[:, None] * inv[None, :]
    shape = (x.shape[1],) + (1,) * (x.ndim - 3) + (d // 2,)
    cos = jnp.cos(ang).reshape(shape)
    sin = jnp.sin(ang).reshape(shape)
    xf = x.astype(jnp.float32)
    x1, x2 = xf[..., :d // 2], xf[..., d // 2:]
    return jnp.concatenate([x1 * cos - x2 * sin, x2 * cos + x1 * sin], axis=-1).astype(x.dtype)

def safe_softmax(s, mask):
    s = jnp.where(mask, s, -jnp.inf)
    m = jnp.max(s, axis=-1, keepdims=True)
    m = jnp.where(jnp.isfinite(m), m, 0.0)
    e = jnp.exp(s - m)
    den = jnp.sum(e, axis=-1, keepdims=True)
    return e / jnp.where(den > 0, den, 1.0)

def split_cols(y, sizes):
    return jnp.split(y, np.cumsum(sizes)[:-1].tolist(), axis=-1)

def qslice(a, i, qb):
    return lax.dynamic_slice_in_dim(a, i * qb, qb, axis=1)

def map_blocks(fn, n_blocks):
    out = lax.map(fn, jnp.arange(n_blocks, dtype=jnp.int32))
    nb, b, qb = out.shape[:3]
    return jnp.moveaxis(out, 0, 1).reshape((b, nb * qb) + out.shape[3:])

def dsa_mixer(q_nope, q_rope, c_kv, k_rope, iq, ik, iw, kv_gain, w_uk, w_uv, pos):
    B, T = c_kv.shape[:2]
    q_nope = q_nope.reshape(B, T, A_HEADS, A_NOPE)
    q_rope = rope(q_rope.reshape(B, T, A_HEADS, A_ROPE), pos)
    c_kv = rmsnorm(c_kv, kv_gain)
    k_rope = rope(k_rope, pos)
    q_lat = jnp.einsum('bthd,hdc->bthc', q_nope, w_uk)
    qc = jnp.concatenate([q_lat, q_rope], axis=-1)
    kc = jnp.concatenate([c_kv, k_rope], axis=-1)
    iq = rope(iq.reshape(B, T, IDX_HEADS, IDX_DIM), pos)
    ik = rope(ik, pos)
    iw = iw * IDX_HEADS ** -0.5
    k_sel = min(TOPK_MAX, T // 4)

    def block(i):
        t = i * Q_BLOCK + jnp.arange(Q_BLOCK, dtype=jnp.int32)
        rel = jax.nn.relu(jnp.einsum('bqhd,bsd->bqhs', qslice(iq, i, Q_BLOCK), ik).astype(jnp.float32) * IDX_DIM ** -0.5)
        score = jnp.einsum('bqhs,bqh->bqs', rel, qslice(iw, i, Q_BLOCK).astype(jnp.float32))
        causal = pos[None, :] <= t[:, None]
        score = jnp.where(causal[None], score, -jnp.inf)
        _, idx = lax.top_k(score, k_sel)
        kg = jax.vmap(lambda k, j: k[j])(kc, idx)
        s = jnp.einsum('bqhc,bqkc->bqhk', qslice(qc, i, Q_BLOCK), kg).astype(jnp.float32) * A_SCALE
        valid = (idx <= t[None, :, None])[:, :, None, :]
        p = safe_softmax(s, valid)
        return jnp.einsum('bqhk,bqkc->bqhc', p.astype(kg.dtype), kg[..., :A_KV_RANK])

    o_lat = map_blocks(block, T // Q_BLOCK)
    o = jnp.einsum('bthc,hcd->bthd', o_lat, w_uv)
    return o.reshape(B, T, A_HEADS * A_V_DIM)

def diff_mixer(q, k, v, lam, subln_gain, lam_init, pos):
    B, T = q.shape[:2]
    q = rope(q.reshape(B, T, B_HEADS * 2, B_QK_DIM), pos).reshape(B, T, B_HEADS, 2, B_QK_DIM)
    k = rope(k.reshape(B, T, B_HEADS * 2, B_QK_DIM), pos).reshape(B, T, B_HEADS, 2, B_QK_DIM)
    v = v.reshape(B, T, B_HEADS, B_V_DIM)
    lf = lam.astype(jnp.float32)
    lam_full = jnp.exp(jnp.sum(lf[0] * lf[1])) - jnp.exp(jnp.sum(lf[2] * lf[3])) + lam_init

    def block(i):
        t = i * Q_BLOCK + jnp.arange(Q_BLOCK, dtype=jnp.int32)
        s = jnp.einsum('bqhmd,bshmd->bhmqs', qslice(q, i, Q_BLOCK), k).astype(jnp.float32) * B_QK_DIM ** -0.5
        causal = pos[None, :] <= t[:, None]
        p = safe_softmax(s, causal)
        a = p[:, :, 0] - lam_full * p[:, :, 1]
        return jnp.einsum('bhqs,bshe->bqhe', a.astype(v.dtype), v)

    o = map_blocks(block, T // Q_BLOCK)
    o = rmsnorm(o, subln_gain) * (1.0 - lam_init)
    return o.reshape(B, T, B_HEADS * B_V_DIM)

def compress(x, pe, w1, w2):
    B, T, G, d = x.shape
    chunks = x.reshape(B, T // CMP_STRIDE, CMP_STRIDE, G, d)
    blocks = jnp.concatenate([chunks[:, :-1], chunks[:, 1:]], axis=2) + pe[None, None, :, None, :]
    flat = blocks.transpose(0, 1, 3, 2, 4).reshape(B, -1, G, CMP_LEN * d)
    return jnp.einsum('bngf,fe->bnge', jax.nn.gelu(flat @ w1), w2)

def nsa_mixer(q, kc_raw, vc_raw, ks, vs, kw, vw, gates, pe, w1, w2, pos):
    B, T = q.shape[:2]
    kv = lambda a: a.reshape(B, T, C_GROUPS, C_DIM)
    q = rope(q.reshape(B, T, C_HEADS, C_DIM), pos).reshape(B, T, C_GROUPS, C_HPG, C_DIM)
    k_cmp = compress(rope(kv(kc_raw), pos), pe[0], w1[0], w2[0])
    v_cmp = compress(kv(vc_raw), pe[1], w1[1], w2[1])
    k_slc, v_slc = rope(kv(ks), pos), kv(vs)
    k_win, v_win = rope(kv(kw), pos), kv(vw)
    gates = jax.nn.sigmoid(gates.astype(jnp.float32)).reshape(B, T, C_GROUPS, C_HPG, 3).astype(q.dtype)
    n_cmp = T // CMP_STRIDE - 1
    n_blk = T // SEL_BLOCK
    top_n = min(SEL_TOPN, n_blk)
    cmp_end = jnp.arange(n_cmp, dtype=jnp.int32) * CMP_STRIDE + CMP_LEN - 1
    cs = np.arange(n_cmp) * CMP_STRIDE
    ss = np.arange(n_blk) * SEL_BLOCK
    overlap = jnp.asarray(((cs[:, None] < ss[None, :] + SEL_BLOCK) & (cs[:, None] + CMP_LEN > ss[None, :])).astype(np.float32))
    k_blocks = k_slc.reshape(B, n_blk, SEL_BLOCK, C_GROUPS, C_DIM).transpose(0, 3, 1, 2, 4)
    v_blocks = v_slc.reshape(B, n_blk, SEL_BLOCK, C_GROUPS, C_DIM).transpose(0, 3, 1, 2, 4)
    k_pad = jnp.pad(k_win, ((0, 0), (WINDOW, 0), (0, 0), (0, 0)))
    v_pad = jnp.pad(v_win, ((0, 0), (WINDOW, 0), (0, 0), (0, 0)))
    blk_ids = jnp.arange(n_blk, dtype=jnp.int32)
    scale = C_DIM ** -0.5
    gather = jax.vmap(jax.vmap(lambda a, j: a[j]))

    def block(i):
        t = i * C_Q_BLOCK + jnp.arange(C_Q_BLOCK, dtype=jnp.int32)
        qb = qslice(q, i, C_Q_BLOCK)
        s = jnp.einsum('bqghd,bngd->bqghn', qb, k_cmp).astype(jnp.float32) * scale
        p_cmp = safe_softmax(s, (cmp_end[None, :] <= t[:, None])[:, None, None, :])
        o_cmp = jnp.einsum('bqghn,bngd->bqghd', p_cmp.astype(v_cmp.dtype), v_cmp)
        imp = jnp.einsum('bqghn,nj->bqgj', p_cmp, overlap)
        cur = t // SEL_BLOCK
        forced = (blk_ids[None, :] == 0) | (blk_ids[None, :] == cur[:, None]) | (blk_ids[None, :] == cur[:, None] - 1)
        admissible = blk_ids[None, :] * SEL_BLOCK <= t[:, None]
        imp = jnp.where(forced[:, None, :], jnp.inf, imp)
        imp = jnp.where(admissible[:, None, :], imp, -jnp.inf)
        _, sel = lax.top_k(imp, top_n)
        sel = sel.transpose(0, 2, 1, 3)
        kg = gather(k_blocks, sel)
        vg = gather(v_blocks, sel)
        s = jnp.einsum('bqghd,bgqnld->bqghnl', qb, kg).astype(jnp.float32) * scale
        tok = sel[..., None] * SEL_BLOCK + jnp.arange(SEL_BLOCK, dtype=jnp.int32)
        m_slc = (tok <= t[None, None, :, None, None]).transpose(0, 2, 1, 3, 4)
        m_slc = m_slc.reshape(B, C_Q_BLOCK, C_GROUPS, 1, top_n * SEL_BLOCK)
        p = safe_softmax(s.reshape(B, C_Q_BLOCK, C_GROUPS, C_HPG, top_n * SEL_BLOCK), m_slc)
        p = p.reshape(B, C_Q_BLOCK, C_GROUPS, C_HPG, top_n, SEL_BLOCK)
        o_slc = jnp.einsum('bqghnl,bgqnld->bqghd', p.astype(vg.dtype), vg)
        kwb = lax.dynamic_slice_in_dim(k_pad, i * C_Q_BLOCK, WINDOW + C_Q_BLOCK, axis=1)
        vwb = lax.dynamic_slice_in_dim(v_pad, i * C_Q_BLOCK, WINDOW + C_Q_BLOCK, axis=1)
        kpos = i * C_Q_BLOCK - WINDOW + jnp.arange(WINDOW + C_Q_BLOCK, dtype=jnp.int32)
        dist = t[:, None] - kpos[None, :]
        m_win = ((dist >= 0) & (dist < WINDOW) & (kpos[None, :] >= 0))[:, None, None, :]
        s = jnp.einsum('bqghd,bsgd->bqghs', qb, kwb).astype(jnp.float32) * scale
        p = safe_softmax(s, m_win)
        o_win = jnp.einsum('bqghs,bsgd->bqghd', p.astype(vwb.dtype), vwb)
        g = qslice(gates, i, C_Q_BLOCK)
        return g[..., 0:1] * o_cmp + g[..., 1:2] * o_slc + g[..., 2:3] * o_win

    o = map_blocks(block, T // C_Q_BLOCK)
    return o.reshape(B, T, C_HEADS * C_DIM)

def swiglu(h, w_gate, w_up, w_down):
    return (jax.nn.silu(h @ w_gate) * (h @ w_up)) @ w_down

def _w(key, shape, fan_in, gain=1.0):
    return jax.random.normal(key, shape, jnp.float32) * (gain * fan_in ** -0.5)

def _gain(key, shape):
    return 1.0 + 0.02 * jax.random.normal(key, shape, jnp.float32)

def second_inputs(seed: int = 0) -> dict:
    key = jax.random.key(seed)
    k = jax.random.split(key, 19)
    n_even = (DEPTH_2 + 1) // 2
    n_odd = DEPTH_2 // 2
    out_gain = (2 * DEPTH_2) ** -0.5
    return {
        'x': jax.random.normal(k[0], (BATCH, SEQ, D_MODEL), jnp.float32),
        'norm_mix': _gain(k[1], (DEPTH_2, D_MODEL)),
        'norm_ffn': _gain(k[2], (DEPTH_2, D_MODEL)),
        'norm_final': _gain(k[3], (D_MODEL,)),
        'ev_w_in': _w(k[4], (n_even, D_MODEL, EVEN_IN), D_MODEL),
        'ev_kv_gain': _gain(k[5], (n_even, A_KV_RANK)),
        'ev_w_uk': _w(k[6], (n_even, A_HEADS, A_NOPE, A_KV_RANK), A_KV_RANK),
        'ev_w_uv': _w(k[7], (n_even, A_HEADS, A_KV_RANK, A_V_DIM), A_KV_RANK),
        'ev_lambda': 0.1 * jax.random.normal(k[8], (n_even, 4, B_QK_DIM), jnp.float32),
        'ev_subln': _gain(k[9], (n_even, B_V_DIM)),
        'ev_w_out': _w(k[10], (n_even, D_MODEL, D_MODEL), D_MODEL, out_gain),
        'od_w_in': _w(k[11], (n_odd, D_MODEL, ODD_IN), D_MODEL),
        'od_cmp_pe': 0.1 * jax.random.normal(k[12], (n_odd, 2, CMP_LEN, C_DIM), jnp.float32),
        'od_cmp_w1': _w(k[13], (n_odd, 2, CMP_LEN * C_DIM, CMP_HIDDEN), CMP_LEN * C_DIM),
        'od_cmp_w2': _w(k[14], (n_odd, 2, CMP_HIDDEN, C_DIM), CMP_HIDDEN),
        'od_w_out': _w(k[15], (n_odd, D_MODEL, D_MODEL), D_MODEL, out_gain),
        'ffn_w_gate': _w(k[16], (DEPTH_2, D_MODEL, D_FF), D_MODEL),
        'ffn_w_up': _w(k[17], (DEPTH_2, D_MODEL, D_FF), D_MODEL),
        'ffn_w_down': _w(k[18], (DEPTH_2, D_FF, D_MODEL), D_FF, out_gain),
    }

def second_block(x, norm_mix, norm_ffn, norm_final,
              ev_w_in, ev_kv_gain, ev_w_uk, ev_w_uv, ev_lambda, ev_subln, ev_w_out,
              od_w_in, od_cmp_pe, od_cmp_w1, od_cmp_w2, od_w_out,
              ffn_w_gate, ffn_w_up, ffn_w_down):
    pos = jnp.arange(x.shape[1], dtype=jnp.int32)
    for layer in range(DEPTH_2):
        j = layer // 2
        h = rmsnorm(x, norm_mix[layer])
        if layer % 2 == 0:
            y = h @ ev_w_in[j]
            qa_nope, qa_rope, c_kv, ka_rope, iq, ik, iw, qb, kb, vb = split_cols(y, EVEN_SPLITS)
            o_a = dsa_mixer(qa_nope, qa_rope, c_kv, ka_rope, iq, ik, iw, ev_kv_gain[j], ev_w_uk[j], ev_w_uv[j], pos)
            lam_init = 0.8 - 0.6 * math.exp(-0.3 * layer)
            o_b = diff_mixer(qb, kb, vb, ev_lambda[j], ev_subln[j], lam_init, pos)
            mix = jnp.concatenate([o_a, o_b], axis=-1) @ ev_w_out[j]
        else:
            y = h @ od_w_in[j]
            qc, kc_raw, vc_raw, ks, vs, kw, vw, gc = split_cols(y, ODD_SPLITS)
            o_c = nsa_mixer(qc, kc_raw, vc_raw, ks, vs, kw, vw, gc, od_cmp_pe[j], od_cmp_w1[j], od_cmp_w2[j], pos)
            mix = o_c @ od_w_out[j]
        x = x + mix
        x = x + swiglu(rmsnorm(x, norm_ffn[layer]), ffn_w_gate[layer], ffn_w_up[layer], ffn_w_down[layer])
    return rmsnorm(x, norm_final)


def setup_inputs(seed=0):
    out = dict(first_inputs(seed))
    for name, value in second_inputs(seed + 1).items():
        if name != "x":
            out[name + "_2"] = value
    return out


def reference(
    x, positions, g_mix, w_in, g_cq, w_uq, g_ckv, w_uk, w_uv, g_qn, g_kn, g_mla_out, rw_mu,
    rw_w0, rw_w2, rw_a0, rw_a2, rw_g2, rw_k_k, rw_k_a, rw_r_k, rw_lnx_g, rw_lnx_b, w_o, g_ffn,
    w_group, b_group, w_expert, b_expert, w_gate, w_up, w_down, norm_mix_2, norm_ffn_2,
    norm_final_2, ev_w_in_2, ev_kv_gain_2, ev_w_uk_2, ev_w_uv_2, ev_lambda_2, ev_subln_2,
    ev_w_out_2, od_w_in_2, od_cmp_pe_2, od_cmp_w1_2, od_cmp_w2_2, od_w_out_2, ffn_w_gate_2,
    ffn_w_up_2, ffn_w_down_2,
):
    x = first_block(
        x, positions, g_mix, w_in, g_cq, w_uq, g_ckv, w_uk, w_uv, g_qn, g_kn, g_mla_out, rw_mu,
        rw_w0, rw_w2, rw_a0, rw_a2, rw_g2, rw_k_k, rw_k_a, rw_r_k, rw_lnx_g, rw_lnx_b, w_o,
        g_ffn, w_group, b_group, w_expert, b_expert, w_gate, w_up, w_down,
    )
    return second_block(
        x, norm_mix_2, norm_ffn_2, norm_final_2, ev_w_in_2, ev_kv_gain_2, ev_w_uk_2, ev_w_uv_2,
        ev_lambda_2, ev_subln_2, ev_w_out_2, od_w_in_2, od_cmp_pe_2, od_cmp_w1_2, od_cmp_w2_2,
        od_w_out_2, ffn_w_gate_2, ffn_w_up_2, ffn_w_down_2,
    )


_drawn_inputs = setup_inputs


def setup_inputs(seed=0):
    import zlib

    import numpy as np

    out = dict(_drawn_inputs(seed))
    spreads = {}
    factors = {'g_cq': 3.49,
     'rw_w2': 3.15,
     'rw_k_k': 4.184,
     'rw_k_a': 4.534,
     'rw_lnx_g': 2.893,
     'rw_lnx_b': 3.533,
     'b_group': 5.366,
     'b_expert': 4.38,
     'norm_mix_2': 5.955,
     'norm_ffn_2': 6.47,
     'norm_final_2': 8.102,
     'ev_kv_gain_2': 8.0,
     'ev_lambda_2': 7.837,
     'ev_subln_2': 8.0,
     'od_cmp_pe_2': 15.657}
    for name, (base, spread) in spreads.items():
        noise = np.random.default_rng([zlib.crc32(name.encode()), seed]).standard_normal(out[name].shape)
        drawn = base * np.exp(spread * noise) if base else spread * noise
        out[name] = __import__('jax').numpy.asarray(drawn.astype(out[name].dtype))
    for name, factor in factors.items():
        out[name] = (out[name] * factor).astype(out[name].dtype)
    return out
```

```python
from contextlib import ExitStack

import numpy as np

import concourse.bass as bass
from concourse import mybir

ALU = mybir.AluOpType
ACT = mybir.ActivationFunctionType
AX_X = mybir.AxisListType.X
F32 = mybir.dt.float32
BF16 = mybir.dt.bfloat16
F16 = mybir.dt.float16
I32 = mybir.dt.int32

P = 128
SEQ = 256
TT = SEQ // P
D = 1024
KC = D // P
EPS = 1e-6
MASKED = -1e30
LEAST_MAX = -1e20
TAKEN = -3e38

W_SCALE = 64.0

SPAN = [(0, 0, P), (1, P, SEQ)]
NCOL = P + SEQ
KEY_BLOCKS = [(0, 0, 0, P), (1, 0, P, P), (1, 1, 2 * P, P)]

MLA_H, MLA_NOPE, MLA_ROPE, MLA_V = 8, 64, 32, 64
MLA_QK = MLA_NOPE + MLA_ROPE
Q_RANK, KV_RANK = 256, 128
MLA_IN = Q_RANK + KV_RANK + MLA_ROPE
RW_H, RW_N = 8, 64
RW_W = RW_H * RW_N
RW_IN = 3 * RW_W + 64 + 64 + 128
IN_W = MLA_IN + RW_IN
N_GROUPS, PER_GROUP = 4, 8
N_EXPERTS = N_GROUPS * PER_GROUP
D_EXPERT = 256
LNX_EPS = 64e-5
SOLVE_LEVELS = 7

EVEN_SPLITS = [512, 256, 128, 32, 512, 64, 8, 512, 512, 512]
EVEN_IN = sum(EVEN_SPLITS)
TOP_KEYS = 64
ODD_SPLITS = [1024] + [256] * 6 + [48]
ODD_IN = sum(ODD_SPLITS)
C_H, C_G, C_DIM = 16, 4, 64
CMP_LEN, CMP_STRIDE = 32, 16
N_CMP = SEQ // CMP_STRIDE - 1
D_FF = 2816


def shape_constants():
    t = np.arange(P)
    c = {}
    c["identity"] = np.eye(P, dtype=np.float32)
    keys = np.arange(SEQ)
    m0 = np.where(t[:, None] >= keys[None, :P], 0.0, MASKED)
    m1 = np.where(t[:, None] + P >= keys[None, :], 0.0, MASKED)
    c["causal"] = np.concatenate([m0, m1], axis=1).astype(np.float32)
    end = np.arange(N_CMP) * CMP_STRIDE + CMP_LEN - 1
    c["cmp_mask"] = np.concatenate(
        [np.where(end[None, :] <= t[:, None] + P * k, 0.0, MASKED) for k in range(TT)], axis=1).astype(np.float32)
    half = P // 2
    i, j = t[:, None], t[None, :]
    upto = (i <= j).astype(np.float32) - (i < half)
    before = (i < j).astype(np.float32) - (i < half)
    c["decay_sums"] = np.concatenate([upto, before], axis=1).astype(np.float32)
    c["decay_ends"] = np.stack([(t >= half), (t < half)], axis=1).astype(np.float32)
    lev = []
    for n in range(SOLVE_LEVELS):
        b = 1 << n
        same = (i // (2 * b)) == (j // (2 * b))
        lev.append((same & (i % (2 * b) < b) & (j % (2 * b) >= b)).astype(np.float32))
    c["level_masks"] = np.concatenate(lev + [lev[0].T, (i <= j).astype(np.float32), (i < j).astype(np.float32)],
                                      axis=1).astype(np.float32)
    inv16 = (1.0 / (np.float32(10000.0) ** (np.arange(16, dtype=np.float32) / np.float32(16)))).astype(np.float32)
    c["inv_freq"] = np.tile(inv16[None], (P, 1)).astype(np.float32)
    for d in (32, 64):
        inv = (np.float32(10000.0) ** (-np.arange(0, d, 2, dtype=np.float32) / np.float32(d))).astype(np.float32)
        ang = (np.arange(SEQ, dtype=np.float32)[:, None] * inv[None]).astype(np.float32)
        cs = np.concatenate([np.cos(ang.astype(np.float64)), np.sin(ang.astype(np.float64))], axis=1)
        c[f"rope{d}"] = cs.reshape(TT, P, d).transpose(1, 0, 2).reshape(P, TT * d).astype(np.float32)
    c["rank8"] = np.tile(np.arange(8, 0, -1, dtype=np.float32)[None], (P, 1)).astype(np.float32)
    return {k: np.ascontiguousarray(v) for k, v in c.items()}


class Link:

    def __init__(self, eng, sem, base=0):
        self.eng, self.sem, self.base, self.n = eng, sem, base, 0

    def __call__(self, ins):
        self.n += 1
        ins.then_inc(self.sem, 1)
        self.eng.wait_ge(self.sem, self.base + self.n)


def wait_alone(eng, passed, sem, value):
    eng.wait_ge(sem, value)
    eng.sem_inc(passed, 1)


class Stage:

    def __init__(self, nc, name, names):
        self.nc, self.name, self.names = nc, name, names

    def __enter__(self):
        self.sems = [self.nc.alloc_semaphore(f"{self.name}_{n}") for n in self.names]
        return self.sems

    def __exit__(self, *exc):
        if exc[0] is None:
            self.nc.clear_and_free_semaphores(self.sems)
            self.nc.all_engine_barrier()


def cols(vector):
    return vector.rearrange("(p c) -> p c", p=P)


def spread(vector):
    return vector.rearrange("(a n) -> a n", a=1).broadcast_to([P, vector.shape[0]])


def project(nc, name, con, src, width, gain, jobs, normed=True, keep_T=None, split=False):
    kc = width // P
    with ExitStack() as ctx:
        sb = lambda n, s, d=F32: ctx.enter_context(nc.sbuf_tensor(f"{name}_{n}", s, d))
        if split:
            sT_hi, sT_lo = keep_T if keep_T is not None else (sb("sT_hi", [P, kc, SEQ], F16),
                                                              sb("sT_lo", [P, kc, SEQ], F16))
        else:
            sT = keep_T if keep_T is not None else sb("sT", [P, kc, SEQ])
        big = max(j[2] for j in jobs) if jobs else 1
        xn = sb("xn", [P, TT, width]) if normed else src
        wt = sb("wt", [P, 2, kc, big])
        if split:
            w_hi = sb("w_hi", [P, 2, kc, big], F16)
            w_lo = sb("w_lo", [P, 2, kc, big], F16)
        back = 1.0 / W_SCALE if split else 1.0
        stats = sb("stats", [P, 3, TT])
        gcol = sb("gcol", [P, kc])
        pT = ctx.enter_context(nc.psum_tensor(f"{name}_pT", [P, 4, 512], F32))
        pY = ctx.enter_context(nc.psum_tensor(f"{name}_pY", [P, 2, TT, 512], F32))
        with Stage(nc, name, ["gain_in", "w0_in", "w1_in", "squares", "recips", "rstd", "normed", "turned",
                              "evac_a", "evac_v", "product", "out_a", "out_v", "vlink", "hi_ready",
                              "lo_ready"]) as sems:
            (gain_in, w0_in, w1_in, squares, recips, rstd, normed_ready, turned, evac_a, evac_v,
             product, out_a, out_v, vlink, hi_ready, lo_ready) = sems
            w_in = [w0_in, w1_in]
            order = [(job, job[1] // job[2]) for job in jobs]
            if split:
                assert len(jobs) < 2 or all(count == 1 for _, count in order)

            with nc.Block(no_gpsimd_drain=True) as block:
                def over_tiles(eng, do, skip=lambda put: False, ahead=None):
                    done = 0
                    total = sum(count for _, count in order)
                    for (w, n, tile, put), count in order:
                        if skip(put):
                            done += count
                            continue

                        def one(at, slot, turn, col, last):
                            if ahead is not None and not last:
                                ahead(w, tile, put, at + 1, 1 - slot, turn + slot)
                            do(w, tile, put, at, slot, turn, col)
                        if count >= 4:
                            assert done % 2 == 0 and count % 2 == 0
                            tail = ahead is not None
                            if ahead is not None:
                                ahead(w, tile, put, done, 0, done // 2)
                            with eng.Fori(0, count // 2 - tail) as i:
                                for s in range(2):
                                    one(i * 2 + (done + s), s, i + done // 2, (i * 2 + s) * tile, False)
                            if tail:
                                for k in (count - 2, count - 1):
                                    one(done + k, k % 2, (done + k) // 2, k * tile, k == count - 1)
                        else:
                            for k in range(count):
                                if ahead is not None:
                                    ahead(w, tile, put, done + k, (done + k) % 2, (done + k) // 2)
                                do(w, tile, put, done + k, (done + k) % 2, (done + k) // 2, k * tile)
                        done += count

                @block.sync
                def _(sp):
                    if normed:
                        sp.dma_start(gcol[:], cols(gain)).then_inc(gain_in, 16)

                    def load(w, tile, put, at, slot, turn, col):
                        sp.wait_ge(lo_ready if split else product, at + 1)
                        wv = w.rearrange("(p c) n -> p c n", p=P)
                        sp.dma_start(wt[:, slot, :, 0:tile], wv[:, :, bass.ds(col, tile)]).then_inc(w_in[slot], 16)
                    over_tiles(sp, load)

                @block.scalar
                def _(act):
                    if normed:
                        for t in range(TT):
                            nc.scalar.activation(xn[:, t, :], src[:, t, :], ACT.Square,
                                                 accum_out=stats[:, 0, t:t + 1]).then_inc(squares, 1)
                        act.wait_ge(recips, 1)
                        nc.scalar.activation(stats[:, 2, :], stats[:, 1, :], ACT.Sqrt).then_inc(rstd, 1)
                        act.wait_ge(gain_in, 16)
                    for c in range(kc) if split else range(1, kc, 2):
                        act.wait_ge(turned, c + 1)
                        into = sT_hi[:, c, :] if split else sT[:, c, :]
                        scale = gcol[:, c:c + 1] if normed else 1.0
                        nc.scalar.activation(into, pT[:, c % 4, 0:SEQ], ACT.Copy, scale=scale).then_inc(evac_a, 1)
                    act.sem_inc(out_a, 2)

                    def high_part(w, tile, put, at, slot, turn):
                        act.wait_ge(w_in[slot], turn * 16 + 16)
                        act.wait_ge(product, at + 1)
                        nc.scalar.activation(w_hi[:, slot, :, 0:tile], wt[:, slot, :, 0:tile], ACT.Copy,
                                             scale=W_SCALE).then_inc(hi_ready, 1)

                    def move(w, tile, put, at, slot, turn, col):
                        if isinstance(put, tuple):
                            return
                        act.wait_ge(product, at + 3)
                        nc.scalar.activation(put[:, 0, bass.ds(col, tile)], pY[:, slot, 0, 0:tile],
                                             ACT.Copy, scale=back).then_inc(out_a, 1)
                    over_tiles(act, move, skip=lambda put: not split and isinstance(put, tuple),
                               ahead=high_part if split else None)

                @block.vector
                def _(dve):
                    link = Link(dve, vlink)
                    if normed:
                        dve.wait_ge(squares, TT)
                        link(nc.vector.tensor_scalar(stats[:, 0, :], stats[:, 0, :], 1.0 / width, EPS,
                                                     ALU.mult, ALU.add))
                        nc.vector.reciprocal(stats[:, 1, :], stats[:, 0, :]).then_inc(recips, 1)
                        dve.wait_ge(rstd, 1)
                        for t in range(TT):
                            nc.vector.tensor_scalar(xn[:, t, :], src[:, t, :], stats[:, 2, t:t + 1], None,
                                                    ALU.mult).then_inc(normed_ready, 1)
                        dve.wait_ge(gain_in, 16)
                    for c in range(kc) if split else range(0, kc, 2):
                        if split:
                            dve.wait_ge(evac_a, c + 1)
                            scale = gcol[:, c:c + 1] if normed else 1.0
                            nc.vector.scalar_tensor_tensor(sT_lo[:, c, :], pT[:, c % 4, 0:SEQ], scale, sT_hi[:, c, :],
                                                           ALU.mult, ALU.subtract).then_inc(evac_v, 1)
                            continue
                        dve.wait_ge(turned, c + 1)
                        if normed:
                            nc.vector.tensor_scalar(sT[:, c, :], pT[:, c % 4, 0:SEQ], gcol[:, c:c + 1], None,
                                                    ALU.mult).then_inc(evac_v, 1)
                        else:
                            nc.vector.tensor_copy(sT[:, c, :], pT[:, c % 4, 0:SEQ]).then_inc(evac_v, 1)
                    dve.sem_inc(out_v, 2)
                    dve.sem_inc(lo_ready, 2)

                    def low_part(w, tile, put, at, slot, turn):
                        dve.wait_ge(hi_ready, at + 1)
                        nc.vector.scalar_tensor_tensor(w_lo[:, slot, :, 0:tile], wt[:, slot, :, 0:tile], W_SCALE,
                                                       w_hi[:, slot, :, 0:tile], ALU.mult,
                                                       ALU.subtract).then_inc(lo_ready, 1)

                    def move(w, tile, put, at, slot, turn, col):
                        dve.wait_ge(product, at + 3)
                        if isinstance(put, tuple):
                            for t in range(TT):
                                into = put[1][:, t, bass.ds(col, tile)]
                                ins = nc.vector.scalar_tensor_tensor(into, pY[:, slot, t, 0:tile], back, into,
                                                                     ALU.mult, ALU.add)
                            ins.then_inc(out_v, 1)
                        else:
                            nc.vector.tensor_scalar(put[:, 1, bass.ds(col, tile)], pY[:, slot, 1, 0:tile], back,
                                                    None, ALU.mult).then_inc(out_v, 1)
                    over_tiles(dve, move, ahead=low_part if split else None)

                @block.tensor
                def _(pe):
                    if normed:
                        pe.wait_ge(normed_ready, TT)
                    for c in range(kc):
                        if c >= 4:
                            if split:
                                pe.wait_ge(evac_v, c - 3)
                            else:
                                pe.wait_ge(evac_a if c % 2 else evac_v, (c - 4) // 2 + 1)
                        for t in range(TT):
                            ins = nc.tensor.transpose(pT[:, c % 4, t * P:(t + 1) * P],
                                                      xn[:, t, c::kc], con["identity"])
                        ins.then_inc(turned, 1)
                    pe.sem_inc(product, 2)
                    pe.wait_ge(evac_v, kc if split else (kc + 1) // 2)
                    if kc > 1 and not split:
                        pe.wait_ge(evac_a, kc // 2)

                    def multiply(w, tile, put, at, slot, turn, col):
                        if split:
                            pe.wait_ge(lo_ready, at + 3)
                            terms = [(sT_hi, w_hi), (sT_hi, w_lo), (sT_lo, w_hi)]
                        else:
                            pe.wait_ge(w_in[slot], turn * 16 + 16)
                            terms = [(sT, wt)]
                        if not isinstance(put, tuple):
                            pe.wait_ge(out_a, at + 1)
                        pe.wait_ge(out_v, at + 1)
                        steps = [(c, x, y) for c in range(kc) for x, y in terms]
                        for t in range(TT):
                            for n, (c, x, y) in enumerate(steps):
                                ins = nc.tensor.matmul(pY[:, slot, t, 0:tile], x[:, c, t * P:(t + 1) * P],
                                                       y[:, slot, c, 0:tile], start=(n == 0),
                                                       stop=(n == len(steps) - 1))
                        ins.then_inc(product, 1)
                    over_tiles(pe, multiply)



ATTN_SLOTS = 4


def attention(nc, name, con, heads, q, k, v, dqk, dv, q_col, k_col, v_col, scale, mask, out,
              spans=SPAN, blocks=KEY_BLOCKS, key_tiles=TT, key_rows=P, empty_rows=False):
    G = ATTN_SLOTS
    turns = heads // G
    ncol = spans[-1][1] + spans[-1][2]
    kw = key_rows if key_tiles == 1 else P
    with ExitStack() as ctx:
        sb = lambda n, s, d=F32: ctx.enter_context(nc.sbuf_tensor(f"{name}_{n}", s, d))
        q_head = sb("q_head", [P, G, TT, dqk])
        k_head = sb("k_head", [P, G, key_tiles, dqk])
        qkT = sb("qkT", [P, G, TT * P + key_tiles * P])
        S = sb("S", [P, G, ncol])
        E = sb("E", [P, G, ncol])
        ET = sb("ET", [P, G, len(blocks) * P])
        row_max = sb("row_max", [P, G, TT])
        bias = sb("bias", [P, G, TT])
        den = sb("den", [P, G, TT])
        rden = sb("rden", [P, G, TT])
        pT = ctx.enter_context(nc.psum_tensor(f"{name}_pT", [P, G, 512], F32))
        pS = ctx.enter_context(nc.psum_tensor(f"{name}_pS", [P, G, 512], F32))
        qw = TT * P
        with Stage(nc, name, ["q_staged", "k_staged", "heads_turned", "heads_out", "scored", "biased", "exped",
                              "probs_turned", "probs_out", "summed", "done", "vlink", "pool_passed",
                              "dve_passed", "pe_passed"]) as sems:
            (q_staged, k_staged, heads_turned, heads_out, scored, biased, exped, probs_turned, probs_out,
             summed, done, vlink, pool_passed, dve_passed, pe_passed) = sems
            with nc.Block(no_gpsimd_drain=True) as block:
                @block.gpsimd
                def _(pool):
                    with pool.Fori(0, turns) as i:
                        for s in range(G):
                            wait_alone(pool, pool_passed, heads_turned, i * G + (s + 1))
                            src = k[0:kw, :, bass.ds(k_col(i, s), dqk)] if key_tiles > 1 else \
                                k[0:kw, bass.ds(k_col(i, s), dqk)]
                            dst = k_head[0:kw, s, :, :] if key_tiles > 1 else k_head[0:kw, s, 0, :]
                            nc.gpsimd.tensor_copy(dst, src).then_inc(k_staged, 1)

                @block.scalar
                def _(act):
                    with act.Fori(0, turns) as i:
                        for s in range(G):
                            act.wait_ge(heads_turned, i * G + (s + 1))
                            nc.scalar.activation(q_head[:, s, :, :], q[:, :, bass.ds(q_col(i, s), dqk)],
                                                 ACT.Copy).then_inc(q_staged, 1)
                        for s in range(G):
                            act.wait_ge(heads_turned, i * G + (s + 1 + G))
                            nc.scalar.activation(qkT[0:dqk, s, 0:qw + key_tiles * kw],
                                                 pT[0:dqk, s, 0:qw + key_tiles * kw],
                                                 ACT.Copy).then_inc(heads_out, 1)
                        for s in range(G):
                            act.wait_ge(biased, i * G + (s + 1))
                            for t, c0, nk in spans:
                                ins = nc.scalar.activation(E[:, s, c0:c0 + nk], S[:, s, c0:c0 + nk], ACT.Exp,
                                                           bias=bias[:, s, t:t + 1], scale=scale,
                                                           accum_out=den[:, s, t:t + 1])
                            ins.then_inc(exped, 1)

                @block.vector
                def _(dve):
                    dve.sem_inc(probs_out, G)
                    dve.sem_inc(done, G)
                    with dve.Fori(0, turns) as i:
                        link = Link(dve, vlink, i * (3 * G if empty_rows else 2 * G))
                        for s in range(G):
                            wait_alone(dve, dve_passed, scored, i * G + (s + 1))
                            for t, c0, nk in spans:
                                ins = nc.vector.tensor_tensor_reduce(
                                    S[:, s, c0:c0 + nk], pS[:, s, c0:c0 + nk], mask[:, c0:c0 + nk], 1.0, LEAST_MAX,
                                    ALU.add, ALU.max, row_max[:, s, t:t + 1])
                            link(ins)
                            nc.vector.tensor_scalar(bias[:, s, :], row_max[:, s, :], -scale, None,
                                                    ALU.mult).then_inc(biased, 1)
                        for s in range(G):
                            dve.wait_ge(probs_turned, i * G + (s + 1))
                            nc.vector.tensor_copy(ET[0:kw, s, :], pT[0:kw, s, 0:len(blocks) * P])\
                                .then_inc(probs_out, 1)
                            if empty_rows:
                                link(nc.vector.tensor_scalar(den[:, s, :], den[:, s, :], 1e-30, None, ALU.max))
                            link(nc.vector.reciprocal(rden[:, s, :], den[:, s, :]))
                        for s in range(G):
                            dve.wait_ge(summed, i * G + (s + 1))
                            for t in range(TT):
                                ins = nc.vector.tensor_scalar(
                                    out[:, t, bass.ds(i * (G * dv) + s * dv, dv)],
                                    pS[:, s, t * dv:(t + 1) * dv], rden[:, s, t:t + 1], None, ALU.mult)
                            ins.then_inc(done, 1)

                @block.tensor
                def _(pe):
                    pe.sem_inc(heads_turned, G)
                    ident = con["identity"]
                    with pe.Fori(0, turns) as i:
                        for s in range(G):
                            pe.wait_ge(q_staged, i * G + (s + 1))
                            pe.wait_ge(k_staged, i * G + (s + 1))
                            wait_alone(pe, pe_passed, probs_out, i * G + (s + 1))
                            for t in range(TT):
                                nc.tensor.transpose(pT[0:dqk, s, t * P:(t + 1) * P], q_head[:, s, t, :], ident)
                            for t in range(key_tiles):
                                ins = nc.tensor.transpose(pT[0:dqk, s, qw + t * kw:qw + (t + 1) * kw],
                                                          k_head[0:kw, s, t, :], ident[0:kw, 0:kw])
                            ins.then_inc(heads_turned, 1)
                        for s in range(G):
                            pe.wait_ge(heads_out, i * G + (s + 1))
                            pe.wait_ge(done, i * G + (s + 1))
                            for t, c0, nk in spans:
                                ins = nc.tensor.matmul(pS[:, s, c0:c0 + nk], qkT[0:dqk, s, t * P:(t + 1) * P],
                                                       qkT[0:dqk, s, qw:qw + nk], start=True, stop=True)
                            ins.then_inc(scored, 1)
                        for s in range(G):
                            wait_alone(pe, pe_passed, exped, i * G + (s + 1))
                            for n, (t, kb, c0, nk) in enumerate(blocks):
                                ins = nc.tensor.transpose(pT[0:nk, s, n * P:(n + 1) * P], E[:, s, c0:c0 + nk], ident)
                            ins.then_inc(probs_turned, 1)
                        for s in range(G):
                            wait_alone(pe, pe_passed, probs_out, i * G + (s + 1 + G))
                            for n, (t, kb, c0, nk) in enumerate(blocks):
                                vv = v[0:nk, kb, bass.ds(v_col(i, s), dv)] if key_tiles > 1 else \
                                    v[0:nk, bass.ds(v_col(i, s), dv)]
                                first = n == 0 or blocks[n - 1][0] != t
                                last = n == len(blocks) - 1 or blocks[n + 1][0] != t
                                ins = nc.tensor.matmul(pS[:, s, t * dv:(t + 1) * dv], ET[0:nk, s, n * P:(n + 1) * P],
                                                       vv, start=first, stop=last)
                            ins.then_inc(summed, 1)


def swiglu(nc, name, con, hT, n_blocks, w_gate, w_up, w_down, combine, x):
    NJ = D_EXPERT // P
    pairs = (n_blocks - 1) // 2
    hT_hi, hT_lo = hT
    with ExitStack() as ctx:
        sb = lambda n, s, d=F32: ctx.enter_context(nc.sbuf_tensor(f"{name}_{n}", s, d))
        w_up32 = sb("w_up32", [P, 2, 2, KC, D_EXPERT])
        w_down32 = sb("w_down32", [P, 2, NJ, D])
        wu_hi = sb("wu_hi", [P, 2, 2, KC, D_EXPERT], F16)
        wu_lo = sb("wu_lo", [P, 2, 2, KC, D_EXPERT], F16)
        wd_hi = sb("wd_hi", [P, 2, NJ, D], F16)
        wd_lo = sb("wd_lo", [P, 2, NJ, D], F16)
        weight = sb("weight", [P, 2, SEQ])
        gated = sb("gated", [P, 2, NJ * SEQ])
        hidden = sb("hidden", [P, 2, NJ * SEQ])
        h_hi = sb("h_hi", [P, 2, NJ * SEQ], F16)
        h_lo = sb("h_lo", [P, 2, NJ * SEQ], F16)
        zeros = sb("zeros", [P, 512], BF16)
        pG = ctx.enter_context(nc.psum_tensor(f"{name}_pG", [P, 2, 512], F32))
        pU = ctx.enter_context(nc.psum_tensor(f"{name}_pU", [P, 2, 512], F32))
        pY = ctx.enter_context(nc.psum_tensor(f"{name}_pY", [P, TT, D], F32))
        with Stage(nc, name, ["up0_in", "up1_in", "down0_in", "down1_in", "weight0_in", "weight1_in", "zeroed",
                              "up_hi", "up_lo", "down_hi", "down_lo", "up_done", "silu_done", "hidden_ready",
                              "hidden_hi", "hidden_lo", "down_done", "summed", "vlink"]) as sems:
            (up0_in, up1_in, down0_in, down1_in, weight0_in, weight1_in, zeroed, up_hi, up_lo, down_hi, down_lo,
             up_done, silu_done, hidden_ready, hidden_hi, hidden_lo, down_done, summed, vlink) = sems
            up_in, down_in, weight_in = [up0_in, up1_in], [down0_in, down1_in], [weight0_in, weight1_in]

            def blocks_with_next(eng, split_up, rest):
                split_up(0, 0, 0)
                with eng.Fori(0, pairs) as i:
                    split_up(i * 2 + 1, 1, i)
                    rest(i * 2, 0, i)
                    split_up(i * 2 + 2, 0, i + 1)
                    rest(i * 2 + 1, 1, i)
                if n_blocks % 2 == 0:
                    split_up(n_blocks - 1, 1, pairs)
                    rest(n_blocks - 2, 0, pairs)
                rest(n_blocks - 1, (n_blocks - 1) % 2, pairs)

            with nc.Block(no_gpsimd_drain=True) as block:
                @block.sync
                def _(sp):
                    def load(e, s):
                        sp.wait_ge(up_lo, e + 1)
                        sp.dma_start(w_up32[:, s, 0, :, :], w_gate(e)).then_inc(up_in[s], 16)
                        sp.dma_start(w_up32[:, s, 1, :, :], w_up(e)).then_inc(up_in[s], 16)
                        if combine:
                            sp.wait_ge(hidden_ready, e + 1)
                            sp.dma_start(weight[:, s, :], combine(e)).then_inc(weight_in[s], 16)
                        sp.wait_ge(down_lo, e + 1)
                        sp.dma_start(w_down32[:, s, :, :], w_down(e)).then_inc(down_in[s], 16)
                    with sp.Fori(0, n_blocks // 2) as i:
                        for s in range(2):
                            load(i * 2 + s, s)
                    if n_blocks % 2:
                        load(n_blocks - 1, 0)

                @block.scalar
                def _(act):
                    def split_up(e, s, turn):
                        act.wait_ge(up_in[s], turn * 32 + 32)
                        act.wait_ge(up_done, e + 1)
                        for m in range(2):
                            ins = nc.scalar.activation(wu_hi[:, s, m, :, :], w_up32[:, s, m, :, :], ACT.Copy,
                                                       scale=W_SCALE)
                        ins.then_inc(up_hi, 1)

                    def rest(e, s, turn):
                        act.wait_ge(up_done, e + 3)
                        act.wait_ge(hidden_ready, e + 1)
                        nc.scalar.activation(gated[:, s, :], pG[:, s, :], ACT.Silu,
                                             scale=1.0 / W_SCALE).then_inc(silu_done, 1)
                        act.wait_ge(down_done, e + 1)
                        act.wait_ge(down_in[s], turn * 16 + 16)
                        nc.scalar.activation(wd_hi[:, s, :, :], w_down32[:, s, :, :], ACT.Copy,
                                             scale=W_SCALE).then_inc(down_hi, 1)
                        act.wait_ge(hidden_ready, e + 3)
                        nc.scalar.activation(h_hi[:, s, :], hidden[:, s, :], ACT.Copy).then_inc(hidden_hi, 1)
                    blocks_with_next(act, split_up, rest)

                @block.vector
                def _(dve):
                    nc.vector.memset(zeros[:], 0.0).then_inc(zeroed, 1)
                    dve.sem_inc(hidden_ready, 2)
                    dve.sem_inc(up_lo, 2)
                    dve.sem_inc(down_lo, 2)

                    def less(out, whole, scale, hi):
                        return nc.vector.scalar_tensor_tensor(out, whole, scale, hi, ALU.mult, ALU.subtract)

                    def split_up(e, s, turn):
                        dve.wait_ge(up_hi, e + 1)
                        for m in range(2):
                            ins = less(wu_lo[:, s, m, :, :].rearrange("p c n -> p (c n)"),
                                       w_up32[:, s, m, :, :].rearrange("p c n -> p (c n)"), W_SCALE,
                                       wu_hi[:, s, m, :, :].rearrange("p c n -> p (c n)"))
                        ins.then_inc(up_lo, 1)

                    def rest(e, s, turn):
                        dve.wait_ge(silu_done, e + 1)
                        into = hidden[:, s, :]
                        ins = nc.vector.scalar_tensor_tensor(into, pU[:, s, :], 1.0 / W_SCALE, gated[:, s, :],
                                                             ALU.mult, ALU.mult)
                        if combine:
                            Link(dve, vlink, e)(ins)
                            dve.wait_ge(weight_in[s], turn * 16 + 16)
                            into3 = into.rearrange("p (j n) -> p j n", j=NJ)
                            by = weight[:, s, :].unsqueeze(1).broadcast_to([P, NJ, SEQ])
                            ins = nc.vector.tensor_tensor(into3, into3, by, ALU.mult)
                        ins.then_inc(hidden_ready, 1)
                        dve.wait_ge(down_hi, e + 1)
                        less(wd_lo[:, s, :, :].rearrange("p c n -> p (c n)"),
                             w_down32[:, s, :, :].rearrange("p c n -> p (c n)"), W_SCALE,
                             wd_hi[:, s, :, :].rearrange("p c n -> p (c n)")).then_inc(down_lo, 1)
                        dve.wait_ge(hidden_hi, e + 1)
                        less(h_lo[:, s, :], into, 1.0, h_hi[:, s, :]).then_inc(hidden_lo, 1)
                    blocks_with_next(dve, split_up, rest)
                    dve.wait_ge(summed, 1)
                    for t in range(TT):
                        ins = nc.vector.scalar_tensor_tensor(x[:, t, :], pY[:, t, :], 1.0 / W_SCALE, x[:, t, :],
                                                             ALU.mult, ALU.add)
                    ins.then_inc(vlink, 1)

                @block.tensor
                def _(pe):
                    def all_sums(start, stop):
                        for t in range(TT):
                            for h in range(2):
                                ins = nc.tensor.matmul(pY[:, t, h * 512:(h + 1) * 512], zeros[:, 0:P], zeros[:],
                                                       start=start, stop=stop, skip_group_check=True)
                        return ins

                    def up(e, s, turn):
                        pe.wait_ge(up_lo, e + 3)
                        for m, p in enumerate((pG, pU)):
                            for j in range(NJ):
                                n = 0
                                for c in range(KC):
                                    for w, h in ((wu_hi, hT_hi), (wu_hi, hT_lo), (wu_lo, hT_hi)):
                                        ins = nc.tensor.matmul(p[:, s, j * SEQ:(j + 1) * SEQ], w[:, s, m, c, j::NJ],
                                                               h[:, c, :], start=(n == 0), stop=(n == 3 * KC - 1))
                                        n += 1
                        ins.then_inc(up_done, 1)

                    def down(e, s, turn):
                        pe.wait_ge(down_lo, e + 3)
                        pe.wait_ge(hidden_lo, e + 1)
                        for t in range(TT):
                            for j in range(NJ):
                                at = j * SEQ + t * P
                                for h, w in ((h_hi, wd_hi), (h_hi, wd_lo), (h_lo, wd_hi)):
                                    for half in range(2):
                                        ins = nc.tensor.matmul(pY[:, t, half * 512:(half + 1) * 512],
                                                               h[:, s, at:at + P],
                                                               w[:, s, j, half * 512:(half + 1) * 512],
                                                               start=False, stop=False, skip_group_check=True)
                        ins.then_inc(down_done, 1)

                    pe.sem_inc(up_done, 2)
                    pe.sem_inc(down_done, 2)
                    pe.wait_ge(zeroed, 1)
                    all_sums(True, False)
                    up(0, 0, 0)
                    with pe.Fori(0, pairs) as i:
                        up(i * 2 + 1, 1, i)
                        down(i * 2, 0, i)
                        up(i * 2 + 2, 0, i + 1)
                        down(i * 2 + 1, 1, i)
                    if n_blocks % 2 == 0:
                        up(n_blocks - 1, 1, pairs)
                        down(n_blocks - 2, 0, pairs)
                    down(n_blocks - 1, (n_blocks - 1) % 2, pairs)
                    all_sums(False, True).then_inc(summed, 1)



def rope(link, eng, x, cs, tmp):
    p, tt, heads, d = x.shape
    half = d // 2
    flat = [tmp[:, n, 0:tt * heads * half].rearrange("p (t h d) -> p t h d", t=tt, h=heads) for n in range(4)]
    cos = cs[:, :, 0:half].unsqueeze(2).broadcast_to([p, tt, heads, half])
    sin = cs[:, :, half:d].unsqueeze(2).broadcast_to([p, tt, heads, half])
    x1, x2 = x[:, :, :, 0:half], x[:, :, :, half:d]
    link(eng.tensor_tensor(flat[0], x1, cos, ALU.mult))
    link(eng.tensor_tensor(flat[1], x2, sin, ALU.mult))
    link(eng.tensor_tensor(flat[2], x2, cos, ALU.mult))
    link(eng.tensor_tensor(flat[3], x1, sin, ALU.mult))
    link(eng.tensor_tensor(x1, flat[0], flat[1], ALU.subtract))
    link(eng.tensor_tensor(x2, flat[2], flat[3], ALU.add))


def heads_of(x, n):
    return x.rearrange("p t (h d) -> p t h d", h=n)


def mla_prepare(nc, con, feat, qk, k_nope, positions, g_qn, g_kn):
    name = "mla"
    with ExitStack() as ctx:
        sb = lambda n, s, d=F32: ctx.enter_context(nc.sbuf_tensor(f"{name}_{n}", s, d))
        gains = sb("gains", [P, 2, MLA_QK])
        pos_i = sb("pos_i", [P, TT], I32)
        pos = sb("pos", [P, TT])
        ang = sb("ang", [P, TT, 16])
        turns = sb("turns", [P, TT, 16])
        wrap = sb("wrap", [P, TT, 16])
        cs = sb("cs", [P, TT, 32])
        arg = sb("arg", [P, TT, 32])
        square = sb("square", [P, 2 * TT * MLA_H, MLA_QK])
        st = sb("st", [P, 3, 2 * TT * MLA_H])
        tmp = sb("tmp", [P, 4, TT * MLA_H * 16])
        rows = qk.rearrange("p a t h d -> p (a t h) d")
        with Stage(nc, name, ["gains_in", "k_filled", "angles", "sines", "squares", "recips", "rstd", "vlink"]) as sems:
            gains_in, k_filled, angles, sines, squares, recips, rstd, vlink = sems
            with nc.Block(no_gpsimd_drain=True) as block:
                @block.sync
                def _(sp):
                    sp.dma_start(gains[:, 0, :], spread(g_qn)).then_inc(gains_in, 16)
                    sp.dma_start(gains[:, 1, :], spread(g_kn)).then_inc(gains_in, 16)
                    sp.dma_start(pos_i[:], positions.rearrange("a (t p) -> p (a t)", p=P),
                                 allow_slow_non_contiguous=True).then_inc(gains_in, 16)

                @block.gpsimd
                def _(pool):
                    for t in range(TT):
                        part = feat[:, t, Q_RANK + KV_RANK:MLA_IN].unsqueeze(1).broadcast_to([P, MLA_H, MLA_ROPE])
                        nc.gpsimd.tensor_copy(qk[:, 1, t, :, MLA_NOPE:MLA_QK], part).then_inc(k_filled, 1)
                        nc.gpsimd.tensor_copy(qk[:, 1, t, :, 0:MLA_NOPE],
                                              heads_of(k_nope, MLA_H)[:, t]).then_inc(k_filled, 1)

                @block.scalar
                def _(act):
                    act.wait_ge(k_filled, 2 * TT)
                    nc.scalar.activation(square[:], rows, ACT.Square).then_inc(squares, 1)
                    act.wait_ge(recips, 1)
                    nc.scalar.activation(st[:, 2, :], st[:, 1, :], ACT.Sqrt).then_inc(rstd, 1)
                    act.wait_ge(angles, 1)
                    nc.scalar.activation(cs[:], arg[:], ACT.Sin).then_inc(sines, 1)

                @block.vector
                def _(dve):
                    link = Link(dve, vlink)
                    v = nc.vector
                    dve.wait_ge(gains_in, 48)
                    link(v.tensor_copy(pos[:], pos_i[:]))
                    for t in range(TT):
                        link(v.tensor_scalar(ang[:, t, :], con["inv_freq"], pos[:, t:t + 1], None, ALU.mult))
                    link(v.tensor_scalar(turns[:], ang[:], float(1 / (2 * np.pi)), 12582912.0, ALU.mult, ALU.add))
                    link(v.tensor_scalar(turns[:], turns[:], -12582912.0, None, ALU.add))
                    part = 2 * np.pi
                    for bits in (8, 10, 24):
                        scale = 2.0 ** (bits - 1 - np.floor(np.log2(part)))
                        c = float(np.float32(np.floor(part * scale) / scale))
                        part -= c
                        link(v.scalar_tensor_tensor(ang[:], turns[:], -c, ang[:], ALU.mult, ALU.add))
                    pi = float(np.float32(3.1415925))
                    link(v.tensor_scalar(arg[:, :, 16:32], ang[:], pi, -pi, ALU.min, ALU.max))
                    link(v.tensor_scalar(ang[:], ang[:], float(np.pi / 2), None, ALU.add))
                    link(v.tensor_scalar(wrap[:], ang[:], pi, -2 * float(np.pi), ALU.is_gt, ALU.mult))
                    link(v.tensor_tensor(ang[:], ang[:], wrap[:], ALU.add))
                    v.tensor_scalar(arg[:, :, 0:16], ang[:], pi, -pi, ALU.min, ALU.max).then_inc(angles, 1)
                    dve.wait_ge(squares, 1)
                    link(v.tensor_reduce(st[:, 0, :], square[:], AX_X, ALU.add))
                    link(v.tensor_scalar(st[:, 0, :], st[:, 0, :], 1.0 / MLA_QK, EPS, ALU.mult, ALU.add))
                    v.reciprocal(st[:, 1, :], st[:, 0, :]).then_inc(recips, 1)
                    dve.wait_ge(rstd, 1)
                    link(v.tensor_tensor(rows, rows, st[:, 2, :].unsqueeze(2).broadcast_to(list(rows.shape)),
                                         ALU.mult))
                    for a in range(2):
                        part = qk[:, a].rearrange("p t h d -> p (t h) d")
                        link(v.tensor_tensor(part, part, gains[:, a, :].unsqueeze(1).broadcast_to(list(part.shape)),
                                             ALU.mult))
                    dve.wait_ge(sines, 1)
                    for a in range(2):
                        rope(link, v, qk[:, a, :, :, MLA_NOPE:MLA_QK], cs[:], tmp)


def rms_scale(nc, name, x, width, gain):
    with ExitStack() as ctx:
        sb = lambda n, s, d=F32: ctx.enter_context(nc.sbuf_tensor(f"{name}_{n}", s, d))
        row = sb("row", [P, width])
        sq = sb("sq", [P, TT, width])
        st = sb("st", [P, 3, TT])
        with Stage(nc, name, ["gain_in", "squares", "recips", "rstd", "vlink"]) as sems:
            gain_in, squares, recips, rstd, vlink = sems
            with nc.Block(no_gpsimd_drain=True) as block:
                @block.sync
                def _(sp):
                    sp.dma_start(row[:], spread(gain)).then_inc(gain_in, 16)

                @block.scalar
                def _(act):
                    for t in range(TT):
                        nc.scalar.activation(sq[:, t, :], x[:, t, :], ACT.Square,
                                             accum_out=st[:, 0, t:t + 1]).then_inc(squares, 1)
                    act.wait_ge(recips, 1)
                    nc.scalar.activation(st[:, 2, :], st[:, 1, :], ACT.Sqrt).then_inc(rstd, 1)

                @block.vector
                def _(dve):
                    link = Link(dve, vlink)
                    dve.wait_ge(squares, TT)
                    link(nc.vector.tensor_scalar(st[:, 0, :], st[:, 0, :], 1.0 / width, EPS, ALU.mult, ALU.add))
                    nc.vector.reciprocal(st[:, 1, :], st[:, 0, :]).then_inc(recips, 1)
                    dve.wait_ge(rstd, 1)
                    dve.wait_ge(gain_in, 16)
                    for t in range(TT):
                        link(nc.vector.scalar_tensor_tensor(x[:, t, :], x[:, t, :], st[:, 2, t:t + 1], row[:],
                                                            ALU.mult, ALU.mult))


DECAY = float(np.exp(-0.5))


def rwkv(nc, con, feat, w, out):
    HT = RW_H * TT
    with ExitStack() as ctx:
        sb = lambda n, s, d=F32: ctx.enter_context(nc.sbuf_tensor(f"rw_{n}", s, d))
        row = sb("row", [P, 7, RW_W])
        W0, A0, K_K, K_A, R_K, LNX_G, LNX_B = range(7)
        lora = sb("lora", [P, 2, RW_W])
        sig = sb("sig", [P, TT, RW_W])
        a = sb("a", [P, TT, RW_W])
        g = sb("g", [P, TT, RW_W])
        r, k, v = (feat[:, :, n * RW_W:(n + 1) * RW_W] for n in range(3))
        bonus = sb("bonus", [P, HT])

        with ExitStack() as inner:
            sbi = lambda n, s, d=F32: inner.enter_context(nc.sbuf_tensor(f"rw1_{n}", s, d))
            mu = sbi("mu", [P, RW_IN])
            prev = sbi("prev", [P, TT, RW_IN])
            loraT = sbi("loraT", [P, TT, 2, P])
            pT = inner.enter_context(nc.psum_tensor("rw1_pT", [P, TT, 512], F32))
            pL = inner.enter_context(nc.psum_tensor("rw1_pL", [P, 3, TT, 512], F32))
            with Stage(nc, "rw1", ["rows_in", "lora_in", "mu_in", "first_zero", "prev_in", "mixed", "squashed",
                                   "turned", "turned_out", "products", "zw_ready", "za_ready", "g_ready",
                                   "vlink"]) as sems:
                (rows_in, lora_in, mu_in, first_zero, prev_in, mixed, squashed, turned, turned_out, products,
                 zw_ready, za_ready, g_ready, vlink) = sems
                with nc.Block(no_gpsimd_drain=True) as block:
                    @block.sync
                    def _(sp):
                        sp.dma_start(prev[1:P, :, :], feat[0:P - 1, :, :]).then_inc(prev_in, 16)
                        sp.dma_start(prev[0:1, 1, :], feat[P - 1:P, 0, :]).then_inc(prev_in, 16)
                        sp.dma_start(mu[:], spread(w["rw_mu"])).then_inc(mu_in, 16)
                        sp.dma_start(lora[0:64, 0, :], w["rw_w2"]).then_inc(lora_in, 16)
                        sp.dma_start(lora[64:P, 0, :], w["rw_a2"]).then_inc(lora_in, 16)
                        sp.dma_start(lora[:, 1, :], w["rw_g2"]).then_inc(lora_in, 16)
                        names = ["rw_w0", "rw_a0", "rw_k_k", "rw_k_a", "rw_r_k", "rw_lnx_g", "rw_lnx_b"]
                        for n, x in enumerate(names):
                            sp.dma_start(row[:, n, :], spread(w[x])).then_inc(rows_in, 16)
                        sp.wait_ge(rows_in, 16 * len(names))

                    @block.gpsimd
                    def _(pool):
                        nc.gpsimd.memset(prev[0:1, 0, :], 0.0).then_inc(first_zero, 1)

                    @block.vector
                    def _(dve):
                        link = Link(dve, vlink)
                        dve.wait_ge(prev_in, 32)
                        dve.wait_ge(first_zero, 1)
                        link(nc.vector.tensor_tensor(prev[:], prev[:], feat, ALU.subtract))
                        dve.wait_ge(mu_in, 16)
                        link(nc.vector.tensor_tensor(prev[:], prev[:],
                                                     mu[:].unsqueeze(1).broadcast_to([P, TT, RW_IN]), ALU.mult))
                        nc.vector.tensor_tensor(feat, feat, prev[:], ALU.add).then_inc(mixed, 1)
                        for t in range(TT):
                            dve.wait_ge(turned, t + 1)
                            nc.vector.tensor_copy(loraT[:, t, :, :], pT[:, t, 0:2 * P]
                                                  .rearrange("p (a n) -> p a n", a=2)).then_inc(turned_out, 1)
                        dve.wait_ge(products, 1)
                        dve.wait_ge(rows_in, 16 * 7)
                        for t in range(TT):
                            nc.vector.tensor_tensor(sig[:, t, :], pL[:, 0, t, :], row[:, W0, :],
                                                    ALU.add).then_inc(zw_ready, 1)
                            nc.vector.tensor_tensor(a[:, t, :], pL[:, 1, t, :], row[:, A0, :],
                                                    ALU.add).then_inc(za_ready, 1)

                    @block.scalar
                    def _(act):
                        act.wait_ge(mixed, 1)
                        nc.scalar.activation(feat[:, :, 1536:1600], feat[:, :, 1536:1600],
                                             ACT.Tanh).then_inc(squashed, 1)
                        nc.scalar.activation(feat[:, :, 1664:RW_IN], feat[:, :, 1664:RW_IN],
                                             ACT.Sigmoid).then_inc(squashed, 1)
                        act.wait_ge(zw_ready, TT)
                        nc.scalar.activation(sig[:], sig[:], ACT.Sigmoid).then_inc(g_ready, 1)
                        act.wait_ge(za_ready, TT)
                        nc.scalar.activation(a[:], a[:], ACT.Sigmoid).then_inc(g_ready, 1)
                        for t in range(TT):
                            nc.scalar.activation(g[:, t, :], pL[:, 2, t, :], ACT.Copy).then_inc(g_ready, 1)

                    @block.tensor
                    def _(pe):
                        pe.wait_ge(squashed, 2)
                        for t in range(TT):
                            for c in range(2):
                                ins = nc.tensor.transpose(pT[:, t, c * P:(c + 1) * P],
                                                          feat[:, t, 1536 + c * P:1536 + (c + 1) * P],
                                                          con["identity"])
                            ins.then_inc(turned, 1)
                        pe.wait_ge(lora_in, 48)
                        for t in range(TT):
                            pe.wait_ge(turned_out, t + 1)
                            nc.tensor.matmul(pL[:, 0, t, :], loraT[0:64, t, 0, :], lora[0:64, 0, :],
                                             start=True, stop=True)
                            nc.tensor.matmul(pL[:, 1, t, :], loraT[64:P, t, 0, :], lora[64:P, 0, :],
                                             start=True, stop=True)
                            ins = nc.tensor.matmul(pL[:, 2, t, :], loraT[:, t, 1, :], lora[:, 1, :],
                                                   start=True, stop=True)
                        ins.then_inc(products, 1)

        kkd = sb("kkd", [P, TT, RW_W])
        rd = sb("rd", [P, TT, RW_W])
        bd = sb("bd", [P, TT, RW_W])
        kd = sb("kd", [P, TT, RW_W])
        carry = sb("carry", [P, RW_H // 2])
        with ExitStack() as inner:
            sbi = lambda n, s, d=F32: inner.enter_context(nc.sbuf_tensor(f"rw2_{n}", s, d))
            decay = sbi("decay", [P, TT, RW_W])
            undo = sbi("undo", [P, TT, RW_W])
            before = sbi("before", [P, TT, RW_W])
            tmp = sbi("tmp", [P, TT, RW_W])
            st = sbi("st", [P, 3, HT])
            pD = inner.enter_context(nc.psum_tensor("rw2_pD", [P, 2, TT, 512], F32))
            pC = inner.enter_context(nc.psum_tensor("rw2_pC", [P, 512], F32))
            flat = lambda x: x.rearrange("p t (h d) -> p (t h) d", h=RW_H)
            with Stage(nc, "rw2", ["sums", "ends", "exps", "norms", "roots", "vlink"]) as sems:
                sums, ends, exps, norms, roots, vlink = sems
                with nc.Block(no_gpsimd_drain=True) as block:
                    @block.tensor
                    def _(pe):
                        for t in range(TT):
                            for n in range(2):
                                ins = nc.tensor.matmul(pD[:, n, t, :], con["decay_sums"][:, n * P:(n + 1) * P],
                                                       sig[:, t, :], start=True, stop=True)
                        ins.then_inc(sums, 1)
                        for m in range(RW_H // 2):
                            for t in range(TT):
                                ins = nc.tensor.matmul(pC[:, m:m + 1], sig[:, t, m * P:(m + 1) * P],
                                                       con["decay_ends"][:, t:t + 1], start=(t == 0), stop=(t == 1))
                        ins.then_inc(ends, 1)

                    @block.scalar
                    def _(act):
                        act.wait_ge(sums, 1)
                        for t in range(TT):
                            nc.scalar.activation(decay[:, t, :], pD[:, 0, t, :], ACT.Exp, scale=-DECAY).then_inc(exps, 1)
                            nc.scalar.activation(undo[:, t, :], pD[:, 0, t, :], ACT.Exp, scale=DECAY).then_inc(exps, 1)
                            nc.scalar.activation(before[:, t, :], pD[:, 1, t, :], ACT.Exp,
                                                 scale=-DECAY).then_inc(exps, 1)
                        act.wait_ge(ends, 1)
                        nc.scalar.activation(carry[:], pC[:, 0:RW_H // 2], ACT.Exp, scale=-DECAY).then_inc(exps, 1)
                        act.wait_ge(norms, 1)
                        nc.scalar.activation(st[:, 2, :], st[:, 1, :], ACT.Sqrt).then_inc(roots, 1)

                    @block.vector
                    def _(dve):
                        link = Link(dve, vlink)
                        tt = lambda o, x, y, op=ALU.mult: link(nc.vector.tensor_tensor(o, x, y, op))
                        rows = lambda n: row[:, n, :].unsqueeze(1).broadcast_to([P, TT, RW_W])
                        tt(kkd[:], k, rows(K_K))
                        tt(tmp[:], kkd[:], kkd[:])
                        link(nc.vector.tensor_reduce(st[:, 0, :], flat(tmp[:]), AX_X, ALU.add))
                        link(nc.vector.tensor_scalar(st[:, 0, :], st[:, 0, :], 1e-12, None, ALU.add))
                        nc.vector.reciprocal(st[:, 1, :], st[:, 0, :]).then_inc(norms, 1)
                        link(nc.vector.tensor_scalar(tmp[:], a[:], -1.0, None, ALU.add))
                        tt(tmp[:], tmp[:], rows(K_A))
                        link(nc.vector.tensor_scalar(tmp[:], tmp[:], 1.0, None, ALU.add))
                        tt(k, k, tmp[:])
                        tt(tmp[:], r, k)
                        tt(tmp[:], tmp[:], rows(R_K))
                        link(nc.vector.tensor_reduce(bonus[:], flat(tmp[:]), AX_X, ALU.add))
                        dve.wait_ge(roots, 1)
                        tt(flat(kkd[:]), flat(kkd[:]), st[:, 2, :].unsqueeze(2).broadcast_to([P, HT, RW_N]))
                        tt(bd[:], kkd[:], a[:])
                        dve.wait_ge(exps, 7)
                        tt(rd[:], r, decay[:])
                        tt(kkd[:], kkd[:], before[:])
                        tt(bd[:], bd[:], undo[:])
                        tt(kd[:], k, undo[:])

        AT = sb("AT", [P, HT, P])
        ET = sb("ET", [P, HT, P])
        BT = sb("BT", [P, HT, P])
        FT = sb("FT", [P, HT, P])
        X = sb("X", [P, HT, P])
        XT = sb("XT", [P, HT, P])
        turned4 = sb("turned4", [P, TT * 4, 4 * P])
        KKT, RT, BBT, KT = range(4)
        masks = con["level_masks"]
        mask = lambda n: masks[:, n * P:(n + 1) * P]
        UPTO, STRICT, LEVEL0_T = SOLVE_LEVELS + 1, SOLVE_LEVELS + 2, SOLVE_LEVELS
        with ExitStack() as inner:
            pQ = inner.enter_context(nc.psum_tensor("rw3_p", [P, 8, 512], F32))
            with Stage(nc, "rw3", ["turned", "out_a", "out_v", "products", "masked", "vlink"]) as sems:
                turned, out_a, out_v, products, masked, vlink = sems
                with nc.Block(no_gpsimd_drain=True) as block:
                    @block.tensor
                    def _(pe):
                        for n in range(TT * 4):
                            t, m = divmod(n, 4)
                            for q, x in enumerate((kkd, rd, bd, kd)):
                                ins = nc.tensor.transpose(pQ[:, n, q * P:(q + 1) * P], x[:, t, m * P:(m + 1) * P],
                                                          con["identity"])
                            ins.then_inc(turned, 1)
                        for n in range(HT):
                            t, h = divmod(n, RW_H)
                            u = t * 4 + h // 2
                            lo = 64 * (h % 2)
                            part = lambda q, w=P: turned4[lo:lo + 64, u, q * P:q * P + w]
                            b = n % 4 * 2
                            pe.wait_ge(out_a if u % 2 else out_v, u // 2 + 1)
                            if n < 4:
                                pe.wait_ge(out_v, b // 2 + 1)
                                pe.wait_ge(out_a, b // 2 + 1)
                            else:
                                pe.wait_ge(masked, n - 3)
                            nc.tensor.matmul(pQ[:, b, 0:2 * P], part(BBT), part(KKT, 2 * P), start=True, stop=True)
                            nc.tensor.matmul(pQ[:, b, 2 * P:3 * P], part(KKT), part(BBT), start=True, stop=True)
                            nc.tensor.matmul(pQ[:, b + 1, 0:2 * P], part(KT), part(KKT, 2 * P),
                                             start=True, stop=True).then_inc(products, 1)

                    @block.scalar
                    def _(act):
                        for u in range(1, TT * 4, 2):
                            act.wait_ge(turned, u + 1)
                            nc.scalar.activation(turned4[:, u, :], pQ[:, u, :], ACT.Copy).then_inc(out_a, 1)

                    @block.vector
                    def _(dve):
                        for u in range(0, TT * 4, 2):
                            dve.wait_ge(turned, u + 1)
                            nc.vector.tensor_copy(turned4[:, u, :], pQ[:, u, :]).then_inc(out_v, 1)
                        link = Link(dve, vlink)
                        tt = nc.vector.tensor_tensor
                        for n in range(HT):
                            b = n % 4 * 2
                            dve.wait_ge(products, n + 1)
                            tt(X[:, n, :], pQ[:, b, 2 * P:3 * P], mask(LEVEL0_T), ALU.mult)
                            tt(XT[:, n, :], pQ[:, b, 0:P], mask(0), ALU.mult)
                            tt(AT[:, n, :], pQ[:, b, 0:P], mask(STRICT), ALU.mult)
                            tt(ET[:, n, :], pQ[:, b, P:2 * P], mask(UPTO), ALU.mult)
                            tt(BT[:, n, :], pQ[:, b + 1, 0:P], mask(STRICT), ALU.mult)
                            tt(FT[:, n, :], pQ[:, b + 1, P:2 * P], mask(UPTO), ALU.mult).then_inc(masked, 1)
                        dve.wait_ge(masked, HT)
                        ident = con["identity"].unsqueeze(1).broadcast_to([P, HT, P])
                        link(tt(X[:], ident, X[:], ALU.subtract))
                        link(tt(XT[:], ident, XT[:], ALU.subtract))

        with ExitStack() as inner:
            sbi = lambda n, s, d=F32: inner.enter_context(nc.sbuf_tensor(f"rw4_{n}", s, d))
            offT = sbi("offT", [P, HT, P])
            Wm = sbi("Wm", [P, HT, P])
            pW = inner.enter_context(nc.psum_tensor("rw4_pW", [P, 4, 512], F32))
            pX = inner.enter_context(nc.psum_tensor("rw4_pX", [P, 4, 512], F32))
            GR = 4
            with Stage(nc, "rw4", ["off_ready", "w_done", "w_out", "xt_done", "x_done", "xt_new", "x_new",
                                   "pool_passed"]) as sems:
                off_ready, w_done, w_out, xt_done, x_done, xt_new, x_new, pool_passed = sems
                with nc.Block(no_gpsimd_drain=True) as block:
                    def group(x, q):
                        return x[:, q * GR:(q + 1) * GR, :]

                    def bank(p, q):
                        return p[:, q, :].rearrange("p (n c) -> p n c", n=GR)

                    @block.gpsimd
                    def _(pool):
                        with pool.Fori(0, SOLVE_LEVELS - 1) as i:
                            for q in range(GR):
                                wait_alone(pool, pool_passed, w_done, i * GR + (q + 1))
                                lev = masks[:, bass.ds(i * P + P, P)].unsqueeze(1).broadcast_to([P, GR, P])
                                nc.gpsimd.tensor_tensor(group(offT, q), group(AT, q), lev,
                                                        ALU.mult).then_inc(off_ready, 1)

                    @block.tensor
                    def _(pe):
                        pe.sem_inc(w_done, GR)
                        with pe.Fori(0, SOLVE_LEVELS - 1) as i:
                            for q in range(GR):
                                pe.wait_ge(off_ready, i * GR + (q + 1))
                                pe.wait_ge(x_new, i * GR + (q + 1))
                                for n in range(GR):
                                    ins = nc.tensor.matmul(pW[:, q, n * P:(n + 1) * P], offT[:, q * GR + n, :],
                                                           X[:, q * GR + n, :], start=True, stop=True)
                                ins.then_inc(w_done, 1)
                            for q in range(GR):
                                pe.wait_ge(w_out, i * GR + (q + 1))
                                pe.wait_ge(xt_new, i * GR + (q + 1))
                                for n in range(GR):
                                    ins = nc.tensor.matmul(pX[:, q, n * P:(n + 1) * P], Wm[:, q * GR + n, :],
                                                           XT[:, q * GR + n, :], start=True, stop=True)
                                ins.then_inc(xt_done, 1)
                                for n in range(GR):
                                    ins = nc.tensor.matmul(pW[:, q, n * P:(n + 1) * P], XT[:, q * GR + n, :],
                                                           Wm[:, q * GR + n, :], start=True, stop=True)
                                ins.then_inc(x_done, 1)

                    @block.scalar
                    def _(act):
                        with act.Fori(0, SOLVE_LEVELS - 1) as i:
                            for q in range(GR):
                                act.wait_ge(w_done, i * GR + (q + 1 + GR))
                                nc.scalar.activation(group(Wm, q), bank(pW, q), ACT.Copy).then_inc(w_out, 1)

                    @block.vector
                    def _(dve):
                        dve.sem_inc(xt_new, GR)
                        dve.sem_inc(x_new, GR)
                        with dve.Fori(0, SOLVE_LEVELS - 1) as i:
                            for q in range(GR):
                                dve.wait_ge(x_done, i * GR + (q + 1))
                                nc.vector.tensor_tensor(group(XT, q), group(XT, q), bank(pX, q),
                                                        ALU.subtract).then_inc(xt_new, 1)
                                nc.vector.tensor_tensor(group(X, q), group(X, q), bank(pW, q),
                                                        ALU.subtract).then_inc(x_new, 1)

        with ExitStack() as inner:
            sbi = lambda n, s, d=F32: inner.enter_context(nc.sbuf_tensor(f"rw5_{n}", s, d))
            rhs = sbi("rhs", [P, TT, RW_W])
            U = sbi("U", [P, TT, RW_W])
            Z = sbi("Z", [P, 4, P])
            y = sbi("y", [P, TT, RW_W])
            sq = sbi("sq", [P, TT, RW_W])
            st = sbi("st", [P, 4, HT])
            pR = inner.enter_context(nc.psum_tensor("rw5_pR", [P, TT, 512], F32))
            pU = inner.enter_context(nc.psum_tensor("rw5_pU", [P, TT, 512], F32))
            pY = inner.enter_context(nc.psum_tensor("rw5_pY", [P, TT, 512], F32))
            pZ = inner.enter_context(nc.psum_tensor("rw5_pZ", [P, 512], F32))
            with Stage(nc, "rw5", ["r_done", "rhs_ready", "u_done", "u_ready", "z_zero", "z_done", "z_ready", "y_done",
                                   "centred", "squares", "recips", "roots", "vlink"]) as sems:
                (r_done, rhs_ready, u_done, u_ready, z_zero, z_done, z_ready, y_done, centred, squares, recips, roots,
                 vlink) = sems
                with nc.Block(no_gpsimd_drain=True) as block:
                    @block.gpsimd
                    def _(pool):
                        nc.gpsimd.memset(Z[:], 0.0).then_inc(z_zero, 1)

                    @block.tensor
                    def _(pe):
                        def with_state(into, which):
                            for m in range(RW_H // 2):
                                ins = nc.tensor.matmul(into[:, 1, m * P:(m + 1) * P],
                                                       turned4[:, 4 + m, which * P:(which + 1) * P], Z[:, m, :],
                                                       start=False, stop=True, skip_group_check=True)
                            return ins

                        for t in range(TT):
                            if t:
                                pe.wait_ge(z_ready, 1)
                            hs = lambda h: slice(h * RW_N, (h + 1) * RW_N)
                            for h in range(RW_H):
                                ins = nc.tensor.matmul(pR[:, t, hs(h)], BT[:, t * RW_H + h, :], v[:, t, hs(h)],
                                                       start=(h == 0), stop=(t == 0), skip_group_check=True)
                            if t:
                                ins = with_state(pR, KKT)
                            ins.then_inc(r_done, 1)
                            pe.wait_ge(rhs_ready, t + 1)
                            for h in range(RW_H):
                                ins = nc.tensor.matmul(pU[:, t, hs(h)], XT[:, t * RW_H + h, :], rhs[:, t, hs(h)],
                                                       start=True, stop=True)
                            ins.then_inc(u_done, 1)
                            pe.wait_ge(u_ready, t + 1)
                            if t == 0:
                                for m in range(RW_H // 2):
                                    ms = slice(m * P, (m + 1) * P)
                                    nc.tensor.matmul(pZ[:, ms], bd[:, 0, ms], U[:, 0, ms], start=True, stop=False)
                                    ins = nc.tensor.matmul(pZ[:, ms], kd[:, 0, ms], v[:, 0, ms],
                                                           start=False, stop=True)
                                ins.then_inc(z_done, 1)
                            for h in range(RW_H):
                                n = t * RW_H + h
                                nc.tensor.matmul(pY[:, t, hs(h)], ET[:, n, :], U[:, t, hs(h)], start=(h == 0), stop=False,
                                                 skip_group_check=True)
                                ins = nc.tensor.matmul(pY[:, t, hs(h)], FT[:, n, :], v[:, t, hs(h)],
                                                       start=False, stop=(t == 0), skip_group_check=True)
                            if t:
                                ins = with_state(pY, RT)
                            ins.then_inc(y_done, 1)

                    @block.scalar
                    def _(act):
                        act.wait_ge(centred, 1)
                        nc.scalar.activation(sq[:], y[:], ACT.Square).then_inc(squares, 1)
                        act.wait_ge(recips, 1)
                        nc.scalar.activation(st[:, 3, :], st[:, 2, :], ACT.Sqrt).then_inc(roots, 1)

                    @block.vector
                    def _(dve):
                        link = Link(dve, vlink)
                        tt = lambda o, x, y, op=ALU.mult: link(nc.vector.tensor_tensor(o, x, y, op))
                        rows = lambda n: row[:, n, :].unsqueeze(1).broadcast_to([P, TT, RW_W])
                        flat = lambda x: x.rearrange("p t (h d) -> p (t h) d", h=RW_H)
                        each = lambda x: x.unsqueeze(2).broadcast_to([P, HT, RW_N])
                        for t in range(TT):
                            dve.wait_ge(r_done, t + 1)
                            nc.vector.tensor_scalar(rhs[:, t, :], pR[:, t, :], -1.0, None,
                                                    ALU.mult).then_inc(rhs_ready, 1)
                            dve.wait_ge(u_done, t + 1)
                            nc.vector.tensor_copy(U[:, t, :], pU[:, t, :]).then_inc(u_ready, 1)
                            if t == 0:
                                dve.wait_ge(z_done, 1)
                                dve.wait_ge(z_zero, 1)
                                for lo in (0, 64):
                                    own = slice(lo, lo + 64)
                                    ins = nc.vector.tensor_tensor(
                                        Z[own, :, own], pZ[own, :].rearrange("p (m c) -> p m c", m=4)[:, :, own],
                                        carry[own, :].unsqueeze(2).broadcast_to([64, 4, 64]), ALU.mult)
                                ins.then_inc(z_ready, 1)
                        dve.wait_ge(y_done, TT)
                        link(nc.vector.tensor_copy(y[:], pY[:]))
                        link(nc.vector.tensor_reduce(st[:, 0, :], flat(y[:]), AX_X, ALU.add))
                        link(nc.vector.tensor_scalar(st[:, 0, :], st[:, 0, :], 1.0 / RW_N, None, ALU.mult))
                        nc.vector.tensor_tensor(flat(y[:]), flat(y[:]), each(st[:, 0, :]),
                                                ALU.subtract).then_inc(centred, 1)
                        dve.wait_ge(squares, 1)
                        link(nc.vector.tensor_reduce(st[:, 1, :], flat(sq[:]), AX_X, ALU.add))
                        link(nc.vector.tensor_scalar(st[:, 1, :], st[:, 1, :], 1.0 / RW_N, LNX_EPS,
                                                     ALU.mult, ALU.add))
                        nc.vector.reciprocal(st[:, 2, :], st[:, 1, :]).then_inc(recips, 1)
                        dve.wait_ge(roots, 1)
                        tt(flat(y[:]), flat(y[:]), each(st[:, 3, :]))
                        tt(y[:], y[:], rows(LNX_G))
                        tt(y[:], y[:], rows(LNX_B), ALU.add)
                        for t in range(TT):
                            vt = v[:, t, :].rearrange("p (h d) -> p h d", h=RW_H)
                            st_ = sq[:, t, :].rearrange("p (h d) -> p h d", h=RW_H)
                            tt(st_, vt, bonus[:, t * RW_H:(t + 1) * RW_H].unsqueeze(2).broadcast_to(
                                [P, RW_H, RW_N]))
                        tt(y[:], y[:], sq[:], ALU.add)
                        tt(out, y[:], g[:])


def route(nc, con, logits, bias, scratch):
    with ExitStack() as ctx:
        sb = lambda n, s, d=F32: ctx.enter_context(nc.sbuf_tensor(f"rt_{n}", s, d))
        nl = N_GROUPS + N_EXPERTS
        row = sb("row", [P, nl])
        top = sb("top", [P, 8, TT])
        ghot = sb("ghot", [P, TT, N_GROUPS])
        gexp = sb("gexp", [P, TT, N_GROUPS])
        pick = sb("pick", [P, TT, N_GROUPS, PER_GROUP])
        within = sb("within", [P, TT, PER_GROUP])
        hot1 = sb("hot1", [P, TT, PER_GROUP])
        hot2 = sb("hot2", [P, TT, PER_GROUP])
        tmp = sb("tmp", [P, TT, PER_GROUP])
        best = sb("best", [P, TT])
        wT = sb("wT", [N_EXPERTS, SEQ])
        pT = ctx.enter_context(nc.psum_tensor("rt_pT", [P, 512], F32))
        M, M1, M2, GSUM, GP, E2, W1, W2 = range(8)
        with Stage(nc, "rt", ["bias_in", "centred", "gap", "exps", "weights", "turned", "turned_out", "stored",
                              "vlink"]) as sems:
            bias_in, centred, gap, exps, weights, turned, turned_out, stored, vlink = sems
            with nc.Block(no_gpsimd_drain=True) as block:
                @block.sync
                def _(sp):
                    sp.dma_start(row[:, 0:N_GROUPS], spread(bias[0])).then_inc(bias_in, 16)
                    sp.dma_start(row[:, N_GROUPS:nl], spread(bias[1])).then_inc(bias_in, 16)
                    sp.wait_ge(turned_out, 1)
                    sp.dma_start(scratch, wT[:]).then_inc(stored, 16)
                    sp.wait_ge(stored, 16)

                @block.scalar
                def _(act):
                    act.wait_ge(centred, 1)
                    nc.scalar.activation(gexp[:], gexp[:], ACT.Exp).then_inc(exps, 1)
                    act.wait_ge(gap, 1)
                    nc.scalar.activation(top[:, E2, :], top[:, E2, :], ACT.Exp).then_inc(exps, 1)

                @block.tensor
                def _(pe):
                    pe.wait_ge(weights, 1)
                    for t in range(TT):
                        ins = nc.tensor.transpose(pT[0:N_EXPERTS, t * P:(t + 1) * P],
                                                  pick[:, t].rearrange("p g e -> p (g e)"), con["identity"])
                    ins.then_inc(turned, 1)

                @block.vector
                def _(dve):
                    link = Link(dve, vlink)
                    tt = lambda o, x, y, op: link(nc.vector.tensor_tensor(o, x, y, op))
                    over = lambda s, n: s.unsqueeze(2).broadcast_to([P, TT, n])
                    dve.wait_ge(bias_in, 32)
                    tt(logits, logits, row[:].unsqueeze(1).broadcast_to([P, TT, nl]), ALU.add)

                    def first_best(x, n, peak, hot):
                        rank = con["rank8"][:, 0:n].unsqueeze(1).broadcast_to([P, TT, n])
                        link(nc.vector.tensor_reduce(peak, x, AX_X, ALU.max))
                        tt(hot, x, over(peak, n), ALU.is_equal)
                        tt(hot, hot, rank, ALU.mult)
                        link(nc.vector.tensor_reduce(best[:], hot, AX_X, ALU.max))
                        tt(hot, hot, over(best[:], n), ALU.is_equal)

                    groups = logits[:, :, 0:N_GROUPS]
                    experts = logits[:, :, N_GROUPS:nl].rearrange("p t (g e) -> p t g e", g=N_GROUPS)
                    first_best(groups, N_GROUPS, top[:, M, :], ghot[:])
                    nc.vector.tensor_tensor(gexp[:], groups, over(top[:, M, :], N_GROUPS),
                                            ALU.subtract).then_inc(centred, 1)
                    tt(pick[:], experts, ghot[:].unsqueeze(3).broadcast_to([P, TT, N_GROUPS, PER_GROUP]), ALU.mult)
                    link(nc.vector.tensor_reduce(within[:], pick[:].rearrange("p t g e -> p t e g"), AX_X, ALU.add))
                    first_best(within[:], PER_GROUP, top[:, M1, :], hot1[:])
                    link(nc.vector.scalar_tensor_tensor(tmp[:], hot1[:], MASKED, within[:], ALU.mult, ALU.add))
                    first_best(tmp[:], PER_GROUP, top[:, M2, :], hot2[:])
                    nc.vector.tensor_tensor(top[:, E2, :], top[:, M2, :], top[:, M1, :],
                                            ALU.subtract).then_inc(gap, 1)
                    dve.wait_ge(exps, 1)
                    link(nc.vector.tensor_reduce(top[:, GSUM, :], gexp[:], AX_X, ALU.add))
                    link(nc.vector.reciprocal(top[:, GP, :], top[:, GSUM, :]))
                    dve.wait_ge(exps, 2)
                    link(nc.vector.tensor_scalar(top[:, W2, :], top[:, E2, :], 1.0, None, ALU.add))
                    link(nc.vector.reciprocal(top[:, W1, :], top[:, W2, :]))
                    tt(top[:, W1, :], top[:, W1, :], top[:, GP, :], ALU.mult)
                    tt(top[:, W2, :], top[:, W1, :], top[:, E2, :], ALU.mult)
                    tt(hot1[:], hot1[:], over(top[:, W1, :], PER_GROUP), ALU.mult)
                    tt(hot2[:], hot2[:], over(top[:, W2, :], PER_GROUP), ALU.mult)
                    tt(hot1[:], hot1[:], hot2[:], ALU.add)
                    for t in range(TT):
                        a = hot1[:, t, :].unsqueeze(1).broadcast_to([P, N_GROUPS, PER_GROUP])
                        b = ghot[:, t, :].unsqueeze(2).broadcast_to([P, N_GROUPS, PER_GROUP])
                        ins = nc.vector.tensor_tensor(pick[:, t], a, b, ALU.mult)
                    ins.then_inc(weights, 1)
                    dve.wait_ge(turned, 1)
                    nc.vector.tensor_copy(wT[:], pT[0:N_EXPERTS, 0:SEQ]).then_inc(turned_out, 1)


def latent_heads(nc, con, ckvT, w_uk, w_uv, k_nope, v):
    with ExitStack() as ctx:
        sb = lambda n, s, d=F32: ctx.enter_context(nc.sbuf_tensor(f"lh_{n}", s, d))
        uk = sb("uk", [P, 4, P])
        ukT = sb("ukT", [P, 512])
        uv = sb("uv", [P, 8, 64])
        pT = ctx.enter_context(nc.psum_tensor("lh_pT", [P, 512], F32))
        pK = ctx.enter_context(nc.psum_tensor("lh_pK", [P, TT, 512], F32))
        pV = ctx.enter_context(nc.psum_tensor("lh_pV", [P, TT, 512], F32))
        with Stage(nc, "lh", ["uk_in", "uv_in", "turned", "turned_out", "k_done", "v_done", "out"]) as sems:
            uk_in, uv_in, turned, turned_out, k_done, v_done, out = sems
            with nc.Block(no_gpsimd_drain=True) as block:
                @block.sync
                def _(sp):
                    sp.dma_start(uk[:], w_uk.rearrange("h d c -> (h d) c").rearrange("(a p) c -> p a c", p=P))\
                        .then_inc(uk_in, 16)
                    sp.dma_start(uv[:], w_uv.rearrange("h c d -> c h d")).then_inc(uv_in, 16)

                @block.tensor
                def _(pe):
                    pe.wait_ge(uk_in, 16)
                    for n in range(4):
                        ins = nc.tensor.transpose(pT[:, n * P:(n + 1) * P], uk[:, n, :], con["identity"])
                    ins.then_inc(turned, 1)
                    pe.wait_ge(uv_in, 16)
                    for t in range(TT):
                        ins = nc.tensor.matmul(pV[:, t, :], ckvT[:, 0, t * P:(t + 1) * P],
                                               uv[:].rearrange("p h d -> p (h d)"), start=True, stop=True)
                    ins.then_inc(v_done, 1)
                    pe.wait_ge(turned_out, 1)
                    for t in range(TT):
                        ins = nc.tensor.matmul(pK[:, t, :], ckvT[:, 0, t * P:(t + 1) * P], ukT[:],
                                               start=True, stop=True)
                    ins.then_inc(k_done, 1)

                @block.vector
                def _(dve):
                    dve.wait_ge(turned, 1)
                    nc.vector.tensor_copy(ukT[:], pT[:]).then_inc(turned_out, 1)
                    dve.wait_ge(k_done, 1)
                    nc.vector.tensor_copy(k_nope, pK[:]).then_inc(out, 1)

                @block.scalar
                def _(act):
                    act.wait_ge(v_done, 1)
                    nc.scalar.activation(v, pV[:], ACT.Copy).then_inc(out, 1)


def even_prepare(nc, con, y, k_nope, q_a, k_a, iw):
    with ExitStack() as ctx:
        sb = lambda n, s, d=F32: ctx.enter_context(nc.sbuf_tensor(f"ep_{n}", s, d))
        tmp = sb("tmp", [P, 4, TT * 8 * 32])
        tmpg = sb("tmpg", [P, 4, TT * 8 * 32])
        r32 = con["rope32"].rearrange("p (t d) -> p t d", t=TT)
        r64 = con["rope64"].rearrange("p (t d) -> p t d", t=TT)
        part = lambda at, n, d: heads_of(y[:, :, at:at + n * d], n)
        with Stage(nc, "ep", ["k_rotated", "vlink", "glink", "alink"]) as sems:
            k_rotated, vlink, glink, alink = sems
            with nc.Block(no_gpsimd_drain=True) as block:
                @block.vector
                def _(dve):
                    link = Link(dve, vlink)
                    rope(link, nc.vector, part(896, 1, 32), r32, tmp)
                    nc.vector.tensor_scalar(iw, y[:, :, 1504:1512], 8 ** -0.5, None, ALU.mult)\
                        .then_inc(k_rotated, 1)
                    rope(link, nc.vector, part(512, 8, 32), r32, tmp)
                    for t in range(TT):
                        link(nc.vector.tensor_copy(q_a[:, t, :, 64:96], part(512, 8, 32)[:, t]))
                    rope(link, nc.vector, part(928, 8, 64), r64, tmp)
                    rope(link, nc.vector, part(1440, 1, 64), r64, tmp)

                @block.gpsimd
                def _(pool):
                    link = Link(pool, glink)
                    rope(link, nc.gpsimd, part(1512, 8, 64), r64, tmpg)
                    rope(link, nc.gpsimd, part(2024, 8, 64), r64, tmpg)

                @block.scalar
                def _(act):
                    link = Link(act, alink)
                    for t in range(TT):
                        link(nc.scalar.activation(q_a[:, t, :, 0:64], part(0, 8, 64)[:, t], ACT.Copy))
                        link(nc.scalar.activation(k_a[:, t, :, 0:64], heads_of(k_nope, 8)[:, t], ACT.Copy))
                    act.wait_ge(k_rotated, 1)
                    for t in range(TT):
                        link(nc.scalar.activation(k_a[:, t, :, 64:96],
                                                  y[:, t, 896:928].unsqueeze(1).broadcast_to([P, 8, 32]), ACT.Copy))


def choose_keys(nc, con, iq, ik, iw, mask):
    with ExitStack() as ctx:
        sb = lambda n, s, d=F32: ctx.enter_context(nc.sbuf_tensor(f"ck_{n}", s, d))
        kT = sb("kT", [64, SEQ])
        qT = sb("qT", [64, 3, SEQ])
        rel = sb("rel", [P, 2, NCOL])
        score = sb("score", [P, NCOL])
        top = sb("top", [P, TT, 8])
        pT = ctx.enter_context(nc.psum_tensor("ck_pT", [P, 4, 512], F32))
        pS = ctx.enter_context(nc.psum_tensor("ck_pS", [P, 4, 512], F32))
        with Stage(nc, "ck", ["k_turned", "k_out", "q_turned", "q_out", "scored", "related", "weighted",
                              "vlink"]) as sems:
            k_turned, k_out, q_turned, q_out, scored, related, weighted, vlink = sems
            with nc.Block(no_gpsimd_drain=True) as block:
                @block.tensor
                def _(pe):
                    for t in range(TT):
                        ins = nc.tensor.transpose(pT[0:64, 3, t * P:(t + 1) * P], ik[:, t, :], con["identity"])
                    ins.then_inc(k_turned, 1)

                    def turn(h):
                        if h >= 3:
                            pe.wait_ge(q_out, h - 2)
                        for t in range(TT):
                            ins = nc.tensor.transpose(pT[0:64, h % 3, t * P:(t + 1) * P], iq[:, t, h, :],
                                                      con["identity"])
                        ins.then_inc(q_turned, 1)

                    def score_of(h):
                        pe.wait_ge(q_out, h + 1)
                        if h >= 4:
                            pe.wait_ge(related, h - 3)
                        for t, c0, nk in SPAN:
                            ins = nc.tensor.matmul(pS[:, h % 4, c0:c0 + nk], qT[:, h % 3, t * P:(t + 1) * P],
                                                   kT[:, 0:nk], start=True, stop=True)
                        ins.then_inc(scored, 1)

                    turn(0)
                    pe.wait_ge(k_out, 1)
                    for h in range(1, 8):
                        turn(h)
                        score_of(h - 1)
                    score_of(7)

                @block.scalar
                def _(act):
                    for h in range(9):
                        if h < 8:
                            act.wait_ge(q_turned, h + 1)
                            if h >= 3:
                                act.wait_ge(scored, h - 2)
                            nc.scalar.activation(qT[:, h % 3, :], pT[0:64, h % 3, 0:SEQ], ACT.Copy).then_inc(q_out, 1)
                        if h:
                            act.wait_ge(scored, h)
                            if h >= 3:
                                act.wait_ge(weighted, h - 2)
                            nc.scalar.activation(rel[:, (h - 1) % 2, :], pS[:, (h - 1) % 4, 0:NCOL], ACT.Relu,
                                                 scale=64 ** -0.5).then_inc(related, 1)

                @block.vector
                def _(dve):
                    link = Link(dve, vlink)
                    dve.wait_ge(k_turned, 1)
                    nc.vector.tensor_copy(kT[:], pT[0:64, 3, 0:SEQ]).then_inc(k_out, 1)
                    for h in range(8):
                        dve.wait_ge(related, h + 1)
                        if h:
                            dve.wait_ge(weighted, h)
                        for t, c0, nk in SPAN:
                            s = score[:, c0:c0 + nk]
                            r = rel[:, h % 2, c0:c0 + nk]
                            if h == 0:
                                ins = nc.vector.tensor_scalar(s, r, iw[:, t, h:h + 1], None, ALU.mult)
                            else:
                                ins = nc.vector.scalar_tensor_tensor(s, r, iw[:, t, h:h + 1], s, ALU.mult, ALU.add)
                        ins.then_inc(weighted, 1)
                    dve.wait_ge(weighted, 8)
                    link(nc.vector.tensor_tensor(score[:], score[:], con["causal"], ALU.add))
                    for n in range(TOP_KEYS // 8):
                        for t, c0, nk in SPAN:
                            link(nc.vector.max(top[:, t, :], score[:, c0:c0 + nk]))
                            link(nc.vector.match_replace(score[:, c0:c0 + nk], top[:, t, :], score[:, c0:c0 + nk],
                                                         TAKEN))
                    link(nc.vector.tensor_scalar(mask, score[:], TAKEN, MASKED, ALU.not_equal, ALU.mult))
                    link(nc.vector.tensor_tensor(mask, mask, con["causal"], ALU.add))


LAM_INIT = 0.8 - 0.6


def differ(nc, con, o, lam, gain, out):
    with ExitStack() as ctx:
        sb = lambda n, s, d=F32: ctx.enter_context(nc.sbuf_tensor(f"df_{n}", s, d))
        l = sb("l", [P, 4, 64])
        prod = sb("prod", [P, 2, 64])
        s = sb("s", [P, 2])
        neg = sb("neg", [P, 1])
        row = sb("row", [P, P])
        sq = sb("sq", [P, TT, 4, P])
        st = sb("st", [P, 3, TT * 4])
        with Stage(nc, "df", ["lam_in", "row_in", "sums", "exps", "less", "squares", "recips", "roots", "vlink"]) as sems:
            lam_in, row_in, sums, exps, less, squares, recips, roots, vlink = sems
            with nc.Block(no_gpsimd_drain=True) as block:
                @block.sync
                def _(sp):
                    sp.dma_start(l[:].rearrange("p a d -> p (a d)"), spread(lam.rearrange("a d -> (a d)")))\
                        .then_inc(lam_in, 16)
                    sp.dma_start(row[:], spread(gain)).then_inc(row_in, 16)

                @block.scalar
                def _(act):
                    act.wait_ge(sums, 1)
                    nc.scalar.activation(s[:], s[:], ACT.Exp).then_inc(exps, 1)
                    act.wait_ge(less, 1)
                    nc.scalar.activation(sq[:], heads_of(out, 4), ACT.Square).then_inc(squares, 1)
                    act.wait_ge(recips, 1)
                    nc.scalar.activation(st[:, 2, :], st[:, 1, :], ACT.Sqrt).then_inc(roots, 1)

                @block.vector
                def _(dve):
                    link = Link(dve, vlink)
                    v = nc.vector
                    dve.wait_ge(lam_in, 16)
                    link(v.tensor_tensor(prod[:], l[:, 0::2, :], l[:, 1::2, :], ALU.mult))
                    v.tensor_reduce(s[:], prod[:], AX_X, ALU.add).then_inc(sums, 1)
                    dve.wait_ge(exps, 1)
                    link(v.tensor_tensor(neg[:], s[:, 1:2], s[:, 0:1], ALU.subtract))
                    link(v.tensor_scalar(neg[:], neg[:], -LAM_INIT, None, ALU.add))
                    for t in range(TT):
                        pair = o[:, t, :].rearrange("p (h m d) -> p h m d", h=4, m=2)
                        ins = v.scalar_tensor_tensor(out[:, t, :].rearrange("p (h d) -> p h d", h=4),
                                                     pair[:, :, 1, :], neg[:], pair[:, :, 0, :], ALU.mult, ALU.add)
                    ins.then_inc(less, 1)
                    dve.wait_ge(squares, 1)
                    link(v.tensor_reduce(st[:, 0, :], sq[:].rearrange("p t h d -> p (t h) d"), AX_X, ALU.add))
                    link(v.tensor_scalar(st[:, 0, :], st[:, 0, :], 1.0 / P, EPS, ALU.mult, ALU.add))
                    v.reciprocal(st[:, 1, :], st[:, 0, :]).then_inc(recips, 1)
                    dve.wait_ge(roots, 1)
                    link(v.tensor_scalar(st[:, 2, :], st[:, 2, :], 1.0 - LAM_INIT, None, ALU.mult))
                    dve.wait_ge(row_in, 16)
                    for t in range(TT):
                        each = out[:, t, :].rearrange("p (h d) -> p h d", h=4)
                        by = st[:, 2, t * 4:(t + 1) * 4].unsqueeze(2).broadcast_to([P, 4, P])
                        link(v.tensor_tensor(each, each, by, ALU.mult))
                        link(v.tensor_tensor(each, each, row[:].unsqueeze(1).broadcast_to([P, 4, P]), ALU.mult))


def odd_prepare(nc, con, y, pe_emb, w1, w2, cmp_kv, gates):
    with ExitStack() as ctx:
        sb = lambda n, s, d=F32: ctx.enter_context(nc.sbuf_tensor(f"op_{n}", s, d))
        tmp = sb("tmp", [P, 4, TT * C_H * 32])
        tmpg = sb("tmpg", [P, 4, TT * C_G * 32])
        xT = sb("xT", [C_DIM, 2, C_G, SEQ])
        w1s = sb("w1s", [C_DIM, 2, CMP_LEN, P])
        w2s = sb("w2s", [P, 2, C_DIM])
        emb = sb("emb", [CMP_LEN, 2, C_DIM])
        embT = sb("embT", [C_DIM, 2, CMP_LEN])
        bias = sb("bias", [P, 2])
        hid = sb("hid", [P, 2, C_G, N_CMP])
        pT = ctx.enter_context(nc.psum_tensor("op_pT", [P, 4, 512], F32))
        pH = ctx.enter_context(nc.psum_tensor("op_pH", [P, 512], F32))
        pB = ctx.enter_context(nc.psum_tensor("op_pB", [P, 512], F32))
        pO = ctx.enter_context(nc.psum_tensor("op_pO", [P, 512], F32))
        r64 = con["rope64"].rearrange("p (t d) -> p t d", t=TT)
        part = lambda at, n: heads_of(y[:, :, at:at + n * 64], n)
        with Stage(nc, "op", ["emb_in", "w1_in", "w2_in", "rotated", "turned", "emb_turned", "x_out", "e_out",
                              "products", "biases", "bias_out", "gelus", "seconds", "done", "vlink", "glink",
                              "alink"]) as sems:
            (emb_in, w1_in, w2_in, rotated, turned, emb_turned, x_out, e_out, products, biases, bias_out, gelus,
             seconds, done, vlink, glink, alink) = sems
            with nc.Block(no_gpsimd_drain=True) as block:
                @block.sync
                def _(sp):
                    sp.dma_start(emb[:], pe_emb.rearrange("a l d -> l a d")).then_inc(emb_in, 16)
                    for a in range(2):
                        sp.dma_start(w1s[:, a, :, :], w1[a].rearrange("(l d) e -> d l e", d=C_DIM)).then_inc(w1_in, 16)
                    sp.dma_start(w2s[:], w2.rearrange("a e d -> e a d")).then_inc(w2_in, 16)

                @block.gpsimd
                def _(pool):
                    link = Link(pool, glink)
                    rope(link, nc.gpsimd, part(1536, C_G), r64, tmpg)
                    rope(link, nc.gpsimd, part(2048, C_G), r64, tmpg)

                @block.vector
                def _(dve):
                    link = Link(dve, vlink)
                    rope(link, nc.vector, part(1024, C_G), r64, tmp)
                    nc.vector.memset(bias[:], 0.0).then_inc(rotated, 1)
                    dve.wait_ge(turned, 1)
                    for a in range(2):
                        nc.vector.tensor_copy(xT[:, a, :, :], pT[0:C_DIM, 2 * a:2 * a + 2, :]
                                              .rearrange("p b (g n) -> p (b g) n", g=2)).then_inc(x_out, 1)
                    dve.wait_ge(emb_turned, 1)
                    nc.vector.tensor_copy(embT[:], pO[0:C_DIM, 0:2 * CMP_LEN]
                                          .rearrange("p (a l) -> p a l", a=2)).then_inc(e_out, 1)
                    rope(link, nc.vector, part(0, C_H), r64, tmp)
                    dve.wait_ge(biases, 1)
                    nc.vector.tensor_copy(bias[:], pB[:, 0:2]).then_inc(bias_out, 1)
                    dve.wait_ge(seconds, 1)
                    nc.vector.tensor_copy(cmp_kv, pO[0:N_CMP, :].rearrange("p (a n) -> p a n", a=2)).then_inc(done, 1)

                @block.scalar
                def _(act):
                    nc.scalar.activation(gates, y[:, :, 2560:2608], ACT.Sigmoid).then_inc(alink, 1)
                    act.wait_ge(products, 1)
                    act.wait_ge(bias_out, 1)
                    for a in range(2):
                        nc.scalar.activation(hid[:, a].rearrange("p g n -> p (g n)"),
                                             pH[:, a * 64:a * 64 + C_G * N_CMP], ACT.Gelu_apprx_tanh,
                                             bias=bias[:, a:a + 1]).then_inc(gelus, 1)

                @block.tensor
                def _(pe):
                    ident = con["identity"]
                    pe.wait_ge(emb_in, 16)
                    for a in range(2):
                        ins = nc.tensor.transpose(pO[0:C_DIM, a * CMP_LEN:(a + 1) * CMP_LEN], emb[:, a, :],
                                                  ident[0:CMP_LEN, 0:CMP_LEN])
                    ins.then_inc(emb_turned, 1)
                    pe.wait_ge(rotated, 1)
                    for a in range(2):
                        for g in range(C_G):
                            for t in range(TT):
                                at = 1024 + a * 256 + g * C_DIM
                                ins = nc.tensor.transpose(pT[0:C_DIM, 2 * a + g // 2,
                                                             (g % 2) * SEQ + t * P:(g % 2) * SEQ + (t + 1) * P],
                                                          y[:, t, at:at + C_DIM], ident)
                    ins.then_inc(turned, 1)
                    pe.wait_ge(w1_in, 32)
                    pe.wait_ge(x_out, 2)
                    pe.wait_ge(e_out, 1)
                    for a in range(2):
                        for l in range(CMP_LEN):
                            w = w1s[:, a, l, :]
                            last = l + CMP_STRIDE * (N_CMP - 1) + 1
                            ins = nc.tensor.matmul(pH[:, a * 64:a * 64 + C_G * N_CMP], w,
                                                   xT[:, a, :, l:last:CMP_STRIDE],
                                                   start=(l == 0), stop=(l == CMP_LEN - 1))
                    ins.then_inc(products, 1)
                    for a in range(2):
                        for l in range(CMP_LEN):
                            ins = nc.tensor.matmul(pB[:, a:a + 1], w1s[:, a, l, :], embT[:, a, l:l + 1],
                                                   start=(l == 0), stop=(l == CMP_LEN - 1))
                    ins.then_inc(biases, 1)
                    pe.wait_ge(w2_in, 16)
                    for a in range(2):
                        pe.wait_ge(gelus, a + 1)
                        for g in range(C_G):
                            at = a * 256 + g * C_DIM
                            ins = nc.tensor.matmul(pO[0:N_CMP, at:at + C_DIM], hid[:, a, g, :], w2s[:, a, :],
                                                   start=True, stop=True)
                    ins.then_inc(seconds, 1)


def blend(nc, parts, gates, out):
    with ExitStack() as ctx:
        tmp = ctx.enter_context(nc.sbuf_tensor("bl_tmp", [P, 2, D], F32))
        with Stage(nc, "bl", ["vlink", "second_ready", "third_ready"]) as (vlink, second_ready, third_ready):
            def gated(eng, into, j, t):
                each = parts[j][:, t, :].rearrange("p (h d) -> p h d", h=C_H)
                by = gates[:, t, j:3 * C_H:3].unsqueeze(2).broadcast_to([P, C_H, C_DIM])
                return eng.tensor_tensor(into.rearrange("p (h d) -> p h d", h=C_H), each, by, ALU.mult)

            with nc.Block(no_gpsimd_drain=True) as block:
                @block.gpsimd
                def _(pool):
                    for t in range(TT):
                        gated(nc.gpsimd, tmp[:, t, :], 2, t).then_inc(third_ready, 1)

                @block.vector
                def _(dve):
                    link = Link(dve, vlink)
                    for t in range(TT):
                        link(gated(nc.vector, out[:, t, :], 0, t))
                        link(gated(nc.vector, parts[1][:, t, :], 1, t))
                        link(nc.vector.tensor_tensor(out[:, t, :], out[:, t, :], parts[1][:, t, :], ALU.add))
                    for t in range(TT):
                        dve.wait_ge(third_ready, t + 1)
                        link(nc.vector.tensor_tensor(out[:, t, :], out[:, t, :], tmp[:, t, :], ALU.add))


def hybrid_kernel(nc, a, out):
    w = {n: v[0] for n, v in a.items() if n in LAYER_INPUTS}
    w["rw_r_k"] = w["rw_r_k"].rearrange("h n -> (h n)")
    flat2 = lambda x: x.rearrange("c h d -> c (h d)")
    tokens = lambda x: x.rearrange("(t p) n -> p t n", p=P)
    scratch = nc.dram_tensor("expert_weights", [N_EXPERTS, SEQ], F32, kind="Internal").ap()
    with ExitStack() as ctx:
        sb = lambda n, s, d=F32: ctx.enter_context(nc.sbuf_tensor(n, s, d))
        x = sb("x", [P, TT, D])
        mix = sb("mix", [P, TT, D])
        con_t = {n: sb("con_" + n, list(a[n].shape)) for n in CONSTANTS if n not in ("level_masks", "decay_sums")}
        con = {n: t[:] for n, t in con_t.items()}
        with Stage(nc, "load", ["loaded"]) as (loaded,):
            with nc.Block(no_gpsimd_drain=True) as block:
                @block.sync
                def _(sp):
                    sp.dma_start(x[:], tokens(a["x"][0])).then_inc(loaded, 16)
                    for n, t in con_t.items():
                        sp.dma_start(t[:], a[n]).then_inc(loaded, 16)
                    sp.wait_ge(loaded, 16 * (len(con_t) + 1))

        by_slot = lambda width: (lambda i, s: i * (ATTN_SLOTS * width) + s * width)

        with ExitStack() as inner:
            sbi = lambda n, s: inner.enter_context(nc.sbuf_tensor(n, s, F32))
            feat = sbi("feat", [P, TT, IN_W])
            project(nc, "in1", con, x, D, w["g_mix"], [(w["w_in"], IN_W, 368, feat)], split=True)
            with ExitStack() as att:
                sba = lambda n, s: att.enter_context(nc.sbuf_tensor(n, s, F32))
                qk = sba("qk", [P, 2, TT, MLA_H, MLA_QK])
                v = sba("v", [P, TT, MLA_H * MLA_V])
                k_nope = sba("k_nope", [P, TT, MLA_H * MLA_NOPE])
                q_flat = qk[:, 0].rearrange("p t h d -> p t (h d)")
                k_flat = qk[:, 1].rearrange("p t h d -> p t (h d)")
                project(nc, "uq", con, feat[:, :, 0:Q_RANK], Q_RANK, w["g_cq"],
                        [(flat2(w["w_uq"]), MLA_H * MLA_QK, 384, q_flat)])
                project(nc, "ukv", con, feat[:, :, Q_RANK:Q_RANK + KV_RANK], KV_RANK, w["g_ckv"],
                        [(flat2(w["w_uk"]), 512, 512, k_nope), (flat2(w["w_uv"]), 512, 512, v)])
                mla_prepare(nc, con, feat, qk[:], k_nope, a["positions"], w["g_qn"], w["g_kn"])
                attention(nc, "mla_at", con, MLA_H, q_flat, k_flat, v, MLA_QK, MLA_V, by_slot(MLA_QK),
                          by_slot(MLA_QK), by_slot(MLA_V), MLA_QK ** -0.5, con["causal"], mix[:, :, 0:512])
            rms_scale(nc, "mla_out", mix[:, :, 0:512], 512, w["g_mla_out"])
            with ExitStack() as rec:
                more = {n: rec.enter_context(nc.sbuf_tensor("con_" + n, list(a[n].shape), F32))
                        for n in ("level_masks", "decay_sums")}
                with Stage(nc, "load_rw", ["loaded"]) as (loaded,):
                    with nc.Block(no_gpsimd_drain=True) as block:
                        @block.sync
                        def _(sp):
                            for n, t in more.items():
                                sp.dma_start(t[:], a[n]).then_inc(loaded, 16)
                            sp.wait_ge(loaded, 16 * len(more))
                rwkv(nc, con | {n: t[:] for n, t in more.items()}, feat[:, :, MLA_IN:IN_W], w, mix[:, :, 512:D])
        project(nc, "out1", con, mix, D, None, [(w["w_o"], D, 512, ("add", x))], normed=False, split=True)
        with ExitStack() as inner:
            sbi = lambda n, s, d=F32: inner.enter_context(nc.sbuf_tensor(n, s, d))
            hT = (sbi("hT_hi", [P, KC, SEQ], F16), sbi("hT_lo", [P, KC, SEQ], F16))
            logits = sbi("logits", [P, TT, N_GROUPS + N_EXPERTS])
            project(nc, "rt_in", con, x, D, w["g_ffn"],
                    [(w["w_group"], N_GROUPS, N_GROUPS, logits[:, :, 0:N_GROUPS]),
                     (w["w_expert"], N_EXPERTS, N_EXPERTS, logits[:, :, N_GROUPS:])], keep_T=hT, split=True)
            route(nc, con, logits[:], (w["b_group"], w["b_expert"]), scratch)
            rows = lambda m: (lambda e: m[e].rearrange("(p c) n -> p c n", p=P))
            swiglu(nc, "moe", con, hT, N_EXPERTS, rows(w["w_gate"]), rows(w["w_up"]), rows(w["w_down"]),
                   lambda e: scratch[e].rearrange("(a n) -> a n", a=1).broadcast_to([P, SEQ]), x)

        def ffn(name, layer):
            with ExitStack() as inner:
                hT = tuple(inner.enter_context(nc.sbuf_tensor(f"{name}_hT_{n}", [P, KC, SEQ], F16))
                           for n in ("hi", "lo"))
                project(nc, name + "_in", con, x, D, a["norm_ffn_2"][layer], [], keep_T=hT, split=True)
                up = lambda m: (lambda e: m[layer].rearrange("(p c) n -> p c n", p=P)[:, :, bass.ds(e * D_EXPERT, D_EXPERT)])
                down = lambda m: (lambda e: m[layer].rearrange("(e p c) n -> e p c n", p=P, c=2)[e])
                swiglu(nc, name, con, hT, D_FF // D_EXPERT, up(a["ffn_w_gate_2"]), up(a["ffn_w_up_2"]),
                       down(a["ffn_w_down_2"]), None, x)

        with ExitStack() as inner:
            sbi = lambda n, s: inner.enter_context(nc.sbuf_tensor(n, s, F32))
            y = sbi("y_even", [P, TT, EVEN_IN])
            project(nc, "in2", con, x, D, a["norm_mix_2"][0], [(w["ev_w_in_2"], EVEN_IN, 508, y)], split=True)
            with ExitStack() as att:
                sba = lambda n, s: att.enter_context(nc.sbuf_tensor(n, s, F32))
                ckvT = sba("ckvT", [P, 1, SEQ])
                k_nope = sba("k_nope2", [P, TT, 512])
                v = sba("v2", [P, TT, 512])
                q_a = sba("q_a", [P, TT, 8, 96])
                k_a = sba("k_a", [P, TT, 8, 96])
                iw = sba("iw", [P, TT, 8])
                mask = sba("mask", [P, NCOL])
                project(nc, "ckv2", con, y[:, :, 768:896], KV_RANK, w["ev_kv_gain_2"], [], keep_T=ckvT)
                latent_heads(nc, con, ckvT, w["ev_w_uk_2"], w["ev_w_uv_2"], k_nope[:], v[:])
                even_prepare(nc, con, y, k_nope[:], q_a, k_a, iw[:])
                choose_keys(nc, con, heads_of(y[:, :, 928:1440], 8), y[:, :, 1440:1504], iw, mask[:])
                attention(nc, "dsa", con, 8, q_a[:].rearrange("p t h d -> p t (h d)"),
                          k_a[:].rearrange("p t h d -> p t (h d)"), v, 96, 64, by_slot(96), by_slot(96), by_slot(64),
                          96 ** -0.5, mask[:], mix[:, :, 0:512])
            with ExitStack() as att:
                o = att.enter_context(nc.sbuf_tensor("o_diff", [P, TT, D], F32))
                attention(nc, "diff", con, 8, y[:, :, 1512:2024], y[:, :, 2024:2536], y[:, :, 2536:3048], 64, 128,
                          by_slot(64), by_slot(64), lambda i, s: i * 256 + (s // 2) * 128, 64 ** -0.5,
                          con["causal"], o)
                differ(nc, con, o, w["ev_lambda_2"], w["ev_subln_2"], mix[:, :, 512:D])
        project(nc, "out2", con, mix, D, None, [(w["ev_w_out_2"], D, 512, ("add", x))], normed=False, split=True)
        ffn("ffn2", 0)

        with ExitStack() as inner:
            sbi = lambda n, s: inner.enter_context(nc.sbuf_tensor(n, s, F32))
            y = sbi("y_odd", [P, TT, ODD_IN])
            cmp_kv = sbi("cmp_kv", [N_CMP, 2, C_G * C_DIM])
            gates = sbi("gates", [P, TT, 3 * C_H])
            parts = [sbi(f"branch{n}", [P, TT, D]) for n in range(3)]
            project(nc, "in3", con, x, D, a["norm_mix_2"][1], [(w["od_w_in_2"], ODD_IN, 326, y)], split=True)
            odd_prepare(nc, con, y, w["od_cmp_pe_2"], w["od_cmp_w1_2"], w["od_cmp_w2_2"], cmp_kv[:], gates[:])
            q = y[:, :, 0:D]
            shared = lambda i, s: i * C_DIM
            attention(nc, "cmp", con, C_H, q, cmp_kv[:, 0, :], cmp_kv[:, 1, :], C_DIM, C_DIM, by_slot(C_DIM),
                      shared, shared, C_DIM ** -0.5, con["cmp_mask"], parts[0],
                      spans=[(0, 0, N_CMP), (1, N_CMP, N_CMP)], blocks=[(0, 0, 0, N_CMP), (1, 0, N_CMP, N_CMP)],
                      key_tiles=1, key_rows=N_CMP, empty_rows=True)
            for n, name in ((1, "slc"), (2, "win")):
                at = 1536 + 512 * (n - 1)
                attention(nc, name, con, C_H, q, y[:, :, at:at + 256], y[:, :, at + 256:at + 512], C_DIM, C_DIM,
                          by_slot(C_DIM), shared, shared, C_DIM ** -0.5, con["causal"], parts[n])
            blend(nc, [p[:] for p in parts], gates, mix)
        project(nc, "out3", con, mix, D, None, [(w["od_w_out_2"], D, 512, ("add", x))], normed=False, split=True)
        ffn("ffn3", 1)
        rms_scale(nc, "final", x[:], D, a["norm_final_2"])
        with Stage(nc, "store", ["stored"]) as (stored,):
            with nc.Block(no_gpsimd_drain=True) as block:
                @block.sync
                def _(sp):
                    sp.dma_start(tokens(out[0]), x[:]).then_inc(stored, 16)
                    sp.wait_ge(stored, 16)


CONSTANTS = ("identity", "causal", "cmp_mask", "decay_sums", "decay_ends", "level_masks", "inv_freq", "rope32",
             "rope64", "rank8")
INPUTS = (
    "x positions g_mix w_in g_cq w_uq g_ckv w_uk w_uv g_qn g_kn g_mla_out rw_mu rw_w0 rw_w2 rw_a0 rw_a2 rw_g2 "
    "rw_k_k rw_k_a rw_r_k rw_lnx_g rw_lnx_b w_o g_ffn w_group b_group w_expert b_expert w_gate w_up w_down "
    "norm_mix_2 norm_ffn_2 norm_final_2 ev_w_in_2 ev_kv_gain_2 ev_w_uk_2 ev_w_uv_2 ev_lambda_2 ev_subln_2 "
    "ev_w_out_2 od_w_in_2 od_cmp_pe_2 od_cmp_w1_2 od_cmp_w2_2 od_w_out_2 ffn_w_gate_2 ffn_w_up_2 ffn_w_down_2"
).split()
LAYER_INPUTS = [n for n in INPUTS if n not in ("x", "positions", "norm_mix_2", "norm_ffn_2", "norm_final_2",
                                               "ffn_w_gate_2", "ffn_w_up_2", "ffn_w_down_2")]


def kernel(**inputs):
    import concourse.bacc as bacc
    from concourse.bass_utils import run_bass_kernel_spmd

    nc = bacc.Bacc("TRN2", target_bir_lowering=False, num_devices=1)
    arrays = {n: np.ascontiguousarray(inputs[n]) for n in INPUTS}
    arrays.update(shape_constants())
    feeds, aps = {}, {}
    for n, v in arrays.items():
        feeds[f"in_{n}"] = v
        aps[n] = nc.dram_tensor(f"in_{n}", v.shape, mybir.dt.from_np(v.dtype), kind="ExternalInput").ap()
    out = nc.dram_tensor("out", (1, SEQ, D), F32, kind="ExternalOutput").ap()
    hybrid_kernel(nc, aps, out)
    return run_bass_kernel_spmd(nc, [feeds], core_ids=[0]).results[0]["out"]
```

```python
from contextlib import ExitStack, nullcontext

import numpy as np

import concourse.bass as bass
from concourse import mybir

ALU = mybir.AluOpType
ACT = mybir.ActivationFunctionType
AX_X = mybir.AxisListType.X
F32 = mybir.dt.float32
BF16 = mybir.dt.bfloat16
F16 = mybir.dt.float16
I32 = mybir.dt.int32

P = 128
SEQ = 256
TT = SEQ // P
D = 1024
KC = D // P
EPS = 1e-6
MASKED = -1e30
LEAST_MAX = -1e20
TAKEN = -3e38

W_SCALE = 64.0

SPAN = [(0, 0, P), (1, P, SEQ)]
NCOL = P + SEQ
KEY_BLOCKS = [(0, 0, 0, P), (1, 0, P, P), (1, 1, 2 * P, P)]

MLA_H, MLA_NOPE, MLA_ROPE, MLA_V = 8, 64, 32, 64
MLA_QK = MLA_NOPE + MLA_ROPE
Q_RANK, KV_RANK = 256, 128
MLA_IN = Q_RANK + KV_RANK + MLA_ROPE
RW_H, RW_N = 8, 64
RW_W = RW_H * RW_N
RW_IN = 3 * RW_W + 64 + 64 + 128
IN_W = MLA_IN + RW_IN
N_GROUPS, PER_GROUP = 4, 8
N_EXPERTS = N_GROUPS * PER_GROUP
D_EXPERT = 256
CAP = 64
LNX_EPS = 64e-5
SOLVE_LEVELS = 7

EVEN_SPLITS = [512, 256, 128, 32, 512, 64, 8, 512, 512, 512]
EVEN_IN = sum(EVEN_SPLITS)
TOP_KEYS = 64
ODD_SPLITS = [1024] + [256] * 6 + [48]
ODD_IN = sum(ODD_SPLITS)
C_H, C_G, C_DIM = 16, 4, 64
CMP_LEN, CMP_STRIDE = 32, 16
N_CMP = SEQ // CMP_STRIDE - 1
D_FF = 2816


def shape_constants():
    t = np.arange(P)
    c = {}
    c["identity"] = np.eye(P, dtype=np.float32)
    keys = np.arange(SEQ)
    m0 = np.where(t[:, None] >= keys[None, :P], 0.0, MASKED)
    m1 = np.where(t[:, None] + P >= keys[None, :], 0.0, MASKED)
    c["causal"] = np.concatenate([m0, m1], axis=1).astype(np.float32)
    end = np.arange(N_CMP) * CMP_STRIDE + CMP_LEN - 1
    c["cmp_mask"] = np.concatenate(
        [np.where(end[None, :] <= t[:, None] + P * k, 0.0, MASKED) for k in range(TT)], axis=1).astype(np.float32)
    half = P // 2
    i, j = t[:, None], t[None, :]
    upto = (i <= j).astype(np.float32) - (i < half)
    before = (i < j).astype(np.float32) - (i < half)
    c["decay_sums"] = np.concatenate([upto, before], axis=1).astype(np.float32)
    c["decay_ends"] = np.stack([(t >= half), (t < half)], axis=1).astype(np.float32)
    lev = []
    for n in range(SOLVE_LEVELS):
        b = 1 << n
        same = (i // (2 * b)) == (j // (2 * b))
        lev.append((same & (i % (2 * b) < b) & (j % (2 * b) >= b)).astype(np.float32))
    c["level_masks"] = np.concatenate(lev + [lev[0].T, (i <= j).astype(np.float32), (i < j).astype(np.float32)],
                                      axis=1).astype(np.float32)
    inv16 = (1.0 / (np.float32(10000.0) ** (np.arange(16, dtype=np.float32) / np.float32(16)))).astype(np.float32)
    c["inv_freq"] = np.tile(inv16[None], (P, 1)).astype(np.float32)
    for d in (32, 64):
        inv = (np.float32(10000.0) ** (-np.arange(0, d, 2, dtype=np.float32) / np.float32(d))).astype(np.float32)
        ang = (np.arange(SEQ, dtype=np.float32)[:, None] * inv[None]).astype(np.float32)
        cs = np.concatenate([np.cos(ang.astype(np.float64)), np.sin(ang.astype(np.float64))], axis=1)
        c[f"rope{d}"] = cs.reshape(TT, P, d).transpose(1, 0, 2).reshape(P, TT * d).astype(np.float32)
    c["rank8"] = np.tile(np.arange(8, 0, -1, dtype=np.float32)[None], (P, 1)).astype(np.float32)
    c["counting"] = np.concatenate([(i < j), np.ones((P, P))], axis=1).astype(np.float32)
    c["slot_ids"] = np.concatenate([np.tile(np.arange(CAP)[None], (P, 1)), t[:, None] % CAP],
                                   axis=1).astype(np.float32)
    return {k: np.ascontiguousarray(v) for k, v in c.items()}


class Link:

    def __init__(self, eng, sem, base=0):
        self.eng, self.sem, self.base, self.n = eng, sem, base, 0

    def __call__(self, ins):
        self.n += 1
        ins.then_inc(self.sem, 1)
        self.eng.wait_ge(self.sem, self.base + self.n)


def wait_alone(eng, passed, sem, value):
    eng.wait_ge(sem, value)
    eng.sem_inc(passed, 1)


class Stage:

    def __init__(self, nc, name, names):
        self.nc, self.name, self.names = nc, name, names

    def __enter__(self):
        self.sems = [self.nc.alloc_semaphore(f"{self.name}_{n}") for n in self.names]
        return self.sems

    def __exit__(self, *exc):
        if exc[0] is None:
            self.nc.clear_and_free_semaphores(self.sems)
            self.nc.all_engine_barrier()


def cols(vector):
    return vector.rearrange("(p c) -> p c", p=P)


def spread(vector):
    return vector.rearrange("(a n) -> a n", a=1).broadcast_to([P, vector.shape[0]])


def first_tiles(wt, w, tile):
    wv = w.rearrange("(p c) n -> p c n", p=P)
    return [(wt[:, s, :, 0:tile], wv[:, :, s * tile:(s + 1) * tile]) for s in range(2)]


def project(nc, name, con, src, width, gain, jobs, normed=True, keep_T=None, split=False, prefetch=(), arrived=None,
            keep_normed=None, first=None):
    kc = width // P
    with ExitStack() as ctx:
        sb = lambda n, s, d=F32: ctx.enter_context(nc.sbuf_tensor(f"{name}_{n}", s, d))
        if split:
            sT_hi, sT_lo = keep_T if keep_T is not None else (sb("sT_hi", [P, kc, SEQ], F16),
                                                              sb("sT_lo", [P, kc, SEQ], F16))
        else:
            sT = keep_T if keep_T is not None else sb("sT", [P, kc, SEQ])
        big = max(j[2] for j in jobs) if jobs else 1
        if keep_normed is not None:
            xn, gcol = keep_normed
        else:
            xn = sb("xn", [P, TT, width]) if normed else src
            gcol = sb("gcol", [P, kc])
        wt = sb("wt", [P, 2, kc, big]) if first is None else first[0]
        if split:
            w_hi = sb("w_hi", [P, 2, kc, big], F16)
            w_lo = sb("w_lo", [P, 2, kc, big], F16)
        back = 1.0 / W_SCALE if split else 1.0
        stats = sb("stats", [P, 3, TT])
        pT = ctx.enter_context(nc.psum_tensor(f"{name}_pT", [P, 4, 512], F32))
        pY = ctx.enter_context(nc.psum_tensor(f"{name}_pY", [P, 2, TT, 512], F32))
        with Stage(nc, name, ["gain_in", "w0_in", "w1_in", "squares", "recips", "rstd", "normed", "turned",
                              "evac_a", "evac_v", "product", "out_a", "out_v", "vlink", "hi_ready",
                              "lo_ready", "prefetched"]) as sems:
            (gain_in, w0_in, w1_in, squares, recips, rstd, normed_ready, turned, evac_a, evac_v,
             product, out_a, out_v, vlink, hi_ready, lo_ready, prefetched) = sems
            w_in = [w0_in, w1_in]
            order = [(job, job[1] // job[2]) for job in jobs]
            if split:
                assert len(jobs) < 2 or all(count == 1 for _, count in order)

            with nc.Block(no_gpsimd_drain=True) as block:
                def over_tiles(eng, do, skip=lambda put: False, ahead=None):
                    done = 0
                    total = sum(count for _, count in order)
                    for (w, n, tile, put), count in order:
                        if skip(put):
                            done += count
                            continue

                        def one(at, slot, turn, col, last):
                            if ahead is not None and not last:
                                ahead(w, tile, put, at + 1, 1 - slot, turn + slot)
                            do(w, tile, put, at, slot, turn, col)
                        if count >= 4:
                            assert done % 2 == 0 and count % 2 == 0
                            tail = ahead is not None
                            if ahead is not None:
                                ahead(w, tile, put, done, 0, done // 2)
                            with eng.Fori(0, count // 2 - tail) as i:
                                for s in range(2):
                                    one(i * 2 + (done + s), s, i + done // 2, (i * 2 + s) * tile, False)
                            if tail:
                                for k in (count - 2, count - 1):
                                    one(done + k, k % 2, (done + k) // 2, k * tile, k == count - 1)
                        else:
                            for k in range(count):
                                if ahead is not None:
                                    ahead(w, tile, put, done + k, (done + k) % 2, (done + k) // 2)
                                do(w, tile, put, done + k, (done + k) % 2, (done + k) // 2, k * tile)
                        done += count

                @block.sync
                def _(sp):
                    if normed:
                        sp.dma_start(gcol[:], cols(gain)).then_inc(gain_in, 16)

                    def load(w, tile, put, at, slot, turn, col):
                        sp.wait_ge(lo_ready if split else product, at + 1)
                        wv = w.rearrange("(p c) n -> p c n", p=P)
                        sp.dma_start(wt[:, slot, :, 0:tile], wv[:, :, bass.ds(col, tile)]).then_inc(w_in[slot], 16)
                    if first is None:
                        over_tiles(sp, load)
                    else:
                        (w, n, tile, put), = jobs
                        sp.wait_ge(first[1], 2 * 16)
                        for s in range(2):
                            sp.sem_inc(w_in[s], 16)
                        with sp.Fori(1, n // tile // 2) as i:
                            for s in range(2):
                                load(w, tile, put, i * 2 + s, s, i, (i * 2 + s) * tile)

                if prefetch:
                    @block.gpsimd
                    def _(pool):
                        if jobs:
                            pool.wait_ge(w1_in, 16)
                        for into, source in prefetch:
                            nc.gpsimd.dma_start(into, source).then_inc(arrived or prefetched, 16)
                        if arrived is None:
                            pool.wait_ge(prefetched, 16 * len(prefetch))

                @block.scalar
                def _(act):
                    if normed:
                        for t in range(TT):
                            nc.scalar.activation(xn[:, t, :], src[:, t, :], ACT.Square,
                                                 accum_out=stats[:, 0, t:t + 1]).then_inc(squares, 1)
                        act.wait_ge(recips, 1)
                        nc.scalar.activation(stats[:, 2, :], stats[:, 1, :], ACT.Sqrt).then_inc(rstd, 1)
                        act.wait_ge(gain_in, 16)
                    for c in range(kc) if split else range(1, kc, 2):
                        act.wait_ge(turned, c + 1)
                        into = sT_hi[:, c, :] if split else sT[:, c, :]
                        scale = gcol[:, c:c + 1] if normed else 1.0
                        nc.scalar.activation(into, pT[:, c % 4, 0:SEQ], ACT.Copy, scale=scale).then_inc(evac_a, 1)
                    act.sem_inc(out_a, 2)

                    def high_part(w, tile, put, at, slot, turn):
                        act.wait_ge(w_in[slot], turn * 16 + 16)
                        act.wait_ge(product, at + 1)
                        nc.scalar.activation(w_hi[:, slot, :, 0:tile], wt[:, slot, :, 0:tile], ACT.Copy,
                                             scale=W_SCALE).then_inc(hi_ready, 1)

                    def move(w, tile, put, at, slot, turn, col):
                        if isinstance(put, tuple):
                            return
                        act.wait_ge(product, at + 3)
                        nc.scalar.activation(put[:, 0, bass.ds(col, tile)], pY[:, slot, 0, 0:tile],
                                             ACT.Copy, scale=back).then_inc(out_a, 1)
                    over_tiles(act, move, skip=lambda put: not split and isinstance(put, tuple),
                               ahead=high_part if split else None)

                @block.vector
                def _(dve):
                    link = Link(dve, vlink)
                    if normed:
                        dve.wait_ge(squares, TT)
                        link(nc.vector.tensor_scalar(stats[:, 0, :], stats[:, 0, :], 1.0 / width, EPS,
                                                     ALU.mult, ALU.add))
                        nc.vector.reciprocal(stats[:, 1, :], stats[:, 0, :]).then_inc(recips, 1)
                        dve.wait_ge(rstd, 1)
                        for t in range(TT):
                            nc.vector.tensor_scalar(xn[:, t, :], src[:, t, :], stats[:, 2, t:t + 1], None,
                                                    ALU.mult).then_inc(normed_ready, 1)
                        dve.wait_ge(gain_in, 16)
                    for c in range(kc) if split else range(0, kc, 2):
                        if split:
                            dve.wait_ge(evac_a, c + 1)
                            scale = gcol[:, c:c + 1] if normed else 1.0
                            nc.vector.scalar_tensor_tensor(sT_lo[:, c, :], pT[:, c % 4, 0:SEQ], scale, sT_hi[:, c, :],
                                                           ALU.mult, ALU.subtract).then_inc(evac_v, 1)
                            continue
                        dve.wait_ge(turned, c + 1)
                        if normed:
                            nc.vector.tensor_scalar(sT[:, c, :], pT[:, c % 4, 0:SEQ], gcol[:, c:c + 1], None,
                                                    ALU.mult).then_inc(evac_v, 1)
                        else:
                            nc.vector.tensor_copy(sT[:, c, :], pT[:, c % 4, 0:SEQ]).then_inc(evac_v, 1)
                    dve.sem_inc(out_v, 2)
                    dve.sem_inc(lo_ready, 2)

                    def low_part(w, tile, put, at, slot, turn):
                        dve.wait_ge(hi_ready, at + 1)
                        nc.vector.scalar_tensor_tensor(w_lo[:, slot, :, 0:tile], wt[:, slot, :, 0:tile], W_SCALE,
                                                       w_hi[:, slot, :, 0:tile], ALU.mult,
                                                       ALU.subtract).then_inc(lo_ready, 1)

                    def move(w, tile, put, at, slot, turn, col):
                        dve.wait_ge(product, at + 3)
                        if isinstance(put, tuple):
                            for t in range(TT):
                                into = put[1][:, t, bass.ds(col, tile)]
                                ins = nc.vector.scalar_tensor_tensor(into, pY[:, slot, t, 0:tile], back, into,
                                                                     ALU.mult, ALU.add)
                            ins.then_inc(out_v, 1)
                        else:
                            nc.vector.tensor_scalar(put[:, 1, bass.ds(col, tile)], pY[:, slot, 1, 0:tile], back,
                                                    None, ALU.mult).then_inc(out_v, 1)
                    over_tiles(dve, move, ahead=low_part if split else None)

                @block.tensor
                def _(pe):
                    if normed:
                        pe.wait_ge(normed_ready, TT)
                    for c in range(kc):
                        if c >= 4:
                            if split:
                                pe.wait_ge(evac_v, c - 3)
                            else:
                                pe.wait_ge(evac_a if c % 2 else evac_v, (c - 4) // 2 + 1)
                        for t in range(TT):
                            ins = nc.tensor.transpose(pT[:, c % 4, t * P:(t + 1) * P],
                                                      xn[:, t, c::kc], con["identity"])
                        ins.then_inc(turned, 1)
                    pe.sem_inc(product, 2)
                    pe.wait_ge(evac_v, kc if split else (kc + 1) // 2)
                    if kc > 1 and not split:
                        pe.wait_ge(evac_a, kc // 2)

                    def multiply(w, tile, put, at, slot, turn, col):
                        if split:
                            pe.wait_ge(lo_ready, at + 3)
                            terms = [(sT_hi, w_hi), (sT_hi, w_lo), (sT_lo, w_hi)]
                        else:
                            pe.wait_ge(w_in[slot], turn * 16 + 16)
                            terms = [(sT, wt)]
                        if not isinstance(put, tuple):
                            pe.wait_ge(out_a, at + 1)
                        pe.wait_ge(out_v, at + 1)
                        steps = [(c, x, y) for c in range(kc) for x, y in terms]
                        for t in range(TT):
                            for n, (c, x, y) in enumerate(steps):
                                ins = nc.tensor.matmul(pY[:, slot, t, 0:tile], x[:, c, t * P:(t + 1) * P],
                                                       y[:, slot, c, 0:tile], start=(n == 0),
                                                       stop=(n == len(steps) - 1))
                        ins.then_inc(product, 1)
                    over_tiles(pe, multiply)



ATTN_SLOTS = 4


def attention(nc, name, con, heads, q, k, v, dqk, dv, q_col, k_col, v_col, scale, mask, out,
              spans=SPAN, blocks=KEY_BLOCKS, key_tiles=TT, key_rows=P, empty_rows=False,
              start=()):
    G = ATTN_SLOTS
    turns = heads // G
    ncol = spans[-1][1] + spans[-1][2]
    kw = key_rows if key_tiles == 1 else P
    with ExitStack() as ctx:
        sb = lambda n, s, d=F32: ctx.enter_context(nc.sbuf_tensor(f"{name}_{n}", s, d))
        q_head = sb("q_head", [P, G, TT, dqk])
        k_head = sb("k_head", [P, G, key_tiles, dqk])
        qkT = sb("qkT", [P, G, TT * P + key_tiles * P])
        S = sb("S", [P, G, ncol])
        E = sb("E", [P, G, ncol])
        ET = sb("ET", [P, G, len(blocks) * P])
        row_max = sb("row_max", [P, G, TT])
        bias = sb("bias", [P, G, TT])
        den = sb("den", [P, G, TT])
        rden = sb("rden", [P, G, TT])
        pT = ctx.enter_context(nc.psum_tensor(f"{name}_pT", [P, G, 512], F32))
        pS = ctx.enter_context(nc.psum_tensor(f"{name}_pS", [P, G, 512], F32))
        qw = TT * P
        with Stage(nc, name, ["q_staged", "k_staged", "heads_turned", "heads_out", "scored", "biased", "exped",
                              "probs_turned", "probs_out", "summed", "done", "vlink", "pool_passed",
                              "dve_passed", "pe_passed"]) as sems:
            (q_staged, k_staged, heads_turned, heads_out, scored, biased, exped, probs_turned, probs_out,
             summed, done, vlink, pool_passed, dve_passed, pe_passed) = sems
            with nc.Block(no_gpsimd_drain=True) as block:
                if start:
                    @block.sync
                    def _(sp):
                        for into, source, arrived in start:
                            sp.dma_start(into, source).then_inc(arrived, 16)

                @block.gpsimd
                def _(pool):
                    with pool.Fori(0, turns) as i:
                        for s in range(G):
                            wait_alone(pool, pool_passed, heads_turned, i * G + (s + 1))
                            src = k[0:kw, :, bass.ds(k_col(i, s), dqk)] if key_tiles > 1 else \
                                k[0:kw, bass.ds(k_col(i, s), dqk)]
                            dst = k_head[0:kw, s, :, :] if key_tiles > 1 else k_head[0:kw, s, 0, :]
                            nc.gpsimd.tensor_copy(dst, src).then_inc(k_staged, 1)

                @block.scalar
                def _(act):
                    with act.Fori(0, turns) as i:
                        for s in range(G):
                            act.wait_ge(heads_turned, i * G + (s + 1))
                            nc.scalar.activation(q_head[:, s, :, :], q[:, :, bass.ds(q_col(i, s), dqk)],
                                                 ACT.Copy).then_inc(q_staged, 1)
                        for s in range(G):
                            act.wait_ge(heads_turned, i * G + (s + 1 + G))
                            nc.scalar.activation(qkT[0:dqk, s, 0:qw + key_tiles * kw],
                                                 pT[0:dqk, s, 0:qw + key_tiles * kw],
                                                 ACT.Copy).then_inc(heads_out, 1)
                        for s in range(G):
                            act.wait_ge(biased, i * G + (s + 1))
                            for t, c0, nk in spans:
                                ins = nc.scalar.activation(E[:, s, c0:c0 + nk], S[:, s, c0:c0 + nk], ACT.Exp,
                                                           bias=bias[:, s, t:t + 1], scale=scale,
                                                           accum_out=den[:, s, t:t + 1])
                            ins.then_inc(exped, 1)

                @block.vector
                def _(dve):
                    dve.sem_inc(probs_out, G)
                    dve.sem_inc(done, G)
                    with dve.Fori(0, turns) as i:
                        link = Link(dve, vlink, i * (3 * G if empty_rows else 2 * G))
                        for s in range(G):
                            wait_alone(dve, dve_passed, scored, i * G + (s + 1))
                            for t, c0, nk in spans:
                                ins = nc.vector.tensor_tensor_reduce(
                                    S[:, s, c0:c0 + nk], pS[:, s, c0:c0 + nk], mask[:, c0:c0 + nk], 1.0, LEAST_MAX,
                                    ALU.add, ALU.max, row_max[:, s, t:t + 1])
                            link(ins)
                            nc.vector.tensor_scalar(bias[:, s, :], row_max[:, s, :], -scale, None,
                                                    ALU.mult).then_inc(biased, 1)
                        for s in range(G):
                            dve.wait_ge(probs_turned, i * G + (s + 1))
                            nc.vector.tensor_copy(ET[0:kw, s, :], pT[0:kw, s, 0:len(blocks) * P])\
                                .then_inc(probs_out, 1)
                            if empty_rows:
                                link(nc.vector.tensor_scalar(den[:, s, :], den[:, s, :], 1e-30, None, ALU.max))
                            link(nc.vector.reciprocal(rden[:, s, :], den[:, s, :]))
                        for s in range(G):
                            dve.wait_ge(summed, i * G + (s + 1))
                            for t in range(TT):
                                ins = nc.vector.tensor_scalar(
                                    out[:, t, bass.ds(i * (G * dv) + s * dv, dv)],
                                    pS[:, s, t * dv:(t + 1) * dv], rden[:, s, t:t + 1], None, ALU.mult)
                            ins.then_inc(done, 1)

                @block.tensor
                def _(pe):
                    pe.sem_inc(heads_turned, G)
                    ident = con["identity"]

                    def turn_heads(i, slots):
                        for s in slots:
                            pe.wait_ge(q_staged, i * G + (s + 1))
                            pe.wait_ge(k_staged, i * G + (s + 1))
                            wait_alone(pe, pe_passed, probs_out, i * G + (s + 1))
                            for t in range(TT):
                                nc.tensor.transpose(pT[0:dqk, s, t * P:(t + 1) * P], q_head[:, s, t, :], ident)
                            for t in range(key_tiles):
                                ins = nc.tensor.transpose(pT[0:dqk, s, qw + t * kw:qw + (t + 1) * kw],
                                                          k_head[0:kw, s, t, :], ident[0:kw, 0:kw])
                            ins.then_inc(heads_turned, 1)

                    def turn(i, next_too):
                        for s in range(G):
                            pe.wait_ge(heads_out, i * G + (s + 1))
                            pe.wait_ge(done, i * G + (s + 1))
                            for t, c0, nk in spans:
                                ins = nc.tensor.matmul(pS[:, s, c0:c0 + nk], qkT[0:dqk, s, t * P:(t + 1) * P],
                                                       qkT[0:dqk, s, qw:qw + nk], start=True, stop=True)
                            ins.then_inc(scored, 1)
                        for s in range(G):
                            wait_alone(pe, pe_passed, exped, i * G + (s + 1))
                            for n, (t, kb, c0, nk) in enumerate(blocks):
                                ins = nc.tensor.transpose(pT[0:nk, s, n * P:(n + 1) * P], E[:, s, c0:c0 + nk], ident)
                            ins.then_inc(probs_turned, 1)
                        for s in range(G):
                            wait_alone(pe, pe_passed, probs_out, i * G + (s + 1 + G))
                            for n, (t, kb, c0, nk) in enumerate(blocks):
                                vv = v[0:nk, kb, bass.ds(v_col(i, s), dv)] if key_tiles > 1 else \
                                    v[0:nk, bass.ds(v_col(i, s), dv)]
                                first = n == 0 or blocks[n - 1][0] != t
                                last = n == len(blocks) - 1 or blocks[n + 1][0] != t
                                ins = nc.tensor.matmul(pS[:, s, t * dv:(t + 1) * dv], ET[0:nk, s, n * P:(n + 1) * P],
                                                       vv, start=first, stop=last)
                            ins.then_inc(summed, 1)
                            if next_too:
                                turn_heads(i + 1, [s])

                    turn_heads(0, range(G))
                    with pe.Fori(0, turns - 1) as i:
                        turn(i, True)
                    turn(turns - 1, False)


def first_weights(weights, w_gate, w_up, w_down):
    w_up32, w_down32 = weights
    return [(w_up32[:, 0, 0, :, :], w_gate(0)), (w_up32[:, 0, 1, :, :], w_up(0)), (w_down32[:, 0, :, :], w_down(0))]


def only_if(eng, flag, value):
    if flag is None:
        return nullcontext()
    held = eng.value_load(flag, min_val=0, max_val=1)
    return eng.If(held < 1) if value == 0 else eng.If(held > 0)


def swiglu(nc, name, con, hT, n_blocks, w_gate, w_up, w_down, combine, x, weights, arrived, flag=None,
           start=()):
    NJ = D_EXPERT // P
    pairs = (n_blocks - 1) // 2
    hT_hi, hT_lo = hT
    with ExitStack() as ctx:
        sb = lambda n, s, d=F32: ctx.enter_context(nc.sbuf_tensor(f"{name}_{n}", s, d))
        w_up32, w_down32 = weights
        wu_hi = sb("wu_hi", [P, 2, 2, KC, D_EXPERT], F16)
        wu_lo = sb("wu_lo", [P, 2, 2, KC, D_EXPERT], F16)
        wd_hi = sb("wd_hi", [P, 2, NJ, D], F16)
        wd_lo = sb("wd_lo", [P, 2, NJ, D], F16)
        weight = sb("weight", [P, 2, SEQ])
        gated = sb("gated", [P, 2, NJ * SEQ])
        hidden = sb("hidden", [P, 2, NJ * SEQ])
        h_hi = sb("h_hi", [P, 2, NJ * SEQ], F16)
        h_lo = sb("h_lo", [P, 2, NJ * SEQ], F16)
        zeros = sb("zeros", [P, 512], BF16)
        pG = ctx.enter_context(nc.psum_tensor(f"{name}_pG", [P, 2, 512], F32))
        pU = ctx.enter_context(nc.psum_tensor(f"{name}_pU", [P, 2, 512], F32))
        pY = ctx.enter_context(nc.psum_tensor(f"{name}_pY", [P, TT, D], F32))
        with Stage(nc, name, ["up0_in", "up1_in", "down0_in", "down1_in", "weight0_in", "weight1_in", "zeroed",
                              "up_hi", "up_lo", "down_hi", "down_lo", "up_done", "silu_done", "hidden_ready",
                              "hidden_hi", "hidden_lo", "down_done", "summed", "vlink"]) as sems:
            (up0_in, up1_in, down0_in, down1_in, weight0_in, weight1_in, zeroed, up_hi, up_lo, down_hi, down_lo,
             up_done, silu_done, hidden_ready, hidden_hi, hidden_lo, down_done, summed, vlink) = sems
            up_in, down_in, weight_in = [up0_in, up1_in], [down0_in, down1_in], [weight0_in, weight1_in]

            def blocks_with_next(eng, split_up, rest):
                split_up(0, 0, 0)
                with eng.Fori(0, pairs) as i:
                    split_up(i * 2 + 1, 1, i)
                    rest(i * 2, 0, i)
                    split_up(i * 2 + 2, 0, i + 1)
                    rest(i * 2 + 1, 1, i)
                if n_blocks % 2 == 0:
                    split_up(n_blocks - 1, 1, pairs)
                    rest(n_blocks - 2, 0, pairs)
                rest(n_blocks - 1, (n_blocks - 1) % 2, pairs)

            with nc.Block(no_gpsimd_drain=True) as block:
                @block.sync
                def _(sp):
                    with only_if(sp, flag, 1):
                        def load(e, s, here=False):
                            sp.wait_ge(up_lo, e + 1)
                            if here:
                                sp.wait_ge(arrived, 3 * 16)
                                sp.sem_inc(up_in[s], 32)
                            else:
                                sp.dma_start(w_up32[:, s, 0, :, :], w_gate(e)).then_inc(up_in[s], 16)
                                sp.dma_start(w_up32[:, s, 1, :, :], w_up(e)).then_inc(up_in[s], 16)
                            if combine:
                                sp.wait_ge(hidden_ready, e + 1)
                                sp.dma_start(weight[:, s, :], combine(e)).then_inc(weight_in[s], 16)
                            sp.wait_ge(down_lo, e + 1)
                            if here:
                                sp.sem_inc(down_in[s], 16)
                            else:
                                sp.dma_start(w_down32[:, s, :, :], w_down(e)).then_inc(down_in[s], 16)
                        load(0, 0, here=True)
                        load(1, 1)
                        with sp.Fori(1, n_blocks // 2) as i:
                            for s in range(2):
                                load(i * 2 + s, s)
                        if n_blocks % 2:
                            load(n_blocks - 1, 0)
                        for into, source, when in start:
                            sp.dma_start(into, source).then_inc(when, 16)

                @block.scalar
                def _(act):
                    with only_if(act, flag, 1):
                        def split_up(e, s, turn):
                            act.wait_ge(up_in[s], turn * 32 + 32)
                            act.wait_ge(up_done, e + 1)
                            for m in range(2):
                                ins = nc.scalar.activation(wu_hi[:, s, m, :, :], w_up32[:, s, m, :, :], ACT.Copy,
                                                           scale=W_SCALE)
                            ins.then_inc(up_hi, 1)

                        def rest(e, s, turn):
                            act.wait_ge(up_done, e + 3)
                            act.wait_ge(hidden_ready, e + 1)
                            nc.scalar.activation(gated[:, s, :], pG[:, s, :], ACT.Silu,
                                                 scale=1.0 / W_SCALE).then_inc(silu_done, 1)
                            act.wait_ge(down_done, e + 1)
                            act.wait_ge(down_in[s], turn * 16 + 16)
                            nc.scalar.activation(wd_hi[:, s, :, :], w_down32[:, s, :, :], ACT.Copy,
                                                 scale=W_SCALE).then_inc(down_hi, 1)
                            act.wait_ge(hidden_ready, e + 3)
                            nc.scalar.activation(h_hi[:, s, :], hidden[:, s, :], ACT.Copy).then_inc(hidden_hi, 1)
                        blocks_with_next(act, split_up, rest)

                @block.vector
                def _(dve):
                    with only_if(dve, flag, 1):
                        nc.vector.memset(zeros[:], 0.0).then_inc(zeroed, 1)
                        dve.sem_inc(hidden_ready, 2)
                        dve.sem_inc(up_lo, 2)
                        dve.sem_inc(down_lo, 2)

                        def less(out, whole, scale, hi):
                            return nc.vector.scalar_tensor_tensor(out, whole, scale, hi, ALU.mult, ALU.subtract)

                        def split_up(e, s, turn):
                            dve.wait_ge(up_hi, e + 1)
                            for m in range(2):
                                ins = less(wu_lo[:, s, m, :, :].rearrange("p c n -> p (c n)"),
                                           w_up32[:, s, m, :, :].rearrange("p c n -> p (c n)"), W_SCALE,
                                           wu_hi[:, s, m, :, :].rearrange("p c n -> p (c n)"))
                            ins.then_inc(up_lo, 1)

                        def rest(e, s, turn):
                            dve.wait_ge(silu_done, e + 1)
                            into = hidden[:, s, :]
                            ins = nc.vector.scalar_tensor_tensor(into, pU[:, s, :], 1.0 if combine else 1.0 / W_SCALE, gated[:, s, :],
                                                                 ALU.mult, ALU.mult)
                            if combine:
                                Link(dve, vlink, e)(ins)
                                dve.wait_ge(weight_in[s], turn * 16 + 16)
                                into3 = into.rearrange("p (j n) -> p j n", j=NJ)
                                by = weight[:, s, :].unsqueeze(1).broadcast_to([P, NJ, SEQ])
                                ins = nc.vector.tensor_tensor(into3, into3, by, ALU.mult)
                            ins.then_inc(hidden_ready, 1)
                            dve.wait_ge(down_hi, e + 1)
                            less(wd_lo[:, s, :, :].rearrange("p c n -> p (c n)"),
                                 w_down32[:, s, :, :].rearrange("p c n -> p (c n)"), W_SCALE,
                                 wd_hi[:, s, :, :].rearrange("p c n -> p (c n)")).then_inc(down_lo, 1)
                            dve.wait_ge(hidden_hi, e + 1)
                            less(h_lo[:, s, :], into, 1.0, h_hi[:, s, :]).then_inc(hidden_lo, 1)
                        blocks_with_next(dve, split_up, rest)
                        dve.wait_ge(summed, 1)
                        for t in range(TT):
                            ins = nc.vector.scalar_tensor_tensor(x[:, t, :], pY[:, t, :], 1.0 / W_SCALE, x[:, t, :],
                                                                 ALU.mult, ALU.add)
                        ins.then_inc(vlink, 1)

                @block.tensor
                def _(pe):
                    with only_if(pe, flag, 1):
                        def all_sums(start, stop):
                            for t in range(TT):
                                for h in range(2):
                                    ins = nc.tensor.matmul(pY[:, t, h * 512:(h + 1) * 512], zeros[:, 0:P], zeros[:],
                                                           start=start, stop=stop, skip_group_check=True)
                            return ins

                        def up(e, s, turn):
                            pe.wait_ge(up_lo, e + 3)
                            for m, p in enumerate((pG, pU)):
                                for j in range(NJ):
                                    n = 0
                                    for c in range(KC):
                                        for w, h in ((wu_hi, hT_hi), (wu_hi, hT_lo), (wu_lo, hT_hi)):
                                            ins = nc.tensor.matmul(p[:, s, j * SEQ:(j + 1) * SEQ], w[:, s, m, c, j::NJ],
                                                                   h[:, c, :], start=(n == 0), stop=(n == 3 * KC - 1))
                                            n += 1
                            ins.then_inc(up_done, 1)

                        def down(e, s, turn):
                            pe.wait_ge(down_lo, e + 3)
                            pe.wait_ge(hidden_lo, e + 1)
                            for t in range(TT):
                                for j in range(NJ):
                                    at = j * SEQ + t * P
                                    for h, w in ((h_hi, wd_hi), (h_hi, wd_lo), (h_lo, wd_hi)):
                                        for half in range(2):
                                            ins = nc.tensor.matmul(pY[:, t, half * 512:(half + 1) * 512],
                                                                   h[:, s, at:at + P],
                                                                   w[:, s, j, half * 512:(half + 1) * 512],
                                                                   start=False, stop=False, skip_group_check=True)
                            ins.then_inc(down_done, 1)

                        pe.sem_inc(up_done, 2)
                        pe.sem_inc(down_done, 2)
                        pe.wait_ge(zeroed, 1)
                        all_sums(True, False)
                        up(0, 0, 0)
                        with pe.Fori(0, pairs) as i:
                            up(i * 2 + 1, 1, i)
                            down(i * 2, 0, i)
                            up(i * 2 + 2, 0, i + 1)
                            down(i * 2 + 1, 1, i)
                        if n_blocks % 2 == 0:
                            up(n_blocks - 1, 1, pairs)
                            down(n_blocks - 2, 0, pairs)
                        down(n_blocks - 1, (n_blocks - 1) % 2, pairs)
                        all_sums(False, True).then_inc(summed, 1)



def few_experts(nc, con, xn, gain, selects, w_gate, w_up, w_down, rows, x, weights, arrived, crowded,
                start):
    NJ = D_EXPERT // P
    BATCH = 8
    steps = 2 * BATCH
    turns = N_EXPERTS // steps
    with ExitStack() as ctx:
        sb = lambda n, s, d=F32: ctx.enter_context(nc.sbuf_tensor("few_" + n, s, d))
        w_up32, w_down32 = weights
        wu_hi = sb("wu_hi", [P, 2, 2, KC, D_EXPERT], F16)
        wu_lo = sb("wu_lo", [P, 2, 2, KC, D_EXPERT], F16)
        wd_hi = sb("wd_hi", [P, 2, NJ, D], F16)
        wd_lo = sb("wd_lo", [P, 2, NJ, D], F16)
        xn_hi = sb("xn_hi", [P, TT, D], F16)
        xn_lo = sb("xn_lo", [P, TT, D], F16)
        h_hi = sb("h_hi", [P, 2, KC, BATCH * CAP], F16)
        h_lo = sb("h_lo", [P, 2, KC, BATCH * CAP], F16)
        row = sb("row", [P, 2, 2, SEQ])
        hits = sb("hits", [P, SEQ])
        scatter = sb("scatter", [P, 2, SEQ], F16)
        share = sb("share", [P, 2, 1])
        gated = sb("gated", [CAP, D_EXPERT])
        hidden = sb("hidden", [CAP, D_EXPERT])
        hidT = sb("hidT", [P, NJ, 2, CAP], F16)
        y_hi = sb("y_hi", [P, D], F16)
        y_lo = sb("y_lo", [P, D], F16)
        pX = ctx.enter_context(nc.psum_tensor("few_pX", [P, 512], F32))
        pU = ctx.enter_context(nc.psum_tensor("few_pU", [P, 2, D_EXPERT], F32))
        pD = ctx.enter_context(nc.psum_tensor("few_pD", [P, D], F32))
        pY = ctx.enter_context(nc.psum_tensor("few_pY", [P, TT, D], F32))
        first_banks = [pX[:], pD[:, 0:512], pD[:, 512:D]]
        slot_id = con["slot_ids"][:, CAP:CAP + 1]
        with Stage(nc, "few", ["up0_in", "up1_in", "down0_in", "down1_in", "row0_in", "row1_in", "zeroed", "xn_split",
                               "up_hi", "up_lo", "down_hi", "down_lo", "up_done", "silu_done", "placed",
                               "hidden_ready", "hidden_turned", "hidT_hi", "hidT_lo", "down_done", "y_hi", "y_lo",
                               "scattered", "gathered", "h_hi", "h_lo", "summed", "vlink", "pe_passed",
                               "v_passed", "pool_passed", "matched",
                               "compared"]) as sems:
            (up0_in, up1_in, down0_in, down1_in, row0_in, row1_in, zeroed, xn_split, up_hi, up_lo, down_hi, down_lo,
             up_done, silu_done, placed, hidden_ready, hidden_turned, hidT_hi, hidT_lo, down_done, y_hi_ready,
             y_lo_ready, scattered, gathered, h_hi_ready, h_lo_ready, summed, vlink, pe_passed, v_passed,
             pool_passed, matched, compared) = sems
            up_in, down_in, row_in = [up0_in, up1_in], [down0_in, down1_in], [row0_in, row1_in]

            def over_experts(eng, step):
                with eng.Fori(0, turns) as i:
                    for k in range(steps):
                        step(i * steps + k, k, i * (steps // 2) + k // 2, i * 2 + k // BATCH)

            with nc.Block(no_gpsimd_drain=True) as block:
                @block.sync
                def _(sp):
                    with only_if(sp, crowded, 0):
                        def load(e, s, here=False):
                            sp.wait_ge(up_lo, e * 2 + 2)
                            if here:
                                sp.wait_ge(arrived, 3 * 16)
                                sp.sem_inc(up_in[s], 32)
                            else:
                                sp.dma_start(w_up32[:, s, 0, :, :], w_gate(e)).then_inc(up_in[s], 16)
                                sp.dma_start(w_up32[:, s, 1, :, :], w_up(e)).then_inc(up_in[s], 16)
                            sp.wait_ge(placed, e + 1)
                            sp.dma_start(row[:, s].rearrange("p a n -> p (a n)"), rows(e)).then_inc(row_in[s], 16)
                            sp.wait_ge(down_lo, e + 1)
                            if here:
                                sp.sem_inc(down_in[s], 16)
                            else:
                                sp.dma_start(w_down32[:, s, :, :], w_down(e)).then_inc(down_in[s], 16)
                        load(0, 0, here=True)
                        load(1, 1)
                        with sp.Fori(1, N_EXPERTS // 2) as i:
                            for s in range(2):
                                load(i * 2 + s, s)
                        sp.wait_ge(up_lo, N_EXPERTS * 2 + 2)
                        sp.sem_inc(up_in[0], 32)
                        sp.wait_ge(down_lo, N_EXPERTS + 1)
                        sp.sem_inc(down_in[0], 16)
                    for into, source, when in start:
                        sp.dma_start(into, source).then_inc(when, 16)

                @block.scalar
                def _(act):
                    with only_if(act, crowded, 0):
                        def split_up(e, s, turn, m):
                            act.wait_ge(up_in[s], turn * 32 + 32)
                            act.wait_ge(up_done, e + 1)
                            nc.scalar.activation(wu_hi[:, s, m, :, :], w_up32[:, s, m, :, :], ACT.Copy,
                                                 scale=W_SCALE).then_inc(up_hi, 1)

                        def keep_gathered(done, batch, c, source=pX):
                            act.wait_ge(gathered, done)
                            nc.scalar.activation(h_hi[:, batch, c, :], source[:], ACT.Copy,
                                                 scale=gain[:, c:c + 1]).then_inc(h_hi_ready, 1)

                        def split_down(s):
                            nc.scalar.activation(wd_hi[:, s, :, :], w_down32[:, s, :, :], ACT.Copy,
                                                 scale=W_SCALE).then_inc(down_hi, 1)

                        def step(e, k, turn, batch):
                            s = k % 2
                            act.wait_ge(matched, e + 1)
                            nc.scalar.activation(hits[:], hits[:], ACT.Copy,
                                                 accum_out=share[:, s, :]).then_inc(placed, 1)
                            split_up(e + 1, 1 - s, turn + s, 0)
                            split_up(e + 1, 1 - s, turn + s, 1)
                            act.wait_ge(up_done, e + 3)
                            act.wait_ge(hidden_ready, e + 1)
                            nc.scalar.activation(gated[:], pU[0:CAP, 0, :], ACT.Silu,
                                                 scale=1.0 / W_SCALE).then_inc(silu_done, 1)
                            keep_gathered(e + (KC + 1), 1 - k // BATCH, k % BATCH)
                            act.wait_ge(hidden_turned, e + 1)
                            nc.scalar.activation(hidT[:, :, 0, :],
                                                 pU[:, 0, 0:NJ * CAP].rearrange("p (j n) -> p j n", j=NJ),
                                                 ACT.Copy).then_inc(hidT_hi, 1)
                            act.wait_ge(down_in[1 - s], (turn + s) * 16 + 16)
                            act.wait_ge(down_done, e + 1)
                            split_down(1 - s)
                            act.wait_ge(down_done, e + 2)
                            act.wait_ge(scattered, e + 2)
                            nc.scalar.activation(y_hi[:], pD[:], ACT.Copy).then_inc(y_hi_ready, 1)

                        nc.scalar.activation(xn_hi[:].rearrange("p t n -> p (t n)"),
                                             xn[:].rearrange("p t n -> p (t n)"), ACT.Copy).then_inc(xn_split, 1)
                        for c in range(KC):
                            if c in (2, 5):
                                split_up(0, 0, 0, (c - 2) // 3)
                            keep_gathered(c + 1, 0, c, first_banks[c % 3])
                        act.wait_ge(down_in[0], 16)
                        split_down(0)
                        over_experts(act, step)

                @block.vector
                def _(dve):
                    with only_if(dve, crowded, 0):
                        def less(out, whole, scale, hi):
                            return nc.vector.scalar_tensor_tensor(out, whole, scale, hi, ALU.mult, ALU.subtract)

                        def split_up(e, s, m):
                            dve.wait_ge(up_hi, e * 2 + (m + 1))
                            flat = lambda w: w[:, s, m, :, :].rearrange("p c n -> p (c n)")
                            less(flat(wu_lo), flat(w_up32), W_SCALE, flat(wu_hi)).then_inc(up_lo, 1)

                        def split_down(done, s):
                            dve.wait_ge(down_hi, done)
                            flat = lambda w: w[:, s, :, :].rearrange("p c n -> p (c n)")
                            less(flat(wd_lo), flat(w_down32), W_SCALE, flat(wd_hi)).then_inc(down_lo, 1)

                        def keep_gathered(done, batch, c, source=pX):
                            dve.wait_ge(h_hi_ready, done)
                            less(h_lo[:, batch, c, :], source[:], gain[:, c:c + 1],
                                 h_hi[:, batch, c, :]).then_inc(h_lo_ready, 1)

                        def step(e, k, turn, batch):
                            s = k % 2
                            split_up(e + 1, 1 - s, 0)
                            wait_alone(dve, v_passed, placed, e + 3)
                            dve.wait_ge(silu_done, e + 1)
                            nc.vector.scalar_tensor_tensor(hidden[:], pU[0:CAP, 1, :], share[0:CAP, s, :], gated[:],
                                                           ALU.mult, ALU.mult).then_inc(hidden_ready, 1)
                            keep_gathered(e + (KC + 1), 1 - k // BATCH, k % BATCH)
                            dve.wait_ge(hidT_hi, e + 1)
                            less(hidT[:, :, 1, :], pU[:, 0, 0:NJ * CAP].rearrange("p (j n) -> p j n", j=NJ), 1.0,
                                 hidT[:, :, 0, :]).then_inc(hidT_lo, 1)
                            split_up(e + 1, 1 - s, 1)
                            split_down(e + 2, 1 - s)
                            dve.wait_ge(y_hi_ready, e + 1)
                            less(y_lo[:], pD[:], 1.0, y_hi[:]).then_inc(y_lo_ready, 1)

                        nc.vector.memset(y_hi[:], 0.0)
                        nc.vector.memset(y_lo[:], 0.0)
                        nc.vector.memset(scatter[:, 1, :], 0.0).then_inc(zeroed, 1)
                        dve.sem_inc(up_lo, 4)
                        dve.sem_inc(down_lo, 2)
                        dve.sem_inc(placed, 2)
                        dve.sem_inc(hidden_ready, 1)
                        dve.wait_ge(xn_split, 1)
                        less(xn_lo[:].rearrange("p t n -> p (t n)"), xn[:].rearrange("p t n -> p (t n)"), 1.0,
                             xn_hi[:].rearrange("p t n -> p (t n)")).then_inc(xn_split, 1)
                        for c in range(KC):
                            if c in (2, 5):
                                split_up(0, 0, (c - 2) // 3)
                            keep_gathered(c + 1, 0, c, first_banks[c % 3])
                        split_down(1, 0)
                        over_experts(dve, step)
                        dve.wait_ge(summed, 1)
                        for t in range(TT):
                            ins = nc.vector.scalar_tensor_tensor(x[:, t, :], pY[:, t, :], 1.0 / W_SCALE, x[:, t, :],
                                                                 ALU.mult, ALU.add)
                        ins.then_inc(vlink, 1)

                @block.gpsimd
                def _(pool):
                    with only_if(pool, crowded, 0):
                        def step(e, k, turn, batch):
                            s = k % 2
                            wait_alone(pool, pool_passed, row_in[s], turn * 16 + 16)
                            wait_alone(pool, pool_passed, scattered, e + 1)
                            wait_alone(pool, pool_passed, placed, e + 2)
                            nc.gpsimd.tensor_scalar(scatter[:, s, :], row[:, s, 1, :], slot_id, None,
                                                    ALU.is_equal).then_inc(compared, 1)
                            wait_alone(pool, pool_passed, compared, e + 1)
                            nc.gpsimd.tensor_tensor(hits[:], scatter[:, s, :], row[:, s, 0, :],
                                                    ALU.mult).then_inc(matched, 1)
                        pool.wait_ge(zeroed, 1)
                        over_experts(pool, step)

                @block.tensor
                def _(pe):
                    with only_if(pe, crowded, 0):
                        def gather(batch, c, into=pX):
                            n = 0
                            for t in range(TT):
                                for part in (xn_hi, xn_lo):
                                    ins = nc.tensor.matmul(into[:], part[:, t, c::KC],
                                                           selects[:, t, bass.ds(batch * (BATCH * CAP), BATCH * CAP)],
                                                           start=(n == 0), stop=(n == 2 * TT - 1))
                                    n += 1
                            ins.then_inc(gathered, 1)

                        def scatter_out(s, last=False):
                            for t in range(TT):
                                for part in (y_hi, y_lo):
                                    for h in range(2):
                                        ins = nc.tensor.matmul(pY[:, t, h * 512:(h + 1) * 512],
                                                               scatter[:, s, t * P:(t + 1) * P],
                                                               part[:, h * 512:(h + 1) * 512],
                                                               start=False, stop=last and part is y_lo,
                                                               skip_group_check=True)
                            ins.then_inc(summed if last else scattered, 1)

                        def step(e, k, turn, batch):
                            s = k % 2
                            wait_alone(pe, pe_passed, up_lo, e * 2 + 6)
                            if k % BATCH == 0:
                                wait_alone(pe, pe_passed, h_lo_ready, batch * BATCH + BATCH)
                            own = slice((k % BATCH) * CAP, (k % BATCH + 1) * CAP)
                            n = 0
                            for c in range(KC):
                                for h, w in ((h_hi, wu_hi), (h_hi, wu_lo), (h_lo, wu_hi)):
                                    ins = nc.tensor.matmul(pU[0:CAP, :, :], h[:, k // BATCH, c, own], w[:, s, :, c, :],
                                                           start=(n == 0), stop=(n == 3 * KC - 1))
                                    n += 1
                            ins.then_inc(up_done, 1)
                            wait_alone(pe, pe_passed, h_lo_ready, e + KC)
                            gather(batch + 1, k % BATCH)
                            wait_alone(pe, pe_passed, hidden_ready, e + 2)
                            for j in range(NJ):
                                ins = nc.tensor.transpose(pU[:, 0, j * CAP:(j + 1) * CAP], hidden[:, j::NJ],
                                                          con["identity"][0:CAP, 0:CAP])
                            ins.then_inc(hidden_turned, 1)
                            wait_alone(pe, pe_passed, y_lo_ready, e + 1)
                            scatter_out(1 - s)
                            wait_alone(pe, pe_passed, down_lo, e + 3)
                            wait_alone(pe, pe_passed, hidT_lo, e + 1)
                            for h in range(2):
                                n = 0
                                for j in range(NJ):
                                    for w in (wd_hi, wd_lo):
                                        ins = nc.tensor.matmul(pD[:, h * 512:(h + 1) * 512],
                                                               hidT[:, j].rearrange("p a n -> p (a n)"),
                                                               w[:, s, j, h * 512:(h + 1) * 512],
                                                               start=(n == 0), stop=(n == 2 * NJ - 1))
                                        n += 1
                            ins.then_inc(down_done, 1)

                        pe.sem_inc(up_done, 2)
                        pe.sem_inc(down_done, 1)
                        pe.sem_inc(scattered, 1)
                        pe.sem_inc(y_lo_ready, 1)
                        pe.wait_ge(zeroed, 1)
                        for t in range(TT):
                            for h in range(2):
                                nc.tensor.matmul(pY[:, t, h * 512:(h + 1) * 512], y_lo[:, 0:P], y_hi[:, 0:512],
                                                 start=True, stop=False, skip_group_check=True)
                        pe.wait_ge(xn_split, 2)
                        for c in range(KC):
                            if c >= 3:
                                pe.wait_ge(h_lo_ready, c - 2)
                            gather(0, c, first_banks[c % 3])
                        over_experts(pe, step)
                        pe.wait_ge(y_lo_ready, N_EXPERTS + 1)
                        scatter_out((N_EXPERTS - 1) % 2, last=True)



def rope(link, eng, x, cs, tmp):
    p, tt, heads, d = x.shape
    half = d // 2
    flat = [tmp[:, n, 0:tt * heads * half].rearrange("p (t h d) -> p t h d", t=tt, h=heads) for n in range(4)]
    cos = cs[:, :, 0:half].unsqueeze(2).broadcast_to([p, tt, heads, half])
    sin = cs[:, :, half:d].unsqueeze(2).broadcast_to([p, tt, heads, half])
    x1, x2 = x[:, :, :, 0:half], x[:, :, :, half:d]
    link(eng.tensor_tensor(flat[0], x1, cos, ALU.mult))
    link(eng.tensor_tensor(flat[1], x2, sin, ALU.mult))
    link(eng.tensor_tensor(flat[2], x2, cos, ALU.mult))
    link(eng.tensor_tensor(flat[3], x1, sin, ALU.mult))
    link(eng.tensor_tensor(x1, flat[0], flat[1], ALU.subtract))
    link(eng.tensor_tensor(x2, flat[2], flat[3], ALU.add))


def heads_of(x, n):
    return x.rearrange("p t (h d) -> p t h d", h=n)


def mla_prepare(nc, con, feat, qk, k_nope, positions, g_qn, g_kn):
    name = "mla"
    with ExitStack() as ctx:
        sb = lambda n, s, d=F32: ctx.enter_context(nc.sbuf_tensor(f"{name}_{n}", s, d))
        gains = sb("gains", [P, 2, MLA_QK])
        pos_i = sb("pos_i", [P, TT], I32)
        pos = sb("pos", [P, TT])
        ang = sb("ang", [P, TT, 16])
        turns = sb("turns", [P, TT, 16])
        wrap = sb("wrap", [P, TT, 16])
        cs = sb("cs", [P, TT, 32])
        arg = sb("arg", [P, TT, 32])
        square = sb("square", [P, 2 * TT * MLA_H, MLA_QK])
        st = sb("st", [P, 3, 2 * TT * MLA_H])
        tmp = sb("tmp", [P, 4, TT * MLA_H * 16])
        rows = [qk[:, n].rearrange("p t h d -> p (t h) d") for n in range(2)]
        half = [slice(n * TT * MLA_H, (n + 1) * TT * MLA_H) for n in range(2)]
        with Stage(nc, name, ["gains_in", "k_filled", "angles", "sines", "squares", "recips", "rstd", "vlink"]) as sems:
            gains_in, k_filled, angles, sines, squares, recips, rstd, vlink = sems
            with nc.Block(no_gpsimd_drain=True) as block:
                @block.sync
                def _(sp):
                    sp.dma_start(gains[:, 0, :], spread(g_qn)).then_inc(gains_in, 16)
                    sp.dma_start(gains[:, 1, :], spread(g_kn)).then_inc(gains_in, 16)
                    sp.dma_start(pos_i[:], positions.rearrange("a (t p) -> p (a t)", p=P),
                                 allow_slow_non_contiguous=True).then_inc(gains_in, 16)

                @block.gpsimd
                def _(pool):
                    for t in range(TT):
                        part = feat[:, t, Q_RANK + KV_RANK:MLA_IN].unsqueeze(1).broadcast_to([P, MLA_H, MLA_ROPE])
                        nc.gpsimd.tensor_copy(qk[:, 1, t, :, MLA_NOPE:MLA_QK], part).then_inc(k_filled, 1)
                        nc.gpsimd.tensor_copy(qk[:, 1, t, :, 0:MLA_NOPE],
                                              heads_of(k_nope, MLA_H)[:, t]).then_inc(k_filled, 1)

                @block.scalar
                def _(act):
                    nc.scalar.activation(square[:, half[0], :], rows[0], ACT.Square).then_inc(squares, 1)
                    act.wait_ge(k_filled, 2 * TT)
                    nc.scalar.activation(square[:, half[1], :], rows[1], ACT.Square).then_inc(squares, 1)
                    for n in range(2):
                        act.wait_ge(recips, n + 1)
                        nc.scalar.activation(st[:, 2, half[n]], st[:, 1, half[n]], ACT.Sqrt).then_inc(rstd, 1)
                    act.wait_ge(angles, 1)
                    nc.scalar.activation(cs[:], arg[:], ACT.Sin).then_inc(sines, 1)

                @block.vector
                def _(dve):
                    link = Link(dve, vlink)
                    v = nc.vector

                    def mean_square(n):
                        dve.wait_ge(squares, n + 1)
                        link(v.tensor_reduce(st[:, 0, half[n]], square[:, half[n], :], AX_X, ALU.add))
                        link(v.tensor_scalar(st[:, 0, half[n]], st[:, 0, half[n]], 1.0 / MLA_QK, EPS,
                                             ALU.mult, ALU.add))
                        v.reciprocal(st[:, 1, half[n]], st[:, 0, half[n]]).then_inc(recips, 1)

                    def normalise(n):
                        dve.wait_ge(rstd, n + 1)
                        shape = list(rows[n].shape)
                        link(v.tensor_tensor(rows[n], rows[n], st[:, 2, half[n]].unsqueeze(2).broadcast_to(shape),
                                             ALU.mult))
                        link(v.tensor_tensor(rows[n], rows[n], gains[:, n, :].unsqueeze(1).broadcast_to(shape),
                                             ALU.mult))

                    mean_square(0)
                    dve.wait_ge(gains_in, 48)
                    link(v.tensor_copy(pos[:], pos_i[:]))
                    for t in range(TT):
                        link(v.tensor_scalar(ang[:, t, :], con["inv_freq"], pos[:, t:t + 1], None, ALU.mult))
                    link(v.tensor_scalar(turns[:], ang[:], float(1 / (2 * np.pi)), 12582912.0, ALU.mult, ALU.add))
                    link(v.tensor_scalar(turns[:], turns[:], -12582912.0, None, ALU.add))
                    part = 2 * np.pi
                    for bits in (8, 10, 24):
                        scale = 2.0 ** (bits - 1 - np.floor(np.log2(part)))
                        c = float(np.float32(np.floor(part * scale) / scale))
                        part -= c
                        link(v.scalar_tensor_tensor(ang[:], turns[:], -c, ang[:], ALU.mult, ALU.add))
                    pi = float(np.float32(3.1415925))
                    link(v.tensor_scalar(arg[:, :, 16:32], ang[:], pi, -pi, ALU.min, ALU.max))
                    link(v.tensor_scalar(ang[:], ang[:], float(np.pi / 2), None, ALU.add))
                    link(v.tensor_scalar(wrap[:], ang[:], pi, -2 * float(np.pi), ALU.is_gt, ALU.mult))
                    link(v.tensor_tensor(ang[:], ang[:], wrap[:], ALU.add))
                    v.tensor_scalar(arg[:, :, 0:16], ang[:], pi, -pi, ALU.min, ALU.max).then_inc(angles, 1)
                    mean_square(1)
                    normalise(0)
                    normalise(1)
                    dve.wait_ge(sines, 1)
                    for a in range(2):
                        rope(link, v, qk[:, a, :, :, MLA_NOPE:MLA_QK], cs[:], tmp)


def rms_scale(nc, name, x, width, gain):
    with ExitStack() as ctx:
        sb = lambda n, s, d=F32: ctx.enter_context(nc.sbuf_tensor(f"{name}_{n}", s, d))
        row = sb("row", [P, width])
        sq = sb("sq", [P, TT, width])
        st = sb("st", [P, 3, TT])
        with Stage(nc, name, ["gain_in", "squares", "recips", "rstd", "vlink"]) as sems:
            gain_in, squares, recips, rstd, vlink = sems
            with nc.Block(no_gpsimd_drain=True) as block:
                @block.sync
                def _(sp):
                    sp.dma_start(row[:], spread(gain)).then_inc(gain_in, 16)

                @block.scalar
                def _(act):
                    for t in range(TT):
                        nc.scalar.activation(sq[:, t, :], x[:, t, :], ACT.Square,
                                             accum_out=st[:, 0, t:t + 1]).then_inc(squares, 1)
                    act.wait_ge(recips, 1)
                    nc.scalar.activation(st[:, 2, :], st[:, 1, :], ACT.Sqrt).then_inc(rstd, 1)

                @block.vector
                def _(dve):
                    link = Link(dve, vlink)
                    dve.wait_ge(squares, TT)
                    link(nc.vector.tensor_scalar(st[:, 0, :], st[:, 0, :], 1.0 / width, EPS, ALU.mult, ALU.add))
                    nc.vector.reciprocal(st[:, 1, :], st[:, 0, :]).then_inc(recips, 1)
                    dve.wait_ge(rstd, 1)
                    dve.wait_ge(gain_in, 16)
                    for t in range(TT):
                        link(nc.vector.scalar_tensor_tensor(x[:, t, :], x[:, t, :], st[:, 2, t:t + 1], row[:],
                                                            ALU.mult, ALU.mult))


DECAY = float(np.exp(-0.5))


def rwkv_tiles(stack, nc):
    sb = lambda n, s: stack.enter_context(nc.sbuf_tensor(f"rw_{n}", s, F32))
    return sb("prev", [P, TT, RW_IN]), sb("mu", [P, RW_IN]), sb("lora", [P, 2, RW_W]), sb("row", [P, 7, RW_W])


def rwkv_loads(tiles, feat, w):
    prev, mu, lora, row = tiles
    names = ["rw_w0", "rw_a0", "rw_k_k", "rw_k_a", "rw_r_k", "rw_lnx_g", "rw_lnx_b"]
    return [(prev[1:P, :, :], feat[0:P - 1, :, :]), (prev[0:1, 1, :], feat[P - 1:P, 0, :]),
            (mu[:], spread(w["rw_mu"])), (lora[0:64, 0, :], w["rw_w2"]), (lora[64:P, 0, :], w["rw_a2"]),
            (lora[:, 1, :], w["rw_g2"])] + [(row[:, n, :], spread(w[x])) for n, x in enumerate(names)]


def rwkv(nc, con, feat, w, out, tiles):
    HT = RW_H * TT
    prev, mu, lora, row = tiles
    with ExitStack() as ctx:
        sb = lambda n, s, d=F32: ctx.enter_context(nc.sbuf_tensor(f"rw_{n}", s, d))
        W0, A0, K_K, K_A, R_K, LNX_G, LNX_B = range(7)
        sig = sb("sig", [P, TT, RW_W])
        a = sb("a", [P, TT, RW_W])
        g = sb("g", [P, TT, RW_W])
        r, k, v = (feat[:, :, n * RW_W:(n + 1) * RW_W] for n in range(3))
        bonus = sb("bonus", [P, HT])

        with ExitStack() as inner:
            sbi = lambda n, s, d=F32: inner.enter_context(nc.sbuf_tensor(f"rw1_{n}", s, d))
            loraT = sbi("loraT", [P, TT, 2, P])
            pT = inner.enter_context(nc.psum_tensor("rw1_pT", [P, TT, 512], F32))
            pL = inner.enter_context(nc.psum_tensor("rw1_pL", [P, 3, TT, 512], F32))
            with Stage(nc, "rw1", ["first_zero", "mixed", "squashed",
                                   "turned", "turned_out", "products", "zw_ready", "za_ready", "g_ready",
                                   "vlink"]) as sems:
                (first_zero, mixed, squashed, turned, turned_out, products,
                 zw_ready, za_ready, g_ready, vlink) = sems
                with nc.Block(no_gpsimd_drain=True) as block:
                    @block.gpsimd
                    def _(pool):
                        nc.gpsimd.memset(prev[0:1, 0, :], 0.0).then_inc(first_zero, 1)

                    @block.vector
                    def _(dve):
                        link = Link(dve, vlink)
                        dve.wait_ge(first_zero, 1)
                        for lo, hi in ((3 * RW_W, RW_IN), (0, 3 * RW_W)):
                            x, p = feat[:, :, lo:hi], prev[:, :, lo:hi]
                            link(nc.vector.tensor_tensor(p, p, x, ALU.subtract))
                            link(nc.vector.tensor_tensor(p, p, mu[:, lo:hi].unsqueeze(1)
                                                         .broadcast_to([P, TT, hi - lo]), ALU.mult))
                            nc.vector.tensor_tensor(x, x, p, ALU.add).then_inc(mixed, 1)
                        dve.wait_ge(products, 1)
                        for t in range(TT):
                            nc.vector.tensor_tensor(sig[:, t, :], pL[:, 0, t, :], row[:, W0, :],
                                                    ALU.add).then_inc(zw_ready, 1)
                            nc.vector.tensor_tensor(a[:, t, :], pL[:, 1, t, :], row[:, A0, :],
                                                    ALU.add).then_inc(za_ready, 1)

                    @block.scalar
                    def _(act):
                        act.wait_ge(mixed, 1)
                        nc.scalar.activation(feat[:, :, 1536:1600], feat[:, :, 1536:1600],
                                             ACT.Tanh).then_inc(squashed, 1)
                        nc.scalar.activation(feat[:, :, 1664:RW_IN], feat[:, :, 1664:RW_IN],
                                             ACT.Sigmoid).then_inc(squashed, 1)
                        for t in range(TT):
                            act.wait_ge(turned, t + 1)
                            nc.scalar.activation(loraT[:, t, :, :], pT[:, t, 0:2 * P].rearrange("p (a n) -> p a n", a=2),
                                                 ACT.Copy).then_inc(turned_out, 1)
                        act.wait_ge(zw_ready, TT)
                        nc.scalar.activation(sig[:], sig[:], ACT.Sigmoid).then_inc(g_ready, 1)
                        act.wait_ge(za_ready, TT)
                        nc.scalar.activation(a[:], a[:], ACT.Sigmoid).then_inc(g_ready, 1)
                        for t in range(TT):
                            nc.scalar.activation(g[:, t, :], pL[:, 2, t, :], ACT.Copy).then_inc(g_ready, 1)

                    @block.tensor
                    def _(pe):
                        pe.wait_ge(squashed, 2)
                        for t in range(TT):
                            for c in range(2):
                                ins = nc.tensor.transpose(pT[:, t, c * P:(c + 1) * P],
                                                          feat[:, t, 1536 + c * P:1536 + (c + 1) * P],
                                                          con["identity"])
                            ins.then_inc(turned, 1)
                        for t in range(TT):
                            pe.wait_ge(turned_out, t + 1)
                            nc.tensor.matmul(pL[:, 0, t, :], loraT[0:64, t, 0, :], lora[0:64, 0, :],
                                             start=True, stop=True)
                            nc.tensor.matmul(pL[:, 1, t, :], loraT[64:P, t, 0, :], lora[64:P, 0, :],
                                             start=True, stop=True)
                            ins = nc.tensor.matmul(pL[:, 2, t, :], loraT[:, t, 1, :], lora[:, 1, :],
                                                   start=True, stop=True)
                        ins.then_inc(products, 1)

        kkd = sb("kkd", [P, TT, RW_W])
        rd = sb("rd", [P, TT, RW_W])
        bd = sb("bd", [P, TT, RW_W])
        kd = sb("kd", [P, TT, RW_W])
        carry = sb("carry", [P, RW_H // 2])
        with ExitStack() as inner:
            sbi = lambda n, s, d=F32: inner.enter_context(nc.sbuf_tensor(f"rw2_{n}", s, d))
            decay = sbi("decay", [P, TT, RW_W])
            undo = sbi("undo", [P, TT, RW_W])
            before = sbi("before", [P, TT, RW_W])
            tmp = sbi("tmp", [P, TT, RW_W])
            st = sbi("st", [P, 3, HT])
            pD = inner.enter_context(nc.psum_tensor("rw2_pD", [P, 2, TT, 512], F32))
            pC = inner.enter_context(nc.psum_tensor("rw2_pC", [P, 512], F32))
            flat = lambda x: x.rearrange("p t (h d) -> p (t h) d", h=RW_H)
            with Stage(nc, "rw2", ["sums", "ends", "exps", "norms", "roots", "vlink"]) as sems:
                sums, ends, exps, norms, roots, vlink = sems
                with nc.Block(no_gpsimd_drain=True) as block:
                    @block.tensor
                    def _(pe):
                        for t in range(TT):
                            for n in range(2):
                                ins = nc.tensor.matmul(pD[:, n, t, :], con["decay_sums"][:, n * P:(n + 1) * P],
                                                       sig[:, t, :], start=True, stop=True)
                        ins.then_inc(sums, 1)
                        for m in range(RW_H // 2):
                            for t in range(TT):
                                ins = nc.tensor.matmul(pC[:, m:m + 1], sig[:, t, m * P:(m + 1) * P],
                                                       con["decay_ends"][:, t:t + 1], start=(t == 0), stop=(t == 1))
                        ins.then_inc(ends, 1)

                    @block.scalar
                    def _(act):
                        act.wait_ge(sums, 1)
                        for t in range(TT):
                            nc.scalar.activation(decay[:, t, :], pD[:, 0, t, :], ACT.Exp, scale=-DECAY).then_inc(exps, 1)
                            nc.scalar.activation(undo[:, t, :], pD[:, 0, t, :], ACT.Exp, scale=DECAY).then_inc(exps, 1)
                            nc.scalar.activation(before[:, t, :], pD[:, 1, t, :], ACT.Exp,
                                                 scale=-DECAY).then_inc(exps, 1)
                        act.wait_ge(ends, 1)
                        nc.scalar.activation(carry[:], pC[:, 0:RW_H // 2], ACT.Exp, scale=-DECAY).then_inc(exps, 1)
                        act.wait_ge(norms, 1)
                        nc.scalar.activation(st[:, 2, :], st[:, 1, :], ACT.Sqrt).then_inc(roots, 1)

                    @block.vector
                    def _(dve):
                        link = Link(dve, vlink)
                        tt = lambda o, x, y, op=ALU.mult: link(nc.vector.tensor_tensor(o, x, y, op))
                        rows = lambda n: row[:, n, :].unsqueeze(1).broadcast_to([P, TT, RW_W])
                        tt(kkd[:], k, rows(K_K))
                        tt(tmp[:], kkd[:], kkd[:])
                        link(nc.vector.tensor_reduce(st[:, 0, :], flat(tmp[:]), AX_X, ALU.add))
                        link(nc.vector.tensor_scalar(st[:, 0, :], st[:, 0, :], 1e-12, None, ALU.add))
                        nc.vector.reciprocal(st[:, 1, :], st[:, 0, :]).then_inc(norms, 1)
                        link(nc.vector.tensor_scalar(tmp[:], a[:], -1.0, None, ALU.add))
                        tt(tmp[:], tmp[:], rows(K_A))
                        link(nc.vector.tensor_scalar(tmp[:], tmp[:], 1.0, None, ALU.add))
                        tt(k, k, tmp[:])
                        tt(tmp[:], r, k)
                        tt(tmp[:], tmp[:], rows(R_K))
                        link(nc.vector.tensor_reduce(bonus[:], flat(tmp[:]), AX_X, ALU.add))
                        dve.wait_ge(roots, 1)
                        tt(flat(kkd[:]), flat(kkd[:]), st[:, 2, :].unsqueeze(2).broadcast_to([P, HT, RW_N]))
                        tt(bd[:], kkd[:], a[:])
                        dve.wait_ge(exps, 7)
                        tt(rd[:], r, decay[:])
                        tt(kkd[:], kkd[:], before[:])
                        tt(bd[:], bd[:], undo[:])
                        tt(kd[:], k, undo[:])

        AT = sb("AT", [P, HT, P])
        ET = sb("ET", [P, HT, P])
        BT = sb("BT", [P, HT, P])
        FT = sb("FT", [P, HT, P])
        X = sb("X", [P, HT, P])
        XT = sb("XT", [P, HT, P])
        turned4 = sb("turned4", [P, TT * 4, 4 * P])
        KKT, RT, BBT, KT = range(4)
        masks = con["level_masks"]
        mask = lambda n: masks[:, n * P:(n + 1) * P]
        UPTO, STRICT, LEVEL0_T = SOLVE_LEVELS + 1, SOLVE_LEVELS + 2, SOLVE_LEVELS
        with ExitStack() as inner:
            pQ = inner.enter_context(nc.psum_tensor("rw3_p", [P, 8, 512], F32))
            with Stage(nc, "rw3", ["turned", "out_a", "out_v", "products", "masked", "vlink"]) as sems:
                turned, out_a, out_v, products, masked, vlink = sems
                with nc.Block(no_gpsimd_drain=True) as block:
                    @block.tensor
                    def _(pe):
                        for n in range(TT * 4):
                            t, m = divmod(n, 4)
                            for q, x in enumerate((kkd, rd, bd, kd)):
                                ins = nc.tensor.transpose(pQ[:, n, q * P:(q + 1) * P], x[:, t, m * P:(m + 1) * P],
                                                          con["identity"])
                            ins.then_inc(turned, 1)
                        for n in range(HT):
                            t, h = divmod(n, RW_H)
                            u = t * 4 + h // 2
                            lo = 64 * (h % 2)
                            part = lambda q, w=P: turned4[lo:lo + 64, u, q * P:q * P + w]
                            b = n % 4 * 2
                            pe.wait_ge(out_a if u % 2 else out_v, u // 2 + 1)
                            if n < 4:
                                pe.wait_ge(out_v, b // 2 + 1)
                                pe.wait_ge(out_a, b // 2 + 1)
                            else:
                                pe.wait_ge(masked, n - 3)
                            nc.tensor.matmul(pQ[:, b, 0:2 * P], part(BBT), part(KKT, 2 * P), start=True, stop=True)
                            nc.tensor.matmul(pQ[:, b, 2 * P:3 * P], part(KKT), part(BBT), start=True, stop=True)
                            nc.tensor.matmul(pQ[:, b + 1, 0:2 * P], part(KT), part(KKT, 2 * P),
                                             start=True, stop=True).then_inc(products, 1)

                    @block.scalar
                    def _(act):
                        for u in range(1, TT * 4, 2):
                            act.wait_ge(turned, u + 1)
                            nc.scalar.activation(turned4[:, u, :], pQ[:, u, :], ACT.Copy).then_inc(out_a, 1)

                    @block.vector
                    def _(dve):
                        for u in range(0, TT * 4, 2):
                            dve.wait_ge(turned, u + 1)
                            nc.vector.tensor_copy(turned4[:, u, :], pQ[:, u, :]).then_inc(out_v, 1)
                        link = Link(dve, vlink)
                        tt = nc.vector.tensor_tensor
                        for n in range(HT):
                            b = n % 4 * 2
                            dve.wait_ge(products, n + 1)
                            tt(X[:, n, :], pQ[:, b, 2 * P:3 * P], mask(LEVEL0_T), ALU.mult)
                            tt(XT[:, n, :], pQ[:, b, 0:P], mask(0), ALU.mult)
                            tt(AT[:, n, :], pQ[:, b, 0:P], mask(STRICT), ALU.mult)
                            tt(ET[:, n, :], pQ[:, b, P:2 * P], mask(UPTO), ALU.mult)
                            tt(BT[:, n, :], pQ[:, b + 1, 0:P], mask(STRICT), ALU.mult)
                            tt(FT[:, n, :], pQ[:, b + 1, P:2 * P], mask(UPTO), ALU.mult).then_inc(masked, 1)
                        dve.wait_ge(masked, HT)
                        ident = con["identity"].unsqueeze(1).broadcast_to([P, HT, P])
                        link(tt(X[:], ident, X[:], ALU.subtract))
                        link(tt(XT[:], ident, XT[:], ALU.subtract))

        with ExitStack() as inner:
            sbi = lambda n, s, d=F32: inner.enter_context(nc.sbuf_tensor(f"rw4_{n}", s, d))
            offT = sbi("offT", [P, HT, P])
            Wm = prev[:].rearrange("p t n -> p (t n)")[:, 0:HT * P].rearrange("p (n i) -> p n i", i=P)
            pW = inner.enter_context(nc.psum_tensor("rw4_pW", [P, 4, 512], F32))
            pX = inner.enter_context(nc.psum_tensor("rw4_pX", [P, 4, 512], F32))
            GR = 4
            with Stage(nc, "rw4", ["off_ready", "w_done", "w_out", "xt_done", "x_done", "xt_new", "x_new",
                                   "pool_passed"]) as sems:
                off_ready, w_done, w_out, xt_done, x_done, xt_new, x_new, pool_passed = sems
                with nc.Block(no_gpsimd_drain=True) as block:
                    def group(x, q):
                        return x[:, q * GR:(q + 1) * GR, :]

                    def bank(p, q):
                        return p[:, q, :].rearrange("p (n c) -> p n c", n=GR)

                    @block.gpsimd
                    def _(pool):
                        with pool.Fori(0, SOLVE_LEVELS - 1) as i:
                            for q in range(GR):
                                wait_alone(pool, pool_passed, w_done, i * GR + (q + 1))
                                lev = masks[:, bass.ds(i * P + P, P)].unsqueeze(1).broadcast_to([P, GR, P])
                                nc.gpsimd.tensor_tensor(group(offT, q), group(AT, q), lev,
                                                        ALU.mult).then_inc(off_ready, 1)

                    @block.tensor
                    def _(pe):
                        pe.sem_inc(w_done, GR)
                        with pe.Fori(0, SOLVE_LEVELS - 1) as i:
                            for q in range(GR):
                                pe.wait_ge(off_ready, i * GR + (q + 1))
                                pe.wait_ge(x_new, i * GR + (q + 1))
                                for n in range(GR):
                                    ins = nc.tensor.matmul(pW[:, q, n * P:(n + 1) * P], offT[:, q * GR + n, :],
                                                           X[:, q * GR + n, :], start=True, stop=True)
                                ins.then_inc(w_done, 1)
                            for q in range(GR):
                                pe.wait_ge(w_out, i * GR + (q + 1))
                                pe.wait_ge(xt_new, i * GR + (q + 1))
                                for n in range(GR):
                                    ins = nc.tensor.matmul(pX[:, q, n * P:(n + 1) * P], Wm[:, q * GR + n, :],
                                                           XT[:, q * GR + n, :], start=True, stop=True)
                                ins.then_inc(xt_done, 1)
                                for n in range(GR):
                                    ins = nc.tensor.matmul(pW[:, q, n * P:(n + 1) * P], XT[:, q * GR + n, :],
                                                           Wm[:, q * GR + n, :], start=True, stop=True)
                                ins.then_inc(x_done, 1)

                    @block.scalar
                    def _(act):
                        with act.Fori(0, SOLVE_LEVELS - 1) as i:
                            for q in range(GR):
                                act.wait_ge(w_done, i * GR + (q + 1 + GR))
                                nc.scalar.activation(group(Wm, q), bank(pW, q), ACT.Copy).then_inc(w_out, 1)

                    @block.vector
                    def _(dve):
                        dve.sem_inc(xt_new, GR)
                        dve.sem_inc(x_new, GR)
                        with dve.Fori(0, SOLVE_LEVELS - 1) as i:
                            for q in range(GR):
                                dve.wait_ge(x_done, i * GR + (q + 1))
                                nc.vector.tensor_tensor(group(XT, q), group(XT, q), bank(pX, q),
                                                        ALU.subtract).then_inc(xt_new, 1)
                                nc.vector.tensor_tensor(group(X, q), group(X, q), bank(pW, q),
                                                        ALU.subtract).then_inc(x_new, 1)

        with ExitStack() as inner:
            sbi = lambda n, s, d=F32: inner.enter_context(nc.sbuf_tensor(f"rw5_{n}", s, d))
            rhs = sbi("rhs", [P, TT, RW_W])
            U = sbi("U", [P, TT, RW_W])
            Z = sbi("Z", [P, 4, P])
            spare = prev[:].rearrange("p t n -> p (t n)")[:, 0:3 * TT * RW_W].rearrange("p (a t n) -> p a t n", a=3, t=TT)
            y, sq, added = spare[:, 0], spare[:, 1], spare[:, 2]
            st = sbi("st", [P, 4, HT])
            pR = inner.enter_context(nc.psum_tensor("rw5_pR", [P, TT, 512], F32))
            pU = inner.enter_context(nc.psum_tensor("rw5_pU", [P, TT, 512], F32))
            pY = inner.enter_context(nc.psum_tensor("rw5_pY", [P, TT, 512], F32))
            pZ = inner.enter_context(nc.psum_tensor("rw5_pZ", [P, 512], F32))
            with Stage(nc, "rw5", ["r_done", "rhs_ready", "u_done", "u_ready", "z_zero", "z_done", "z_ready", "y_done",
                                   "centred", "squares", "recips", "roots", "vlink"]) as sems:
                (r_done, rhs_ready, u_done, u_ready, z_zero, z_done, z_ready, y_done, centred, squares, recips, roots,
                 vlink) = sems
                with nc.Block(no_gpsimd_drain=True) as block:
                    @block.gpsimd
                    def _(pool):
                        nc.gpsimd.memset(Z[:], 0.0).then_inc(z_zero, 1)

                    @block.tensor
                    def _(pe):
                        def with_state(into, which):
                            for m in range(RW_H // 2):
                                ins = nc.tensor.matmul(into[:, 1, m * P:(m + 1) * P],
                                                       turned4[:, 4 + m, which * P:(which + 1) * P], Z[:, m, :],
                                                       start=False, stop=True, skip_group_check=True)
                            return ins

                        for t in range(TT):
                            if t:
                                pe.wait_ge(z_ready, 1)
                            hs = lambda h: slice(h * RW_N, (h + 1) * RW_N)
                            for h in range(RW_H):
                                ins = nc.tensor.matmul(pR[:, t, hs(h)], BT[:, t * RW_H + h, :], v[:, t, hs(h)],
                                                       start=(h == 0), stop=(t == 0), skip_group_check=True)
                            if t:
                                ins = with_state(pR, KKT)
                            ins.then_inc(r_done, 1)
                            pe.wait_ge(rhs_ready, t + 1)
                            for h in range(RW_H):
                                ins = nc.tensor.matmul(pU[:, t, hs(h)], XT[:, t * RW_H + h, :], rhs[:, t, hs(h)],
                                                       start=True, stop=True)
                            ins.then_inc(u_done, 1)
                            pe.wait_ge(u_ready, t + 1)
                            if t == 0:
                                for m in range(RW_H // 2):
                                    ms = slice(m * P, (m + 1) * P)
                                    nc.tensor.matmul(pZ[:, ms], bd[:, 0, ms], U[:, 0, ms], start=True, stop=False)
                                    ins = nc.tensor.matmul(pZ[:, ms], kd[:, 0, ms], v[:, 0, ms],
                                                           start=False, stop=True)
                                ins.then_inc(z_done, 1)
                            for h in range(RW_H):
                                n = t * RW_H + h
                                nc.tensor.matmul(pY[:, t, hs(h)], ET[:, n, :], U[:, t, hs(h)], start=(h == 0), stop=False,
                                                 skip_group_check=True)
                                ins = nc.tensor.matmul(pY[:, t, hs(h)], FT[:, n, :], v[:, t, hs(h)],
                                                       start=False, stop=(t == 0), skip_group_check=True)
                            if t:
                                ins = with_state(pY, RT)
                            ins.then_inc(y_done, 1)

                    @block.scalar
                    def _(act):
                        for t in range(TT):
                            own = slice(t * RW_H, (t + 1) * RW_H)
                            act.wait_ge(centred, t + 1)
                            nc.scalar.activation(sq[:, t, :], y[:, t, :], ACT.Square).then_inc(squares, 1)
                            act.wait_ge(recips, t + 1)
                            nc.scalar.activation(st[:, 3, own], st[:, 2, own], ACT.Sqrt).then_inc(roots, 1)

                    @block.vector
                    def _(dve):
                        link = Link(dve, vlink)
                        tt = lambda o, x, y, op=ALU.mult: link(nc.vector.tensor_tensor(o, x, y, op))
                        heads = lambda x: x.rearrange("p (h d) -> p h d", h=RW_H)
                        each = lambda x: x.unsqueeze(2).broadcast_to([P, RW_H, RW_N])

                        def finish(t):
                            own = slice(t * RW_H, (t + 1) * RW_H)
                            yt = y[:, t, :]
                            dve.wait_ge(y_done, t + 1)
                            link(nc.vector.tensor_reduce(st[:, 0, own], heads(pY[:, t, :]), AX_X, ALU.add))
                            link(nc.vector.tensor_scalar(st[:, 0, own], st[:, 0, own], 1.0 / RW_N, None, ALU.mult))
                            nc.vector.tensor_tensor(heads(yt), heads(pY[:, t, :]), each(st[:, 0, own]),
                                                    ALU.subtract).then_inc(centred, 1)
                            dve.wait_ge(squares, t + 1)
                            link(nc.vector.tensor_reduce(st[:, 1, own], heads(sq[:, t, :]), AX_X, ALU.add))
                            link(nc.vector.tensor_scalar(st[:, 1, own], st[:, 1, own], 1.0 / RW_N, LNX_EPS,
                                                         ALU.mult, ALU.add))
                            nc.vector.reciprocal(st[:, 2, own], st[:, 1, own]).then_inc(recips, 1)
                            dve.wait_ge(roots, t + 1)
                            tt(heads(yt), heads(yt), each(st[:, 3, own]))
                            tt(yt, yt, row[:, LNX_G, :])
                            tt(yt, yt, added[:, t, :], ALU.add)
                            tt(out[:, t, :], yt, g[:, t, :])

                        for t in range(TT):
                            tt(heads(added[:, t, :]), heads(v[:, t, :]), each(bonus[:, t * RW_H:(t + 1) * RW_H]))
                            tt(added[:, t, :], added[:, t, :], row[:, LNX_B, :], ALU.add)
                        for t in range(TT):
                            dve.wait_ge(r_done, t + 1)
                            nc.vector.tensor_scalar(rhs[:, t, :], pR[:, t, :], -1.0, None,
                                                    ALU.mult).then_inc(rhs_ready, 1)
                            dve.wait_ge(u_done, t + 1)
                            nc.vector.tensor_copy(U[:, t, :], pU[:, t, :]).then_inc(u_ready, 1)
                            if t == 0:
                                dve.wait_ge(z_done, 1)
                                dve.wait_ge(z_zero, 1)
                                for lo in (0, 64):
                                    own = slice(lo, lo + 64)
                                    ins = nc.vector.tensor_tensor(
                                        Z[own, :, own], pZ[own, :].rearrange("p (m c) -> p m c", m=4)[:, :, own],
                                        carry[own, :].unsqueeze(2).broadcast_to([64, 4, 64]), ALU.mult)
                                ins.then_inc(z_ready, 1)
                            finish(t)


def route(nc, con, logits, bias, scratch, selects, crowded):
    with ExitStack() as ctx:
        sb = lambda n, s, d=F32: ctx.enter_context(nc.sbuf_tensor(f"rt_{n}", s, d))
        nl = N_GROUPS + N_EXPERTS
        row = sb("row", [P, nl])
        top = sb("top", [P, 8, TT])
        ghot = sb("ghot", [P, TT, N_GROUPS])
        gexp = sb("gexp", [P, TT, N_GROUPS])
        pick = sb("pick", [P, TT, N_GROUPS, PER_GROUP])
        within = sb("within", [P, TT, PER_GROUP])
        hot1 = sb("hot1", [P, TT, PER_GROUP])
        hot2 = sb("hot2", [P, TT, PER_GROUP])
        tmp = sb("tmp", [P, TT, PER_GROUP])
        best = sb("best", [P, TT])
        wT = sb("wT", [N_EXPERTS, 2, SEQ])
        chosen = sb("chosen", [P, TT, N_EXPERTS])
        place = sb("place", [P, TT, N_EXPERTS])
        fullest = sb("fullest", [P, 1])
        pT = ctx.enter_context(nc.psum_tensor("rt_pT", [P, 512], F32))
        pC = ctx.enter_context(nc.psum_tensor("rt_pC", [P, 512], F32))
        M, M1, M2, GSUM, GP, E2, W1, W2 = range(8)
        with Stage(nc, "rt", ["bias_in", "centred", "gap", "exps", "weights", "counted", "placed", "turned",
                              "turned_out", "stored", "vlink"]) as sems:
            bias_in, centred, gap, exps, weights, counted, placed, turned, turned_out, stored, vlink = sems
            with nc.Block(no_gpsimd_drain=True) as block:
                @block.sync
                def _(sp):
                    sp.dma_start(row[:, 0:N_GROUPS], spread(bias[0])).then_inc(bias_in, 16)
                    sp.dma_start(row[:, N_GROUPS:nl], spread(bias[1])).then_inc(bias_in, 16)
                    sp.wait_ge(turned_out, 2)
                    sp.dma_start(scratch, wT[:]).then_inc(stored, 16)
                    sp.wait_ge(stored, 16)

                @block.scalar
                def _(act):
                    act.wait_ge(centred, 1)
                    nc.scalar.activation(gexp[:], gexp[:], ACT.Exp).then_inc(exps, 1)
                    act.wait_ge(gap, 1)
                    nc.scalar.activation(top[:, E2, :], top[:, E2, :], ACT.Exp).then_inc(exps, 1)

                @block.tensor
                def _(pe):
                    pe.wait_ge(weights, 1)
                    earlier, every = con["counting"][:, 0:P], con["counting"][:, P:2 * P]
                    ne = N_EXPERTS
                    sums = [(0, [(earlier, 0)]), (1, [(every, 0), (earlier, 1)]), (2, [(every, 0), (every, 1)])]
                    for n, terms in sums:
                        for k, (mask, t) in enumerate(terms):
                            ins = nc.tensor.matmul(pC[:, n * ne:(n + 1) * ne], mask, chosen[:, t, :],
                                                   start=(k == 0), stop=(k == len(terms) - 1))
                    ins.then_inc(counted, 1)
                    pe.wait_ge(placed, 1)
                    for n, source in enumerate((pick.rearrange("p t g e -> p t (g e)"), place)):
                        for t in range(TT):
                            at = n * SEQ + t * P
                            ins = nc.tensor.transpose(pT[0:ne, at:at + P], source[:, t], con["identity"])
                    ins.then_inc(turned, 1)

                @block.vector
                def _(dve):
                    link = Link(dve, vlink)
                    tt = lambda o, x, y, op: link(nc.vector.tensor_tensor(o, x, y, op))
                    over = lambda s, n: s.unsqueeze(2).broadcast_to([P, TT, n])
                    dve.wait_ge(bias_in, 32)
                    tt(logits, logits, row[:].unsqueeze(1).broadcast_to([P, TT, nl]), ALU.add)

                    def first_best(x, n, peak, hot):
                        rank = con["rank8"][:, 0:n].unsqueeze(1).broadcast_to([P, TT, n])
                        link(nc.vector.tensor_reduce(peak, x, AX_X, ALU.max))
                        tt(hot, x, over(peak, n), ALU.is_equal)
                        tt(hot, hot, rank, ALU.mult)
                        link(nc.vector.tensor_reduce(best[:], hot, AX_X, ALU.max))
                        tt(hot, hot, over(best[:], n), ALU.is_equal)

                    groups = logits[:, :, 0:N_GROUPS]
                    experts = logits[:, :, N_GROUPS:nl].rearrange("p t (g e) -> p t g e", g=N_GROUPS)
                    first_best(groups, N_GROUPS, top[:, M, :], ghot[:])
                    nc.vector.tensor_tensor(gexp[:], groups, over(top[:, M, :], N_GROUPS),
                                            ALU.subtract).then_inc(centred, 1)
                    tt(pick[:], experts, ghot[:].unsqueeze(3).broadcast_to([P, TT, N_GROUPS, PER_GROUP]), ALU.mult)
                    link(nc.vector.tensor_reduce(within[:], pick[:].rearrange("p t g e -> p t e g"), AX_X, ALU.add))
                    first_best(within[:], PER_GROUP, top[:, M1, :], hot1[:])
                    link(nc.vector.scalar_tensor_tensor(tmp[:], hot1[:], MASKED, within[:], ALU.mult, ALU.add))
                    first_best(tmp[:], PER_GROUP, top[:, M2, :], hot2[:])
                    nc.vector.tensor_tensor(top[:, E2, :], top[:, M2, :], top[:, M1, :],
                                            ALU.subtract).then_inc(gap, 1)
                    dve.wait_ge(exps, 1)
                    link(nc.vector.tensor_reduce(top[:, GSUM, :], gexp[:], AX_X, ALU.add))
                    link(nc.vector.reciprocal(top[:, GP, :], top[:, GSUM, :]))
                    dve.wait_ge(exps, 2)
                    link(nc.vector.tensor_scalar(top[:, W2, :], top[:, E2, :], 1.0, None, ALU.add))
                    link(nc.vector.reciprocal(top[:, W1, :], top[:, W2, :]))
                    tt(top[:, W1, :], top[:, W1, :], top[:, GP, :], ALU.mult)
                    tt(top[:, W2, :], top[:, W1, :], top[:, E2, :], ALU.mult)
                    tt(hot1[:], hot1[:], over(top[:, W1, :], PER_GROUP), ALU.mult)
                    tt(hot2[:], hot2[:], over(top[:, W2, :], PER_GROUP), ALU.mult)
                    tt(hot1[:], hot1[:], hot2[:], ALU.add)
                    for t in range(TT):
                        a = hot1[:, t, :].unsqueeze(1).broadcast_to([P, N_GROUPS, PER_GROUP])
                        b = ghot[:, t, :].unsqueeze(2).broadcast_to([P, N_GROUPS, PER_GROUP])
                        link(nc.vector.tensor_tensor(pick[:, t], a, b, ALU.mult))
                    nc.vector.tensor_scalar(chosen[:], pick.rearrange("p t g e -> p t (g e)"), 0.0, None,
                                            ALU.is_gt).then_inc(weights, 1)
                    nc.vector.memset(selects[:, :, N_EXPERTS * CAP:], 0.0)
                    dve.wait_ge(counted, 1)
                    link(nc.vector.tensor_reduce(fullest[:], pC[:, 2 * N_EXPERTS:3 * N_EXPERTS], AX_X, ALU.max))
                    nc.vector.tensor_scalar(crowded, fullest[0:1, :], float(CAP), None, ALU.is_gt)
                    before = pC[:, 0:TT * N_EXPERTS].rearrange("p (t e) -> p t e", t=TT)
                    link(nc.vector.scalar_tensor_tensor(place[:], before, 1.0, chosen[:], ALU.add, ALU.mult))
                    ins = nc.vector.tensor_scalar(place[:], place[:], -1.0, None, ALU.add)
                    link(ins)
                    dve.sem_inc(placed, 1)
                    dve.wait_ge(turned, 1)
                    nc.vector.tensor_scalar(wT[:, 0, :], pT[0:N_EXPERTS, 0:SEQ], 1.0 / W_SCALE, None,
                                            ALU.mult).then_inc(turned_out, 1)
                    nc.vector.tensor_copy(wT[:, 1, :], pT[0:N_EXPERTS, SEQ:]).then_inc(turned_out, 1)
                    for t in range(TT):
                        nc.vector.tensor_tensor(
                            selects[:, t, 0:N_EXPERTS * CAP].rearrange("p (e n) -> p e n", n=CAP),
                            place[:, t, :].unsqueeze(2).broadcast_to([P, N_EXPERTS, CAP]),
                            con["slot_ids"][:, 0:CAP].unsqueeze(1).broadcast_to([P, N_EXPERTS, CAP]), ALU.is_equal)


def latent_heads(nc, con, ckvT, w_uk, w_uv, k_nope, v):
    with ExitStack() as ctx:
        sb = lambda n, s, d=F32: ctx.enter_context(nc.sbuf_tensor(f"lh_{n}", s, d))
        uk = sb("uk", [P, 4, P])
        ukT = sb("ukT", [P, 512])
        uv = sb("uv", [P, 8, 64])
        pT = ctx.enter_context(nc.psum_tensor("lh_pT", [P, 512], F32))
        pK = ctx.enter_context(nc.psum_tensor("lh_pK", [P, TT, 512], F32))
        pV = ctx.enter_context(nc.psum_tensor("lh_pV", [P, TT, 512], F32))
        with Stage(nc, "lh", ["uk_in", "uv_in", "turned", "turned_out", "k_done", "v_done", "out"]) as sems:
            uk_in, uv_in, turned, turned_out, k_done, v_done, out = sems
            with nc.Block(no_gpsimd_drain=True) as block:
                @block.sync
                def _(sp):
                    sp.dma_start(uk[:], w_uk.rearrange("h d c -> (h d) c").rearrange("(a p) c -> p a c", p=P))\
                        .then_inc(uk_in, 16)
                    sp.dma_start(uv[:], w_uv.rearrange("h c d -> c h d")).then_inc(uv_in, 16)

                @block.tensor
                def _(pe):
                    pe.wait_ge(uk_in, 16)
                    for n in range(4):
                        ins = nc.tensor.transpose(pT[:, n * P:(n + 1) * P], uk[:, n, :], con["identity"])
                    ins.then_inc(turned, 1)
                    pe.wait_ge(uv_in, 16)
                    for t in range(TT):
                        ins = nc.tensor.matmul(pV[:, t, :], ckvT[:, 0, t * P:(t + 1) * P],
                                               uv[:].rearrange("p h d -> p (h d)"), start=True, stop=True)
                    ins.then_inc(v_done, 1)
                    pe.wait_ge(turned_out, 1)
                    for t in range(TT):
                        ins = nc.tensor.matmul(pK[:, t, :], ckvT[:, 0, t * P:(t + 1) * P], ukT[:],
                                               start=True, stop=True)
                    ins.then_inc(k_done, 1)

                @block.vector
                def _(dve):
                    dve.wait_ge(turned, 1)
                    nc.vector.tensor_copy(ukT[:], pT[:]).then_inc(turned_out, 1)
                    dve.wait_ge(k_done, 1)
                    nc.vector.tensor_copy(k_nope, pK[:]).then_inc(out, 1)

                @block.scalar
                def _(act):
                    act.wait_ge(v_done, 1)
                    nc.scalar.activation(v, pV[:], ACT.Copy).then_inc(out, 1)


def even_prepare(nc, con, y, k_nope, q_a, k_a, iw):
    with ExitStack() as ctx:
        sb = lambda n, s, d=F32: ctx.enter_context(nc.sbuf_tensor(f"ep_{n}", s, d))
        tmp = sb("tmp", [P, 4, TT * 8 * 32])
        tmpg = sb("tmpg", [P, 4, TT * 8 * 32])
        r32 = con["rope32"].rearrange("p (t d) -> p t d", t=TT)
        r64 = con["rope64"].rearrange("p (t d) -> p t d", t=TT)
        part = lambda at, n, d: heads_of(y[:, :, at:at + n * d], n)
        with Stage(nc, "ep", ["k_rotated", "vlink", "glink", "alink"]) as sems:
            k_rotated, vlink, glink, alink = sems
            with nc.Block(no_gpsimd_drain=True) as block:
                @block.vector
                def _(dve):
                    link = Link(dve, vlink)
                    rope(link, nc.vector, part(896, 1, 32), r32, tmp)
                    nc.vector.tensor_scalar(iw, y[:, :, 1504:1512], 8 ** -0.5, None, ALU.mult)\
                        .then_inc(k_rotated, 1)
                    rope(link, nc.vector, part(512, 8, 32), r32, tmp)
                    for t in range(TT):
                        link(nc.vector.tensor_copy(q_a[:, t, :, 64:96], part(512, 8, 32)[:, t]))
                    rope(link, nc.vector, part(928, 8, 64), r64, tmp)
                    rope(link, nc.vector, part(1440, 1, 64), r64, tmp)

                @block.gpsimd
                def _(pool):
                    link = Link(pool, glink)
                    rope(link, nc.gpsimd, part(1512, 8, 64), r64, tmpg)
                    rope(link, nc.gpsimd, part(2024, 8, 64), r64, tmpg)

                @block.scalar
                def _(act):
                    link = Link(act, alink)
                    for t in range(TT):
                        link(nc.scalar.activation(q_a[:, t, :, 0:64], part(0, 8, 64)[:, t], ACT.Copy))
                        link(nc.scalar.activation(k_a[:, t, :, 0:64], heads_of(k_nope, 8)[:, t], ACT.Copy))
                    act.wait_ge(k_rotated, 1)
                    for t in range(TT):
                        link(nc.scalar.activation(k_a[:, t, :, 64:96],
                                                  y[:, t, 896:928].unsqueeze(1).broadcast_to([P, 8, 32]), ACT.Copy))


def choose_keys(nc, con, iq, ik, iw, mask):
    with ExitStack() as ctx:
        sb = lambda n, s, d=F32: ctx.enter_context(nc.sbuf_tensor(f"ck_{n}", s, d))
        kT = sb("kT", [64, SEQ])
        qT = sb("qT", [64, 3, SEQ])
        rel = sb("rel", [P, 2, NCOL])
        score = sb("score", [P, NCOL])
        top = sb("top", [P, TT, 8])
        pT = ctx.enter_context(nc.psum_tensor("ck_pT", [P, 4, 512], F32))
        pS = ctx.enter_context(nc.psum_tensor("ck_pS", [P, 4, 512], F32))
        with Stage(nc, "ck", ["k_turned", "k_out", "q_turned", "q_out", "scored", "related", "weighted",
                              "vlink"]) as sems:
            k_turned, k_out, q_turned, q_out, scored, related, weighted, vlink = sems
            with nc.Block(no_gpsimd_drain=True) as block:
                @block.tensor
                def _(pe):
                    for t in range(TT):
                        ins = nc.tensor.transpose(pT[0:64, 3, t * P:(t + 1) * P], ik[:, t, :], con["identity"])
                    ins.then_inc(k_turned, 1)

                    def turn(h):
                        if h >= 3:
                            pe.wait_ge(q_out, h - 2)
                        for t in range(TT):
                            ins = nc.tensor.transpose(pT[0:64, h % 3, t * P:(t + 1) * P], iq[:, t, h, :],
                                                      con["identity"])
                        ins.then_inc(q_turned, 1)

                    def score_of(h):
                        pe.wait_ge(q_out, h + 1)
                        if h >= 4:
                            pe.wait_ge(related, h - 3)
                        for t, c0, nk in SPAN:
                            ins = nc.tensor.matmul(pS[:, h % 4, c0:c0 + nk], qT[:, h % 3, t * P:(t + 1) * P],
                                                   kT[:, 0:nk], start=True, stop=True)
                        ins.then_inc(scored, 1)

                    turn(0)
                    pe.wait_ge(k_out, 1)
                    for h in range(1, 8):
                        turn(h)
                        score_of(h - 1)
                    score_of(7)

                @block.scalar
                def _(act):
                    for h in range(9):
                        if h < 8:
                            act.wait_ge(q_turned, h + 1)
                            if h >= 3:
                                act.wait_ge(scored, h - 2)
                            nc.scalar.activation(qT[:, h % 3, :], pT[0:64, h % 3, 0:SEQ], ACT.Copy).then_inc(q_out, 1)
                        if h:
                            act.wait_ge(scored, h)
                            if h >= 3:
                                act.wait_ge(weighted, h - 2)
                            nc.scalar.activation(rel[:, (h - 1) % 2, :], pS[:, (h - 1) % 4, 0:NCOL], ACT.Relu,
                                                 scale=64 ** -0.5).then_inc(related, 1)

                @block.vector
                def _(dve):
                    link = Link(dve, vlink)
                    dve.wait_ge(k_turned, 1)
                    nc.vector.tensor_copy(kT[:], pT[0:64, 3, 0:SEQ]).then_inc(k_out, 1)
                    for h in range(8):
                        dve.wait_ge(related, h + 1)
                        if h:
                            dve.wait_ge(weighted, h)
                        for t, c0, nk in SPAN:
                            s = score[:, c0:c0 + nk]
                            r = rel[:, h % 2, c0:c0 + nk]
                            if h == 0:
                                ins = nc.vector.tensor_scalar(s, r, iw[:, t, h:h + 1], None, ALU.mult)
                            else:
                                ins = nc.vector.scalar_tensor_tensor(s, r, iw[:, t, h:h + 1], s, ALU.mult, ALU.add)
                        ins.then_inc(weighted, 1)
                    dve.wait_ge(weighted, 8)
                    link(nc.vector.tensor_tensor(score[:], score[:], con["causal"], ALU.add))
                    for n in range(TOP_KEYS // 8):
                        for t, c0, nk in SPAN:
                            link(nc.vector.max(top[:, t, :], score[:, c0:c0 + nk]))
                            link(nc.vector.match_replace(score[:, c0:c0 + nk], top[:, t, :], score[:, c0:c0 + nk],
                                                         TAKEN))
                    link(nc.vector.tensor_scalar(mask, score[:], TAKEN, MASKED, ALU.not_equal, ALU.mult))
                    link(nc.vector.tensor_tensor(mask, mask, con["causal"], ALU.add))


LAM_INIT = 0.8 - 0.6


def differ(nc, con, o, lam, gain, out):
    with ExitStack() as ctx:
        sb = lambda n, s, d=F32: ctx.enter_context(nc.sbuf_tensor(f"df_{n}", s, d))
        l = sb("l", [P, 4, 64])
        prod = sb("prod", [P, 2, 64])
        s = sb("s", [P, 2])
        neg = sb("neg", [P, 1])
        row = sb("row", [P, P])
        sq = sb("sq", [P, TT, 4, P])
        st = sb("st", [P, 3, TT * 4])
        with Stage(nc, "df", ["lam_in", "row_in", "sums", "exps", "less", "squares", "recips", "roots", "vlink"]) as sems:
            lam_in, row_in, sums, exps, less, squares, recips, roots, vlink = sems
            with nc.Block(no_gpsimd_drain=True) as block:
                @block.sync
                def _(sp):
                    sp.dma_start(l[:].rearrange("p a d -> p (a d)"), spread(lam.rearrange("a d -> (a d)")))\
                        .then_inc(lam_in, 16)
                    sp.dma_start(row[:], spread(gain)).then_inc(row_in, 16)

                @block.scalar
                def _(act):
                    act.wait_ge(sums, 1)
                    nc.scalar.activation(s[:], s[:], ACT.Exp).then_inc(exps, 1)
                    act.wait_ge(less, 1)
                    nc.scalar.activation(sq[:], heads_of(out, 4), ACT.Square).then_inc(squares, 1)
                    act.wait_ge(recips, 1)
                    nc.scalar.activation(st[:, 2, :], st[:, 1, :], ACT.Sqrt).then_inc(roots, 1)

                @block.vector
                def _(dve):
                    link = Link(dve, vlink)
                    v = nc.vector
                    dve.wait_ge(lam_in, 16)
                    link(v.tensor_tensor(prod[:], l[:, 0::2, :], l[:, 1::2, :], ALU.mult))
                    v.tensor_reduce(s[:], prod[:], AX_X, ALU.add).then_inc(sums, 1)
                    dve.wait_ge(exps, 1)
                    link(v.tensor_tensor(neg[:], s[:, 1:2], s[:, 0:1], ALU.subtract))
                    link(v.tensor_scalar(neg[:], neg[:], -LAM_INIT, None, ALU.add))
                    for t in range(TT):
                        pair = o[:, t, :].rearrange("p (h m d) -> p h m d", h=4, m=2)
                        ins = v.scalar_tensor_tensor(out[:, t, :].rearrange("p (h d) -> p h d", h=4),
                                                     pair[:, :, 1, :], neg[:], pair[:, :, 0, :], ALU.mult, ALU.add)
                    ins.then_inc(less, 1)
                    dve.wait_ge(squares, 1)
                    link(v.tensor_reduce(st[:, 0, :], sq[:].rearrange("p t h d -> p (t h) d"), AX_X, ALU.add))
                    link(v.tensor_scalar(st[:, 0, :], st[:, 0, :], 1.0 / P, EPS, ALU.mult, ALU.add))
                    v.reciprocal(st[:, 1, :], st[:, 0, :]).then_inc(recips, 1)
                    dve.wait_ge(roots, 1)
                    link(v.tensor_scalar(st[:, 2, :], st[:, 2, :], 1.0 - LAM_INIT, None, ALU.mult))
                    dve.wait_ge(row_in, 16)
                    for t in range(TT):
                        each = out[:, t, :].rearrange("p (h d) -> p h d", h=4)
                        by = st[:, 2, t * 4:(t + 1) * 4].unsqueeze(2).broadcast_to([P, 4, P])
                        link(v.tensor_tensor(each, each, by, ALU.mult))
                        link(v.tensor_tensor(each, each, row[:].unsqueeze(1).broadcast_to([P, 4, P]), ALU.mult))


def odd_prepare(nc, con, y, pe_emb, w1s, w2, cmp_kv, gates):
    with ExitStack() as ctx:
        sb = lambda n, s, d=F32: ctx.enter_context(nc.sbuf_tensor(f"op_{n}", s, d))
        tmp = sb("tmp", [P, 4, TT * C_H * 32])
        tmpg = sb("tmpg", [P, 4, TT * C_G * 32])
        w2s = sb("w2s", [P, 2, C_DIM])
        emb = sb("emb", [CMP_LEN, 2, C_DIM])
        embT = sb("embT", [C_DIM, 2, CMP_LEN])
        per_g = SEQ // CMP_STRIDE
        n_win = C_G * per_g - 1
        xE = sb("xE", [C_DIM, 2, 2, C_G * SEQ])
        hid = sb("hid", [n_win, 2, P])
        hidT = sb("hidT", [P, 2, n_win])
        pT = ctx.enter_context(nc.psum_tensor("op_pT", [P, 4, 512], F32))
        pH = ctx.enter_context(nc.psum_tensor("op_pH", [P, 512], F32))
        pO = ctx.enter_context(nc.psum_tensor("op_pO", [P, 512], F32))
        r64 = con["rope64"].rearrange("p (t d) -> p t d", t=TT)
        part = lambda at, n: heads_of(y[:, :, at:at + n * 64], n)
        with Stage(nc, "op", ["emb_in", "w2_in", "rotated", "turned", "emb_turned", "x_out",
                              "products", "gelus", "gelus_turned", "hid_out", "seconds", "done", "vlink", "glink",
                              "alink"]) as sems:
            (emb_in, w2_in, rotated, turned, emb_turned, x_out, products, gelus, gelus_turned, hid_out,
             seconds, done, vlink, glink, alink) = sems
            with nc.Block(no_gpsimd_drain=True) as block:
                @block.sync
                def _(sp):
                    sp.dma_start(emb[:], pe_emb.rearrange("a l d -> l a d")).then_inc(emb_in, 16)
                    sp.dma_start(w2s[:], w2.rearrange("a e d -> e a d")).then_inc(w2_in, 16)

                @block.gpsimd
                def _(pool):
                    link = Link(pool, glink)
                    rope(link, nc.gpsimd, part(1536, C_G), r64, tmpg)
                    rope(link, nc.gpsimd, part(2048, C_G), r64, tmpg)

                @block.vector
                def _(dve):
                    link = Link(dve, vlink)
                    rope(link, nc.vector, part(1024, C_G), r64, tmp)
                    dve.sem_inc(rotated, 1)
                    dve.wait_ge(emb_turned, 1)
                    link(nc.vector.tensor_copy(embT[:], pO[0:C_DIM, 0:2 * CMP_LEN]
                                               .rearrange("p (a l) -> p a l", a=2)))
                    dve.wait_ge(turned, 1)
                    for a in range(2):
                        for half in range(2):
                            for g2 in range(2):
                                e = embT[:, a, half * CMP_STRIDE:(half + 1) * CMP_STRIDE].unsqueeze(1)\
                                    .broadcast_to([C_DIM, 2 * SEQ // CMP_STRIDE, CMP_STRIDE])
                                split = lambda ap: ap.rearrange("p (n l) -> p n l", l=CMP_STRIDE)
                                ins = nc.vector.tensor_tensor(
                                    split(xE[:, half, a, g2 * 2 * SEQ:(g2 + 1) * 2 * SEQ]),
                                    split(pT[0:C_DIM, 2 * a + g2, :]), e, ALU.add)
                        ins.then_inc(x_out, 1)
                    rope(link, nc.vector, part(0, C_H), r64, tmp)
                    dve.wait_ge(gelus_turned, 1)
                    nc.vector.tensor_copy(hidT[:], pT[:, 0, 0:2 * n_win]
                                          .rearrange("p (a n) -> p a n", a=2)).then_inc(hid_out, 1)
                    dve.wait_ge(seconds, 1)
                    nc.vector.tensor_copy(cmp_kv, pO[0:N_CMP, :].rearrange("p (a n) -> p a n", a=2)).then_inc(done, 1)

                @block.scalar
                def _(act):
                    nc.scalar.activation(gates, y[:, :, 2560:2608], ACT.Sigmoid).then_inc(alink, 1)
                    act.wait_ge(products, 1)
                    nc.scalar.activation(hid[:].rearrange("p a n -> p (a n)"), pH[0:n_win, 0:2 * P],
                                         ACT.Gelu_apprx_tanh).then_inc(gelus, 1)

                @block.tensor
                def _(pe):
                    ident = con["identity"]
                    pe.wait_ge(emb_in, 16)
                    for a in range(2):
                        ins = nc.tensor.transpose(pO[0:C_DIM, a * CMP_LEN:(a + 1) * CMP_LEN], emb[:, a, :],
                                                  ident[0:CMP_LEN, 0:CMP_LEN])
                    ins.then_inc(emb_turned, 1)
                    pe.wait_ge(rotated, 1)
                    for a in range(2):
                        for g in range(C_G):
                            for t in range(TT):
                                at = 1024 + a * 256 + g * C_DIM
                                ins = nc.tensor.transpose(pT[0:C_DIM, 2 * a + g // 2,
                                                             (g % 2) * SEQ + t * P:(g % 2) * SEQ + (t + 1) * P],
                                                          y[:, t, at:at + C_DIM], ident)
                    ins.then_inc(turned, 1)
                    for a in range(2):
                        pe.wait_ge(x_out, a + 1)
                        for l in range(CMP_LEN):
                            last = l + CMP_STRIDE * (n_win - 1) + 1
                            windows = xE[:, l // CMP_STRIDE, a, l:last:CMP_STRIDE]
                            ins = nc.tensor.matmul(pH[0:n_win, a * P:(a + 1) * P], windows, w1s[:, a, l, :],
                                                   start=(l == 0), stop=(l == CMP_LEN - 1))
                    ins.then_inc(products, 1)
                    pe.wait_ge(gelus, 1)
                    for a in range(2):
                        ins = nc.tensor.transpose(pT[:, 0, a * n_win:(a + 1) * n_win], hid[:, a, :],
                                                  ident[0:n_win, 0:n_win])
                    ins.then_inc(gelus_turned, 1)
                    pe.wait_ge(w2_in, 16)
                    pe.wait_ge(hid_out, 1)
                    for a in range(2):
                        for g in range(C_G):
                            at = a * 256 + g * C_DIM
                            ins = nc.tensor.matmul(pO[0:N_CMP, at:at + C_DIM],
                                                   hidT[:, a, g * per_g:g * per_g + N_CMP], w2s[:, a, :],
                                                   start=True, stop=True)
                    ins.then_inc(seconds, 1)


def blend(nc, parts, gates, out):
    with ExitStack() as ctx:
        tmp = ctx.enter_context(nc.sbuf_tensor("bl_tmp", [P, 2, D], F32))
        with Stage(nc, "bl", ["vlink", "second_ready", "third_ready"]) as (vlink, second_ready, third_ready):
            def gated(eng, into, j, t):
                each = parts[j][:, t, :].rearrange("p (h d) -> p h d", h=C_H)
                by = gates[:, t, j:3 * C_H:3].unsqueeze(2).broadcast_to([P, C_H, C_DIM])
                return eng.tensor_tensor(into.rearrange("p (h d) -> p h d", h=C_H), each, by, ALU.mult)

            with nc.Block(no_gpsimd_drain=True) as block:
                @block.gpsimd
                def _(pool):
                    for t in range(TT):
                        gated(nc.gpsimd, tmp[:, t, :], 2, t).then_inc(third_ready, 1)

                @block.vector
                def _(dve):
                    link = Link(dve, vlink)
                    for t in range(TT):
                        link(gated(nc.vector, out[:, t, :], 0, t))
                        link(gated(nc.vector, parts[1][:, t, :], 1, t))
                        link(nc.vector.tensor_tensor(out[:, t, :], out[:, t, :], parts[1][:, t, :], ALU.add))
                    for t in range(TT):
                        dve.wait_ge(third_ready, t + 1)
                        link(nc.vector.tensor_tensor(out[:, t, :], out[:, t, :], tmp[:, t, :], ALU.add))


AHEAD = {"in1": 276, "out1": 256, "in2": 254, "out2": 256, "in3": 326, "out3": 256}


def hybrid_kernel(nc, a, out):
    w = {n: v[0] for n, v in a.items() if n in LAYER_INPUTS}
    w["rw_r_k"] = w["rw_r_k"].rearrange("h n -> (h n)")
    flat2 = lambda x: x.rearrange("c h d -> c (h d)")
    tokens = lambda x: x.rearrange("(t p) n -> p t n", p=P)
    scratch = nc.dram_tensor("expert_rows", [N_EXPERTS, 2, SEQ], F32, kind="Internal").ap()
    with ExitStack() as ctx:
        sb = lambda n, s, d=F32: ctx.enter_context(nc.sbuf_tensor(n, s, d))
        x = sb("x", [P, TT, D])
        mix = sb("mix", [P, TT, D])
        con_t = {n: sb("con_" + n, list(a[n].shape)) for n in CONSTANTS if n not in ("level_masks", "decay_sums")}
        con = {n: t[:] for n, t in con_t.items()}
        early = ["rw", "moe", "ffn2", "ffn3"] + list(AHEAD)
        arrived_of = dict(zip(early, ctx.enter_context(Stage(nc, "arrived", early))))

        wt = sb("wt", [P, 2, KC, max(AHEAD.values())])
        first = {name: (wt, arrived_of[name]) for name in AHEAD}

        def loads(name, w):
            return [pair + (arrived_of[name],) for pair in first_tiles(wt, w, AHEAD[name])]

        with Stage(nc, "load", ["loaded"]) as (loaded,):
            with nc.Block(no_gpsimd_drain=True) as block:
                @block.sync
                def _(sp):
                    sp.dma_start(x[:], tokens(a["x"][0])).then_inc(loaded, 16)
                    sp.dma_start(con_t["identity"][:], a["identity"]).then_inc(loaded, 16)
                    for into, source, arrived in loads("in1", w["w_in"]):
                        sp.dma_start(into, source).then_inc(arrived, 16)
                    sp.wait_ge(loaded, 2 * 16)

        by_slot = lambda width: (lambda i, s: i * (ATTN_SLOTS * width) + s * width)

        with ExitStack() as inner:
            sbi = lambda n, s: inner.enter_context(nc.sbuf_tensor(n, s, F32))
            feat = sbi("feat", [P, TT, IN_W])
            project(nc, "in1", con, x, D, w["g_mix"], [(w["w_in"], IN_W, AHEAD["in1"], feat)], split=True, first=first["in1"],
                    prefetch=[(t[:], a[n]) for n, t in con_t.items() if n != "identity"])
            more = {n: inner.enter_context(nc.sbuf_tensor("con_" + n, list(a[n].shape), F32))
                    for n in ("level_masks", "decay_sums")}
            rw_tiles = rwkv_tiles(inner, nc)
            rw_loads = rwkv_loads(rw_tiles, feat[:, :, MLA_IN:IN_W], w) + [(t[:], a[n]) for n, t in more.items()]
            with ExitStack() as att:
                sba = lambda n, s: att.enter_context(nc.sbuf_tensor(n, s, F32))
                qk = sba("qk", [P, 2, TT, MLA_H, MLA_QK])
                v = sba("v", [P, TT, MLA_H * MLA_V])
                k_nope = sba("k_nope", [P, TT, MLA_H * MLA_NOPE])
                q_flat = qk[:, 0].rearrange("p t h d -> p t (h d)")
                k_flat = qk[:, 1].rearrange("p t h d -> p t (h d)")
                project(nc, "uq", con, feat[:, :, 0:Q_RANK], Q_RANK, w["g_cq"],
                        [(flat2(w["w_uq"]), MLA_H * MLA_QK, 384, q_flat)])
                project(nc, "ukv", con, feat[:, :, Q_RANK:Q_RANK + KV_RANK], KV_RANK, w["g_ckv"],
                        [(flat2(w["w_uk"]), 512, 512, k_nope), (flat2(w["w_uv"]), 512, 512, v)])
                mla_prepare(nc, con, feat, qk[:], k_nope, a["positions"], w["g_qn"], w["g_kn"])
                attention(nc, "mla_at", con, MLA_H, q_flat, k_flat, v, MLA_QK, MLA_V, by_slot(MLA_QK),
                          by_slot(MLA_QK), by_slot(MLA_V), MLA_QK ** -0.5, con["causal"], mix[:, :, 0:512],
                          start=[pair + (arrived_of["rw"],) for pair in rw_loads] + loads("out1", w["w_o"]))
            rms_scale(nc, "mla_out", mix[:, :, 0:512], 512, w["g_mla_out"])
            with nc.Block(no_gpsimd_drain=True) as block:
                @block.sync
                def _(sp):
                    sp.wait_ge(arrived_of["rw"], 16 * len(rw_loads))
            rwkv(nc, con | {n: t[:] for n, t in more.items()}, feat[:, :, MLA_IN:IN_W], w, mix[:, :, 512:D],
                 rw_tiles)
        with ExitStack() as inner:
            sbi = lambda n, s, d=F32: inner.enter_context(nc.sbuf_tensor(n, s, d))
            weights = (sbi("moe_w_up32", [P, 2, 2, KC, D_EXPERT]), sbi("moe_w_down32", [P, 2, 2, D]))
            rows = lambda m: (lambda e: m[e].rearrange("(p c) n -> p c n", p=P))
            expert = (rows(w["w_gate"]), rows(w["w_up"]), rows(w["w_down"]))
            project(nc, "out1", con, mix, D, None, [(w["w_o"], D, AHEAD["out1"], ("add", x))], normed=False, split=True,
                    first=first["out1"], prefetch=first_weights(weights, *expert), arrived=arrived_of["moe"])
            hT = (sbi("hT_hi", [P, KC, SEQ], F16), sbi("hT_lo", [P, KC, SEQ], F16))
            logits = sbi("logits", [P, TT, N_GROUPS + N_EXPERTS])
            arrived = arrived_of["moe"]
            gain = sbi("moe_gain", [P, KC])
            selects = sbi("selects", [P, TT, (N_EXPERTS + 8) * CAP], F16)
            crowded = sbi("crowded", [1, 1], I32)
            project(nc, "rt_in", con, x, D, w["g_ffn"],
                    [(w["w_group"], N_GROUPS, N_GROUPS, logits[:, :, 0:N_GROUPS]),
                     (w["w_expert"], N_EXPERTS, N_EXPERTS, logits[:, :, N_GROUPS:])], keep_T=hT, split=True,
                    keep_normed=(mix, gain))
            route(nc, con, logits[:], (w["b_group"], w["b_expert"]), scratch, selects[:], crowded[:])
            few_experts(nc, con, mix, gain, selects, *expert,
                        lambda e: scratch[e].rearrange("a n -> (a n)").rearrange("(o n) -> o n", o=1)
                        .broadcast_to([P, 2 * SEQ]), x, weights, arrived, crowded[:],
                        start=loads("in2", w["ev_w_in_2"]))
            swiglu(nc, "moe", con, hT, N_EXPERTS, *expert,
                   lambda e: scratch[e, 0:1].broadcast_to([P, SEQ]), x, weights, arrived, flag=crowded[:])

        def out_ffn(out_name, w_out, name, layer, start=()):
            with ExitStack() as inner:
                arrived = arrived_of[name]
                hT = tuple(inner.enter_context(nc.sbuf_tensor(f"{name}_hT_{n}", [P, KC, SEQ], F16))
                           for n in ("hi", "lo"))
                weights = tuple(inner.enter_context(nc.sbuf_tensor(f"{name}_w_{n}32", s, F32))
                                for n, s in (("up", [P, 2, 2, KC, D_EXPERT]), ("down", [P, 2, 2, D])))
                up = lambda m: (lambda e: m[layer].rearrange("(p c) n -> p c n", p=P)[:, :, bass.ds(e * D_EXPERT, D_EXPERT)])
                down = lambda m: (lambda e: m[layer].rearrange("(e p c) n -> e p c n", p=P, c=2)[e])
                blocks = (up(a["ffn_w_gate_2"]), up(a["ffn_w_up_2"]), down(a["ffn_w_down_2"]))
                project(nc, out_name, con, mix, D, None, [(w_out, D, AHEAD[out_name], ("add", x))], normed=False, split=True,
                        first=first[out_name], prefetch=first_weights(weights, *blocks), arrived=arrived)
                project(nc, name + "_in", con, x, D, a["norm_ffn_2"][layer], [], keep_T=hT, split=True)
                swiglu(nc, name, con, hT, D_FF // D_EXPERT, *blocks, None, x, weights, arrived, start=start)

        with ExitStack() as inner:
            sbi = lambda n, s: inner.enter_context(nc.sbuf_tensor(n, s, F32))
            y = sbi("y_even", [P, TT, EVEN_IN])
            project(nc, "in2", con, x, D, a["norm_mix_2"][0], [(w["ev_w_in_2"], EVEN_IN, AHEAD["in2"], y)], split=True,
                    first=first["in2"])
            with ExitStack() as att:
                sba = lambda n, s: att.enter_context(nc.sbuf_tensor(n, s, F32))
                ckvT = sba("ckvT", [P, 1, SEQ])
                k_nope = sba("k_nope2", [P, TT, 512])
                v = sba("v2", [P, TT, 512])
                q_a = sba("q_a", [P, TT, 8, 96])
                k_a = sba("k_a", [P, TT, 8, 96])
                iw = sba("iw", [P, TT, 8])
                mask = sba("mask", [P, NCOL])
                project(nc, "ckv2", con, y[:, :, 768:896], KV_RANK, w["ev_kv_gain_2"], [], keep_T=ckvT)
                latent_heads(nc, con, ckvT, w["ev_w_uk_2"], w["ev_w_uv_2"], k_nope[:], v[:])
                even_prepare(nc, con, y, k_nope[:], q_a, k_a, iw[:])
                choose_keys(nc, con, heads_of(y[:, :, 928:1440], 8), y[:, :, 1440:1504], iw, mask[:])
                attention(nc, "dsa", con, 8, q_a[:].rearrange("p t h d -> p t (h d)"),
                          k_a[:].rearrange("p t h d -> p t (h d)"), v, 96, 64, by_slot(96), by_slot(96), by_slot(64),
                          96 ** -0.5, mask[:], mix[:, :, 0:512])
            with ExitStack() as att:
                o = att.enter_context(nc.sbuf_tensor("o_diff", [P, TT, D], F32))
                attention(nc, "diff", con, 8, y[:, :, 1512:2024], y[:, :, 2024:2536], y[:, :, 2536:3048], 64, 128,
                          by_slot(64), by_slot(64), lambda i, s: i * 256 + (s // 2) * 128, 64 ** -0.5,
                          con["causal"], o, start=loads("out2", w["ev_w_out_2"]))
                differ(nc, con, o, w["ev_lambda_2"], w["ev_subln_2"], mix[:, :, 512:D])
        out_ffn("out2", w["ev_w_out_2"], "ffn2", 0, start=loads("in3", w["od_w_in_2"]))

        with ExitStack() as inner:
            sbi = lambda n, s: inner.enter_context(nc.sbuf_tensor(n, s, F32))
            y = sbi("y_odd", [P, TT, ODD_IN])
            cmp_kv = sbi("cmp_kv", [N_CMP, 2, C_G * C_DIM])
            gates = sbi("gates", [P, TT, 3 * C_H])
            parts = [sbi(f"branch{n}", [P, TT, D]) for n in range(3)]
            with nc.sbuf_tensor("cmp_w1", [C_DIM, 2, CMP_LEN, P], F32) as w1s:
                project(nc, "in3", con, x, D, a["norm_mix_2"][1], [(w["od_w_in_2"], ODD_IN, AHEAD["in3"], y)], split=True,
                        first=first["in3"],
                        prefetch=[(w1s[:, n, :, :], w["od_cmp_w1_2"][n].rearrange("(l d) e -> d l e", d=C_DIM))
                                  for n in range(2)])
                odd_prepare(nc, con, y, w["od_cmp_pe_2"], w1s, w["od_cmp_w2_2"], cmp_kv[:], gates[:])
            q = y[:, :, 0:D]
            shared = lambda i, s: i * C_DIM
            attention(nc, "cmp", con, C_H, q, cmp_kv[:, 0, :], cmp_kv[:, 1, :], C_DIM, C_DIM, by_slot(C_DIM),
                      shared, shared, C_DIM ** -0.5, con["cmp_mask"], parts[0],
                      spans=[(0, 0, N_CMP), (1, N_CMP, N_CMP)], blocks=[(0, 0, 0, N_CMP), (1, 0, N_CMP, N_CMP)],
                      key_tiles=1, key_rows=N_CMP, empty_rows=True)
            for n, name in ((1, "slc"), (2, "win")):
                at = 1536 + 512 * (n - 1)
                attention(nc, name, con, C_H, q, y[:, :, at:at + 256], y[:, :, at + 256:at + 512], C_DIM, C_DIM,
                          by_slot(C_DIM), shared, shared, C_DIM ** -0.5, con["causal"], parts[n],
                          start=loads("out3", w["od_w_out_2"]) if n == 2 else ())
            blend(nc, [p[:] for p in parts], gates, mix)
        out_ffn("out3", w["od_w_out_2"], "ffn3", 1)
        rms_scale(nc, "final", x[:], D, a["norm_final_2"])
        with Stage(nc, "store", ["stored"]) as (stored,):
            with nc.Block(no_gpsimd_drain=True) as block:
                @block.sync
                def _(sp):
                    sp.dma_start(tokens(out[0]), x[:]).then_inc(stored, 16)
                    sp.wait_ge(stored, 16)


CONSTANTS = ("identity", "causal", "cmp_mask", "decay_sums", "decay_ends", "level_masks", "inv_freq", "rope32",
             "rope64", "rank8", "counting", "slot_ids")
INPUTS = (
    "x positions g_mix w_in g_cq w_uq g_ckv w_uk w_uv g_qn g_kn g_mla_out rw_mu rw_w0 rw_w2 rw_a0 rw_a2 rw_g2 "
    "rw_k_k rw_k_a rw_r_k rw_lnx_g rw_lnx_b w_o g_ffn w_group b_group w_expert b_expert w_gate w_up w_down "
    "norm_mix_2 norm_ffn_2 norm_final_2 ev_w_in_2 ev_kv_gain_2 ev_w_uk_2 ev_w_uv_2 ev_lambda_2 ev_subln_2 "
    "ev_w_out_2 od_w_in_2 od_cmp_pe_2 od_cmp_w1_2 od_cmp_w2_2 od_w_out_2 ffn_w_gate_2 ffn_w_up_2 ffn_w_down_2"
).split()
LAYER_INPUTS = [n for n in INPUTS if n not in ("x", "positions", "norm_mix_2", "norm_ffn_2", "norm_final_2",
                                               "ffn_w_gate_2", "ffn_w_up_2", "ffn_w_down_2")]


def kernel(**inputs):
    import concourse.bacc as bacc
    from concourse.bass_utils import run_bass_kernel_spmd

    nc = bacc.Bacc("TRN2", target_bir_lowering=False, num_devices=1)
    arrays = {n: np.ascontiguousarray(inputs[n]) for n in INPUTS}
    arrays.update(shape_constants())
    feeds, aps = {}, {}
    for n, v in arrays.items():
        feeds[f"in_{n}"] = v
        aps[n] = nc.dram_tensor(f"in_{n}", v.shape, mybir.dt.from_np(v.dtype), kind="ExternalInput").ap()
    out = nc.dram_tensor("out", (1, SEQ, D), F32, kind="ExternalOutput").ap()
    hybrid_kernel(nc, aps, out)
    return run_bass_kernel_spmd(nc, [feeds], core_ids=[0]).results[0]["out"]
```
